# Optimizing a Trainium2 kernel written in Bass

```python
import jax, jax.numpy as jnp
from jax import lax
import numpy as np

D_MODEL = 1024
BATCH = 1
SEQ = 256
DEPTH = 1

R_HEADS = 8
R_HEAD_DIM = 64
R_WIDTH = R_HEADS * R_HEAD_DIM
DECAY_LORA = 64
ICLR_LORA = 64
GATE_LORA = 160
LNX_EPS = 64e-5
R_COLS = 3 * R_WIDTH + DECAY_LORA + ICLR_LORA + GATE_LORA
N_Q_HEADS = 8
N_KV_HEADS = 2
GQA = N_Q_HEADS // N_KV_HEADS
HEAD_DIM = 64
N_WIDTH = N_Q_HEADS * HEAD_DIM
KV_WIDTH = N_KV_HEADS * HEAD_DIM
N_COLS = N_WIDTH + 6 * KV_WIDTH + 3 * N_Q_HEADS
CMP_BLOCK = 32
CMP_STRIDE = 16
CMP_HIDDEN = 256
SEL_BLOCK = 64
SEL_TOPK = 16
WINDOW = 512
Q_BLOCK = 128
ROPE_THETA = 500000.0
ROT_DIM = HEAD_DIM // 4
IN_COLS = R_COLS + N_COLS
MIX_WIDTH = R_WIDTH + N_WIDTH
D_FF = ((8 * D_MODEL + 3 * 256 - 1) // (3 * 256)) * 256
NORM_EPS = 1e-6
MASK = -1e30
FORCE = 1e6


def rms_norm(x, g):
    xf = x.astype(jnp.float32)
    y = xf * lax.rsqrt(jnp.mean(xf * xf, axis=-1, keepdims=True) + NORM_EPS)
    return (y * g.astype(jnp.float32)).astype(x.dtype)

def partial_rope(x, pos):
    half = ROT_DIM // 2
    inv_freq = jnp.power(jnp.float32(ROPE_THETA), -jnp.arange(half, dtype=jnp.float32) * 2.0 / ROT_DIM)
    ang = pos.astype(jnp.float32)[..., None] * inv_freq
    cos = jnp.cos(ang)[:, :, None, :]
    sin = jnp.sin(ang)[:, :, None, :]
    xf = x.astype(jnp.float32)
    x1 = xf[..., :half]
    x2 = xf[..., half:ROT_DIM]
    out = jnp.concatenate([x1 * cos - x2 * sin, x2 * cos + x1 * sin, xf[..., ROT_DIM:]], axis=-1)
    return out.astype(x.dtype)

def rwkv7_group(cols, mu_shift, w0, w2, a0, a2, g2, k_k, k_a, r_k, lnx_w, lnx_b):
    B, S, _ = cols.shape
    f32 = jnp.float32
    prev = jnp.pad(cols, ((0, 0), (1, 0), (0, 0)))[:, :-1]
    cols = cols + (prev - cols) * mu_shift
    o = 0
    r = cols[..., o:o + R_WIDTH]; o += R_WIDTH
    k = cols[..., o:o + R_WIDTH]; o += R_WIDTH
    v = cols[..., o:o + R_WIDTH]; o += R_WIDTH
    w_lat = cols[..., o:o + DECAY_LORA]; o += DECAY_LORA
    a_lat = cols[..., o:o + ICLR_LORA]; o += ICLR_LORA
    g_lat = cols[..., o:o + GATE_LORA]

    w = -jax.nn.softplus(-(w0 + jnp.tanh(w_lat) @ w2).astype(f32)) - 0.5
    decay = jnp.exp(-jnp.exp(w))
    a = jax.nn.sigmoid((a0 + a_lat @ a2).astype(f32))
    g = jax.nn.sigmoid(g_lat) @ g2
    kk = (k * k_k).astype(f32)
    k_mod = k.astype(f32) * (1.0 + (a - 1.0) * k_a.astype(f32))

    heads = lambda t: t.astype(f32).reshape(B, S, R_HEADS, R_HEAD_DIM)
    kk = heads(kk)
    kk = kk / jnp.maximum(jnp.sqrt(jnp.sum(kk * kk, axis=-1, keepdims=True)), 1e-12)
    rh, kh, vh, ah, wh = heads(r), heads(k_mod), heads(v), heads(a), heads(decay)

    def step(state, inp):
        r_t, w_t, k_t, v_t, an_t, b_t = inp
        sa = jnp.einsum('bhvk,bhk->bhv', state, an_t)
        state = state * w_t[:, :, None, :] + sa[..., None] * b_t[:, :, None, :] + v_t[..., None] * k_t[:, :, None, :]
        return state, jnp.einsum('bhvk,bhk->bhv', state, r_t)

    seq_first = lambda t: jnp.moveaxis(t, 1, 0)
    state0 = jnp.zeros((B, R_HEADS, R_HEAD_DIM, R_HEAD_DIM), f32)
    xs = (seq_first(rh), seq_first(wh), seq_first(kh), seq_first(vh), seq_first(-kk), seq_first(kk * ah))
    _, y = lax.scan(step, state0, xs)
    y = jnp.moveaxis(y, 0, 1)

    mean = jnp.mean(y, axis=-1, keepdims=True)
    var = jnp.mean(jnp.square(y - mean), axis=-1, keepdims=True)
    y = ((y - mean) * lax.rsqrt(var + LNX_EPS)).reshape(B, S, R_WIDTH) * lnx_w + lnx_b
    bonus = jnp.sum(rh * kh * r_k.astype(f32), axis=-1, keepdims=True) * vh
    y = (y + bonus.reshape(B, S, R_WIDTH)) * g
    return y.astype(cols.dtype)

def compress(t, pe, w1, b1, w2):
    B, Hk, S, D = t.shape
    n_blk = S // CMP_STRIDE
    n_sub = CMP_BLOCK // CMP_STRIDE
    n_cmp = n_blk - n_sub + 1
    blocks = t.reshape(B, Hk, n_blk, CMP_STRIDE, D)
    win = jnp.concatenate([blocks[:, :, i:i + n_cmp] for i in range(n_sub)], axis=3)
    win = (win + pe).reshape(B, Hk, n_cmp, CMP_BLOCK * D)
    return jax.nn.silu(win @ w1 + b1) @ w2

def nsa_group(cols, positions, pe_k, wk1, bk1, wk2, pe_v, wv1, bv1, wv2):
    B, S, _ = cols.shape
    f32 = jnp.float32
    scale = HEAD_DIM ** -0.5
    q = partial_rope(cols[..., :N_WIDTH].reshape(B, S, N_Q_HEADS, HEAD_DIM), positions)
    q = q.reshape(B, S, N_KV_HEADS, GQA, HEAD_DIM).transpose(0, 2, 3, 1, 4)

    def kv(i, rope):
        o = N_WIDTH + i * KV_WIDTH
        t = cols[..., o:o + KV_WIDTH].reshape(B, S, N_KV_HEADS, HEAD_DIM)
        if rope:
            t = partial_rope(t, positions)
        return t.transpose(0, 2, 1, 3)

    k_cmp, v_cmp = kv(0, False), kv(1, False)
    k_slc, v_slc = kv(2, True), kv(3, True)
    k_win, v_win = kv(4, True), kv(5, True)
    gates = jax.nn.sigmoid(cols[..., N_WIDTH + 6 * KV_WIDTH:].reshape(B, S, N_KV_HEADS, GQA, 3))
    gates = gates.transpose(0, 2, 3, 1, 4)

    kc = compress(k_cmp, pe_k, wk1, bk1, wk2)
    vc = compress(v_cmp, pe_v, wv1, bv1, wv2)
    n_cmp = kc.shape[2]
    pos_c = positions[:, CMP_BLOCK - 1::CMP_STRIDE][:, :n_cmp]
    kc = partial_rope(kc.transpose(0, 2, 1, 3), pos_c).transpose(0, 2, 1, 3)
    cmp_end = jnp.arange(n_cmp) * CMP_STRIDE + CMP_BLOCK - 1

    n_sel = S // SEL_BLOCK
    n_top = min(SEL_TOPK, n_sel)
    ks_blocks = k_slc.reshape(B, N_KV_HEADS, n_sel, SEL_BLOCK, HEAD_DIM)
    vs_blocks = v_slc.reshape(B, N_KV_HEADS, n_sel, SEL_BLOCK, HEAD_DIM)
    c_start = jnp.arange(n_cmp)[:, None] * CMP_STRIDE
    s_start = jnp.arange(n_sel)[None, :] * SEL_BLOCK
    cover = ((c_start < s_start + SEL_BLOCK) & (c_start + CMP_BLOCK > s_start)).astype(f32)
    sel_ids = jnp.arange(n_sel)
    bidx = jnp.arange(B)[:, None, None, None]
    hidx = jnp.arange(N_KV_HEADS)[None, :, None, None]

    kw_pad = jnp.pad(k_win, ((0, 0), (0, 0), (WINDOW, 0), (0, 0)))
    vw_pad = jnp.pad(v_win, ((0, 0), (0, 0), (WINDOW, 0), (0, 0)))

    def q_block(qb):
        start = qb * Q_BLOCK
        t = start + jnp.arange(Q_BLOCK)
        qq = lax.dynamic_slice_in_dim(q, start, Q_BLOCK, axis=3)
        gg = lax.dynamic_slice_in_dim(gates, start, Q_BLOCK, axis=3)

        s = jnp.einsum('bkgqd,bknd->bkgqn', qq, kc).astype(f32) * scale
        valid = cmp_end[None, :] <= t[:, None]
        p = jax.nn.softmax(jnp.where(valid, s, MASK), axis=-1)
        p = jnp.where(valid, p, 0.0)
        o_cmp = jnp.einsum('bkgqn,bknd->bkgqd', p.astype(vc.dtype), vc)

        imp = jnp.sum(p, axis=2) @ cover
        cur = t // SEL_BLOCK
        forced = (sel_ids[None] == 0) | (sel_ids[None] == cur[:, None]) | (sel_ids[None] == cur[:, None] - 1)
        score = jnp.where(forced, FORCE, jnp.where(sel_ids[None] <= cur[:, None], imp, MASK))
        _, idx = lax.top_k(score, n_top)
        k_sel = ks_blocks[bidx, hidx, idx]
        v_sel = vs_blocks[bidx, hidx, idx]
        tok = idx[..., None] * SEL_BLOCK + jnp.arange(SEL_BLOCK)
        valid = (tok <= t[:, None, None])[:, :, None]
        s = jnp.einsum('bkgqd,bkqjld->bkgqjl', qq, k_sel).astype(f32) * scale
        s = jnp.where(valid, s, MASK).reshape(B, N_KV_HEADS, GQA, Q_BLOCK, n_top * SEL_BLOCK)
        p = jax.nn.softmax(s, axis=-1).reshape(B, N_KV_HEADS, GQA, Q_BLOCK, n_top, SEL_BLOCK)
        o_sel = jnp.einsum('bkgqjl,bkqjld->bkgqd', p.astype(v_sel.dtype), v_sel)

        kw = lax.dynamic_slice_in_dim(kw_pad, start, WINDOW + Q_BLOCK, axis=2)
        vw = lax.dynamic_slice_in_dim(vw_pad, start, WINDOW + Q_BLOCK, axis=2)
        kpos = start - WINDOW + jnp.arange(WINDOW + Q_BLOCK)
        valid = (kpos[None] <= t[:, None]) & (kpos[None] > t[:, None] - WINDOW) & (kpos[None] >= 0)
        s = jnp.einsum('bkgqd,bksd->bkgqs', qq, kw).astype(f32) * scale
        p = jax.nn.softmax(jnp.where(valid, s, MASK), axis=-1)
        o_win = jnp.einsum('bkgqs,bksd->bkgqd', p.astype(vw.dtype), vw)

        o = gg[..., 0:1] * o_cmp + gg[..., 1:2] * o_sel + gg[..., 2:3] * o_win
        return o.astype(cols.dtype)

    out = lax.map(q_block, jnp.arange(S // Q_BLOCK))
    out = jnp.moveaxis(out, 0, 3).reshape(B, N_KV_HEADS, GQA, S, HEAD_DIM)
    return out.transpose(0, 3, 1, 2, 4).reshape(B, S, N_WIDTH)

def swiglu(x, w_gate, w_up, w_down):
    return (jax.nn.silu(x @ w_gate) * (x @ w_up)) @ w_down

def first_inputs(seed: int = 0) -> dict:
    key = jax.random.key(seed)
    ks = iter(jax.random.split(key, 40))
    f32 = jnp.float32
    L = DEPTH
    nrm = lambda shape, s: jax.random.normal(next(ks), shape, f32) * s
    uni = lambda shape, lo, hi: jax.random.uniform(next(ks), shape, f32, lo, hi)
    x = nrm((BATCH, SEQ, D_MODEL), 1.0)
    positions = (jax.random.randint(next(ks), (BATCH, 1), 0, 4096, jnp.int32)
                 + jnp.arange(SEQ, dtype=jnp.int32)[None, :])
    return {
        "x": x,
        "positions": positions,
        "norm_mix": 1.0 + nrm((L, D_MODEL), 0.02),
        "w_in": nrm((L, D_MODEL, IN_COLS), D_MODEL ** -0.5),
        "mu_shift": uni((L, R_COLS), 0.0, 1.0),
        "w0": uni((L, R_WIDTH), -6.0, -1.0),
        "w2": nrm((L, DECAY_LORA, R_WIDTH), 0.1),
        "a0": nrm((L, R_WIDTH), 0.1),
        "a2": nrm((L, ICLR_LORA, R_WIDTH), 0.1),
        "g2": nrm((L, GATE_LORA, R_WIDTH), GATE_LORA ** -0.5),
        "k_k": 0.85 + nrm((L, R_WIDTH), 0.05),
        "k_a": 1.0 + nrm((L, R_WIDTH), 0.05),
        "r_k": nrm((L, R_HEADS, R_HEAD_DIM), 0.1),
        "lnx_w": 1.0 + nrm((L, R_WIDTH), 0.02),
        "lnx_b": nrm((L, R_WIDTH), 0.01),
        "pe_k": nrm((L, CMP_BLOCK, HEAD_DIM), 0.1),
        "wk1": nrm((L, CMP_BLOCK * HEAD_DIM, CMP_HIDDEN), (CMP_BLOCK * HEAD_DIM) ** -0.5),
        "bk1": nrm((L, CMP_HIDDEN), 0.01),
        "wk2": nrm((L, CMP_HIDDEN, HEAD_DIM), CMP_HIDDEN ** -0.5),
        "pe_v": nrm((L, CMP_BLOCK, HEAD_DIM), 0.1),
        "wv1": nrm((L, CMP_BLOCK * HEAD_DIM, CMP_HIDDEN), (CMP_BLOCK * HEAD_DIM) ** -0.5),
        "bv1": nrm((L, CMP_HIDDEN), 0.01),
        "wv2": nrm((L, CMP_HIDDEN, HEAD_DIM), CMP_HIDDEN ** -0.5),
        "w_out": nrm((L, MIX_WIDTH, D_MODEL), MIX_WIDTH ** -0.5),
        "norm_ffn": 1.0 + nrm((L, D_MODEL), 0.02),
        "w_gate": nrm((L, D_MODEL, D_FF), D_MODEL ** -0.5),
        "w_up": nrm((L, D_MODEL, D_FF), D_MODEL ** -0.5),
        "w_down": nrm((L, D_FF, D_MODEL), D_FF ** -0.5),
        "norm_final": 1.0 + nrm((D_MODEL,), 0.02),
    }

def first_block(x, positions, norm_mix, w_in, mu_shift, w0, w2, a0, a2, g2, k_k, k_a, r_k, lnx_w, lnx_b,
              pe_k, wk1, bk1, wk2, pe_v, wv1, bv1, wv2, w_out, norm_ffn, w_gate, w_up, w_down, norm_final):
    h = x
    for l in range(DEPTH):
        xn = rms_norm(h, norm_mix[l])
        proj = xn @ w_in[l]
        y_r = rwkv7_group(proj[..., :R_COLS], mu_shift[l], w0[l], w2[l], a0[l], a2[l], g2[l],
                          k_k[l], k_a[l], r_k[l], lnx_w[l], lnx_b[l])
        y_n = nsa_group(proj[..., R_COLS:], positions, pe_k[l], wk1[l], bk1[l], wk2[l],
                        pe_v[l], wv1[l], bv1[l], wv2[l])
        h = h + jnp.concatenate([y_r, y_n], axis=-1) @ w_out[l]
        h = h + swiglu(rms_norm(h, norm_ffn[l]), w_gate[l], w_up[l], w_down[l])
    return rms_norm(h, norm_final)


DEPTH_2 = 2

CTX_LEN = 256
GRID_W = 64
N_MOD = 9
D_FF_2 = 2816
EPS = 1e-6
NEG_INF = -1e30
NA_HEADS = 4
NA_WIN_H_MAX = 8
NA_WIN_W = 16
NA_QCB = 16
NA_KCB = 32
NA_WIDTH = NA_HEADS * HEAD_DIM
POOL_WINDOWS = (2, 4, 8, 16)
POOL_GROUPS = 4
POOL_WIDTH = 256
POOL_GC = POOL_WIDTH // POOL_GROUPS
GQA_Q_HEADS = 8
GQA_KV_HEADS = 2
GQA_GROUP = GQA_Q_HEADS // GQA_KV_HEADS
GQA_QB = 128
GQA_Q_WIDTH = GQA_Q_HEADS * HEAD_DIM
GQA_KV_WIDTH = GQA_KV_HEADS * HEAD_DIM
ROPE_THETA_2 = 10000.0
OFF_A_Q = 0
OFF_A_K = OFF_A_Q + NA_WIDTH
OFF_A_V = OFF_A_K + NA_WIDTH
OFF_B_U = OFF_A_V + NA_WIDTH
OFF_C_Q = OFF_B_U + POOL_WIDTH
OFF_C_K = OFF_C_Q + GQA_Q_WIDTH
OFF_C_V = OFF_C_K + GQA_KV_WIDTH
D_IN = OFF_C_V + GQA_KV_WIDTH
D_MIX = NA_WIDTH + POOL_WIDTH + GQA_Q_WIDTH


def _rmsnorm(x, g):
    x32 = x.astype(jnp.float32)
    y = x32 * lax.rsqrt(jnp.mean(x32 * x32, axis=-1, keepdims=True) + EPS)
    return (y * g.astype(jnp.float32)).astype(x.dtype)

def _modulate(h, shift, scale):
    return h * (1 + scale) + shift

def _swiglu(h, w_up, w_down):
    a, b = jnp.split(h @ w_up, 2, axis=-1)
    return (jax.nn.silu(a) * b) @ w_down

def _half_ffn(h, g, shift, scale, gate, w_up, w_down):
    return h + 0.5 * gate * _swiglu(_modulate(_rmsnorm(h, g), shift, scale), w_up, w_down)

def _rope_axis(x, ang):
    m = x.shape[-1] // 2
    x32 = x.astype(jnp.float32)
    x1, x2 = x32[..., :m], x32[..., m:]
    cos = jnp.cos(ang)[:, None, :]
    sin = jnp.sin(ang)[:, None, :]
    return jnp.concatenate([x1 * cos - x2 * sin, x1 * sin + x2 * cos], axis=-1)

def _rope_2d(x, ang_row, ang_col):
    half = x.shape[-1] // 2
    out = jnp.concatenate([_rope_axis(x[..., :half], ang_row), _rope_axis(x[..., half:], ang_col)], axis=-1)
    return out.astype(x.dtype)

def _gqa_attend(q, k, v):
    s = jnp.einsum('bqkgd,bskd->bkgqs', q, k, preferred_element_type=jnp.float32) * (q.shape[-1] ** -0.5)
    p = jax.nn.softmax(s, axis=-1).astype(v.dtype)
    return jnp.einsum('bkgqs,bskd->bqkgd', p, v)

def _gqa_blocks(q, k_all, v_all):
    bn, n = q.shape[0], q.shape[1]
    nqb = n // GQA_QB
    qb = q.reshape(bn, nqb, GQA_QB, GQA_KV_HEADS, GQA_GROUP, HEAD_DIM).transpose(1, 0, 2, 3, 4, 5)
    o = lax.map(lambda blk: _gqa_attend(blk, k_all, v_all), qb)
    return o.transpose(1, 0, 2, 3, 4, 5).reshape(bn, n, GQA_Q_WIDTH)

def _neighbourhood_attn(q, k, v, k_ctx, v_ctx, rpb):
    bn, n, nh, dh = q.shape
    rows = n // GRID_W
    kh = min(NA_WIN_H_MAX, rows)
    ncb = GRID_W // NA_QCB
    col = jnp.arange(GRID_W)
    win_c0 = jnp.clip(col - NA_WIN_W // 2, 0, GRID_W - NA_WIN_W)
    blk_c0 = jnp.clip(win_c0[::NA_QCB], 0, GRID_W - NA_KCB)
    key_col = blk_c0[:, None] + jnp.arange(NA_KCB)
    q_c0 = win_c0.reshape(ncb, NA_QCB)[:, :, None]
    kc = key_col[:, None, :]
    valid = (kc >= q_c0) & (kc < q_c0 + NA_WIN_W)
    dx = kc - col.reshape(ncb, NA_QCB)[:, :, None]
    dx_idx = jnp.clip(dx, -(NA_WIN_W - 1), NA_WIN_W - 1) + NA_WIN_W - 1
    scale = dh ** -0.5
    q_grid = q.reshape(bn, rows, ncb, NA_QCB, nh, dh)

    def one_row(r):
        q_r = lax.dynamic_index_in_dim(q_grid, r, axis=1, keepdims=False)
        r0 = jnp.clip(r - kh // 2, 0, rows - kh)
        key_row = r0 + jnp.arange(kh)
        tok = key_row[None, :, None] * GRID_W + key_col[:, None, :]
        k_blk = k[:, tok]
        v_blk = v[:, tok]
        s_lat = jnp.einsum('bjqhd,bjykhd->bhjqyk', q_r, k_blk, preferred_element_type=jnp.float32) * scale
        dy_idx = key_row - r + NA_WIN_H_MAX - 1
        bias = rpb[:, dy_idx[None, None, :, None], dx_idx[:, :, None, :]]
        s_lat = jnp.where(valid[:, :, None, :], s_lat + bias.astype(jnp.float32), NEG_INF)
        s_lat = s_lat.reshape(bn, nh, ncb, NA_QCB, kh * NA_KCB)
        s_ctx = jnp.einsum('bjqhd,bchd->bhjqc', q_r, k_ctx, preferred_element_type=jnp.float32) * scale
        p = jax.nn.softmax(jnp.concatenate([s_lat, s_ctx], axis=-1), axis=-1).astype(v.dtype)
        p_lat = p[..., :kh * NA_KCB].reshape(bn, nh, ncb, NA_QCB, kh, NA_KCB)
        p_ctx = p[..., kh * NA_KCB:]
        o = jnp.einsum('bhjqyk,bjykhd->bjqhd', p_lat, v_blk) + jnp.einsum('bhjqc,bchd->bjqhd', p_ctx, v_ctx)
        return o.reshape(bn, GRID_W, nh, dh)

    o = lax.map(one_row, jnp.arange(rows))
    return o.transpose(1, 0, 2, 3, 4).reshape(bn, n, nh * dh)

def _pool_mix(u, w_pool, scale):
    bn, n, _ = u.shape
    u32 = u.astype(jnp.float32)
    cs = jnp.concatenate([jnp.zeros_like(u32[:, :1]), jnp.cumsum(u32, axis=1)], axis=1)
    cs = cs.reshape(bn, n + 1, POOL_GROUPS, POOL_GC)
    t = jnp.arange(n)[:, None]
    win = jnp.array(POOL_WINDOWS, dtype=jnp.int32)[None, :]
    lo = jnp.clip(t - win // 2, 0, n)
    hi = jnp.clip(t - win // 2 + win, 0, n)
    g_idx = jnp.arange(POOL_GROUPS)[None, :]
    sums = cs[:, hi, g_idx] - cs[:, lo, g_idx]
    mean = sums / (hi - lo).astype(jnp.float32)[None, :, :, None]
    y = (mean - u32.reshape(bn, n, POOL_GROUPS, POOL_GC)).astype(u.dtype)
    y = jnp.einsum('blgc,gcd->blgd', y, w_pool)
    return y.reshape(bn, n, POOL_WIDTH) * scale

def second_inputs(seed: int = 0) -> dict:
    key = jax.random.key(seed)
    ks = jax.random.split(key, 20)
    nrm = jax.random.normal
    f32 = jnp.float32
    return {
        'x': nrm(ks[0], (BATCH, SEQ, D_MODEL), f32),
        'c': nrm(ks[1], (BATCH, D_MODEL), f32),
        'ctx': nrm(ks[2], (BATCH, CTX_LEN, D_MODEL), f32),
        'c_ctx': nrm(ks[3], (D_MODEL,), f32),
        'w_ada': nrm(ks[4], (DEPTH_2, D_MODEL, N_MOD * D_MODEL), f32) * D_MODEL ** -0.5,
        'b_ada': nrm(ks[5], (DEPTH_2, N_MOD * D_MODEL), f32) * 0.02,
        'norm_g': 1.0 + 0.05 * nrm(ks[6], (DEPTH_2, 3, D_MODEL), f32),
        'ffn1_up': nrm(ks[7], (DEPTH_2, D_MODEL, 2 * D_FF_2), f32) * D_MODEL ** -0.5,
        'ffn1_down': nrm(ks[8], (DEPTH_2, D_FF_2, D_MODEL), f32) * D_FF_2 ** -0.5,
        'ffn2_up': nrm(ks[9], (DEPTH_2, D_MODEL, 2 * D_FF_2), f32) * D_MODEL ** -0.5,
        'ffn2_down': nrm(ks[10], (DEPTH_2, D_FF_2, D_MODEL), f32) * D_FF_2 ** -0.5,
        'w_in': nrm(ks[11], (DEPTH_2, D_MODEL, D_IN), f32) * D_MODEL ** -0.5,
        'w_out': nrm(ks[12], (DEPTH_2, D_MIX, D_MODEL), f32) * D_MIX ** -0.5,
        'na_rpb': nrm(ks[13], (DEPTH_2, NA_HEADS, 2 * NA_WIN_H_MAX - 1, 2 * NA_WIN_W - 1), f32) * 0.1,
        'pool_w': nrm(ks[14], (DEPTH_2, POOL_GROUPS, POOL_GC, POOL_GC), f32) * POOL_GC ** -0.5,
        'pool_scale': 1.0 + 0.1 * nrm(ks[15], (DEPTH_2, POOL_WIDTH), f32),
        'q_norm_g': 1.0 + 0.05 * nrm(ks[16], (DEPTH_2, HEAD_DIM), f32),
        'k_norm_g': 1.0 + 0.05 * nrm(ks[17], (DEPTH_2, HEAD_DIM), f32),
        'final_g': 1.0 + 0.05 * nrm(ks[18], (D_MODEL,), f32),
    }

def second_block(x, c, ctx, c_ctx, w_ada, b_ada, norm_g, ffn1_up, ffn1_down, ffn2_up, ffn2_down,
              w_in, w_out, na_rpb, pool_w, pool_scale, q_norm_g, k_norm_g, final_g):
    bn, n, d = x.shape
    ncx = ctx.shape[1]
    pos = jnp.arange(n)
    inv_freq = ROPE_THETA_2 ** (-jnp.arange(0, HEAD_DIM // 2, 2, dtype=jnp.float32) / (HEAD_DIM // 2))
    ang_row = (pos // GRID_W).astype(jnp.float32)[:, None] * inv_freq[None, :]
    ang_col = (pos % GRID_W).astype(jnp.float32)[:, None] * inv_freq[None, :]
    h_x, h_c = x, ctx
    for l in range(DEPTH_2):
        last = l == DEPTH_2 - 1
        mod_x = (jax.nn.silu(c) @ w_ada[l] + b_ada[l]).reshape(bn, 1, N_MOD, d)
        mod_c = (jax.nn.silu(c_ctx) @ w_ada[l] + b_ada[l]).reshape(1, 1, N_MOD, d)
        h_x = _half_ffn(h_x, norm_g[l, 0], mod_x[:, :, 0], mod_x[:, :, 1], mod_x[:, :, 2], ffn1_up[l], ffn1_down[l])
        h_c = _half_ffn(h_c, norm_g[l, 0], mod_c[:, :, 0], mod_c[:, :, 1], mod_c[:, :, 2], ffn1_up[l], ffn1_down[l])
        a_x = _modulate(_rmsnorm(h_x, norm_g[l, 1]), mod_x[:, :, 3], mod_x[:, :, 4])
        a_c = _modulate(_rmsnorm(h_c, norm_g[l, 1]), mod_c[:, :, 3], mod_c[:, :, 4])
        p_x = a_x @ w_in[l]
        kv_a_c = a_c @ w_in[l][:, OFF_A_K:OFF_B_U]
        kv_c_c = a_c @ w_in[l][:, OFF_C_K:D_IN]
        q_a = p_x[..., OFF_A_Q:OFF_A_K].reshape(bn, n, NA_HEADS, HEAD_DIM)
        k_a = p_x[..., OFF_A_K:OFF_A_V].reshape(bn, n, NA_HEADS, HEAD_DIM)
        v_a = p_x[..., OFF_A_V:OFF_B_U].reshape(bn, n, NA_HEADS, HEAD_DIM)
        k_a_c = kv_a_c[..., :NA_WIDTH].reshape(bn, ncx, NA_HEADS, HEAD_DIM)
        v_a_c = kv_a_c[..., NA_WIDTH:].reshape(bn, ncx, NA_HEADS, HEAD_DIM)
        q_c = _rope_2d(_rmsnorm(p_x[..., OFF_C_Q:OFF_C_K].reshape(bn, n, GQA_Q_HEADS, HEAD_DIM), q_norm_g[l]), ang_row, ang_col)
        q_c = q_c.reshape(bn, n, GQA_KV_HEADS, GQA_GROUP, HEAD_DIM)
        k_c = _rope_2d(_rmsnorm(p_x[..., OFF_C_K:OFF_C_V].reshape(bn, n, GQA_KV_HEADS, HEAD_DIM), k_norm_g[l]), ang_row, ang_col)
        v_c = p_x[..., OFF_C_V:D_IN].reshape(bn, n, GQA_KV_HEADS, HEAD_DIM)
        k_c_c = _rmsnorm(kv_c_c[..., :GQA_KV_WIDTH].reshape(bn, ncx, GQA_KV_HEADS, HEAD_DIM), k_norm_g[l])
        v_c_c = kv_c_c[..., GQA_KV_WIDTH:].reshape(bn, ncx, GQA_KV_HEADS, HEAD_DIM)
        o_a = _neighbourhood_attn(q_a, k_a, v_a, k_a_c, v_a_c, na_rpb[l])
        o_b = _pool_mix(p_x[..., OFF_B_U:OFF_C_Q], pool_w[l], pool_scale[l])
        o_c = _gqa_blocks(q_c, jnp.concatenate([k_c, k_c_c], axis=1), jnp.concatenate([v_c, v_c_c], axis=1))
        h_x = h_x + mod_x[:, :, 5] * (jnp.concatenate([o_a, o_b, o_c], axis=-1) @ w_out[l])
        h_x = _half_ffn(h_x, norm_g[l, 2], mod_x[:, :, 6], mod_x[:, :, 7], mod_x[:, :, 8], ffn2_up[l], ffn2_down[l])
        if not last:
            q_a_c = (a_c @ w_in[l][:, OFF_A_Q:OFF_A_K]).reshape(bn, ncx, NA_HEADS, 1, HEAD_DIM)
            u_c = a_c @ w_in[l][:, OFF_B_U:OFF_C_Q]
            q_c_c = _rmsnorm((a_c @ w_in[l][:, OFF_C_Q:OFF_C_K]).reshape(bn, ncx, GQA_Q_HEADS, HEAD_DIM), q_norm_g[l])
            q_c_c = q_c_c.reshape(bn, ncx, GQA_KV_HEADS, GQA_GROUP, HEAD_DIM)
            oa_c = _gqa_attend(q_a_c, k_a_c, v_a_c).reshape(bn, ncx, NA_WIDTH)
            ob_c = _pool_mix(u_c, pool_w[l], pool_scale[l])
            oc_c = _gqa_attend(q_c_c, k_c_c, v_c_c).reshape(bn, ncx, GQA_Q_WIDTH)
            h_c = h_c + mod_c[:, :, 5] * (jnp.concatenate([oa_c, ob_c, oc_c], axis=-1) @ w_out[l])
            h_c = _half_ffn(h_c, norm_g[l, 2], mod_c[:, :, 6], mod_c[:, :, 7], mod_c[:, :, 8], ffn2_up[l], ffn2_down[l])
    return _rmsnorm(h_x, final_g)


def setup_inputs(seed=0):
    out = dict(first_inputs(seed))
    for name, value in second_inputs(seed + 1).items():
        if name != "x":
            out[name + "_2"] = value
    return out


def reference(
    x, positions, norm_mix, w_in, mu_shift, w0, w2, a0, a2, g2, k_k, k_a, r_k, lnx_w, lnx_b,
    pe_k, wk1, bk1, wk2, pe_v, wv1, bv1, wv2, w_out, norm_ffn, w_gate, w_up, w_down, norm_final,
    c_2, ctx_2, c_ctx_2, w_ada_2, b_ada_2, norm_g_2, ffn1_up_2, ffn1_down_2, ffn2_up_2,
    ffn2_down_2, w_in_2, w_out_2, na_rpb_2, pool_w_2, pool_scale_2, q_norm_g_2, k_norm_g_2,
    final_g_2,
):
    x = first_block(
        x, positions, norm_mix, w_in, mu_shift, w0, w2, a0, a2, g2, k_k, k_a, r_k, lnx_w, lnx_b,
        pe_k, wk1, bk1, wk2, pe_v, wv1, bv1, wv2, w_out, norm_ffn, w_gate, w_up, w_down,
        norm_final,
    )
    return second_block(
        x, c_2, ctx_2, c_ctx_2, w_ada_2, b_ada_2, norm_g_2, ffn1_up_2, ffn1_down_2, ffn2_up_2,
        ffn2_down_2, w_in_2, w_out_2, na_rpb_2, pool_w_2, pool_scale_2, q_norm_g_2, k_norm_g_2,
        final_g_2,
    )


_drawn_inputs = setup_inputs


def setup_inputs(seed=0):
    import zlib

    import numpy as np

    out = dict(_drawn_inputs(seed))
    spreads = {}
    factors = {'norm_mix': 3.406,
     'w2': 3.703,
     'a0': 3.51,
     'k_k': 3.157,
     'lnx_w': 6.706,
     'lnx_b': 8.0,
     'pe_k': 8.0,
     'bk1': 8.0,
     'pe_v': 2.952,
     'bv1': 8.0,
     'norm_ffn': 3.924,
     'na_rpb_2': 8.0,
     'q_norm_g_2': 8.0,
     'k_norm_g_2': 8.0}
    for name, (base, spread) in spreads.items():
        noise = np.random.default_rng([zlib.crc32(name.encode()), seed]).standard_normal(out[name].shape)
        drawn = base * np.exp(spread * noise) if base else spread * noise
        out[name] = __import__('jax').numpy.asarray(drawn.astype(out[name].dtype))
    for name, factor in factors.items():
        out[name] = (out[name] * factor).astype(out[name].dtype)
    return out
```

```python
from contextlib import ExitStack
import math

import numpy as np
import concourse.bass as bass
from concourse import mybir

F32 = mybir.dt.float32
F32R = mybir.dt.float32r
I32 = mybir.dt.int32
ALU = mybir.AluOpType
ACT = mybir.ActivationFunctionType
AX_X = mybir.AxisListType.X

P = 128
D = 1024
KT = D // P
S = 256
T2 = 2 * S
FF = 2816
FT = FF // P
FH = FT // 2
R_COLS, N_COLS = 1824, 1304
LAYERS = 2
N_MOD = 9
HD = 64
NEG = -1e30
RING = 3
CH = KT * 2 * P
DECAY = math.exp(-0.5)
SCALE = HD ** -0.5
CHUNK = 64
NCMP = 15


def const_layout():
    names = [("ident", P), ("ones", P), ("bd", P), ("rot1", P), ("rot2", P), ("bdmask", P),
             ("m_su", P), ("m_u", P), ("m16", P), ("moff", P), ("m16t", P),
             ("scan0", S), ("freq", 1), ("causal", 2 * P), ("cmp_add", 2 * NCMP), ("cmp_ok", 2 * NCMP),
             ("na_mask", S), ("cos2", S), ("sin2", S), ("pool_inv", 2 * S)]
    at, n = {}, 0
    for name, w in names:
        at[name] = (n, w)
        n += w
    return at, n


def const_array():
    at, n = const_layout()
    c = np.zeros((P, n), np.float32)

    def put(name, a):
        o, w = at[name]
        c[:, o:o + w] = np.asarray(a, np.float32).reshape(P, w)

    p = np.arange(P)[:, None]
    f = np.arange(P)[None, :]
    put("ident", p == f)
    put("ones", np.full((P, P), 1.0 / D))
    put("bd", p // HD == f // HD)
    put("bdmask", p // HD == f // HD)
    r1 = np.zeros((P, P))
    r2 = np.zeros((P, P))
    for h in (0, HD):
        for i in range(8):
            r1[h + i + 8, h + i] = -1.0
            r1[h + i, h + i + 8] = 1.0
        for q in (0, 32):
            for i in range(16):
                r2[h + q + i + 16, h + q + i] = -1.0
                r2[h + q + i, h + q + i + 16] = 1.0
    put("rot1", r1)
    put("rot2", r2)
    same = p // CHUNK == f // CHUNK
    same16 = p // 16 == f // 16
    put("m_su", same & (p < f))
    put("m_u", same & (p <= f))
    put("m16", same16 & (p < f))
    put("moff", same & (p < f) & ~same16)
    put("m16t", same16 & (f < p))
    t = np.arange(S)
    put("scan0", np.broadcast_to((t % CHUNK != 0), (P, S)))
    inv = np.power(np.float32(500000.0), -np.arange(8, dtype=np.float32) * np.float32(2.0) / np.float32(16))
    fr = np.zeros(P, np.float32)
    for h in (0, HD):
        fr[h:h + 8] = inv
        fr[h + 8:h + 16] = inv
    put("freq", fr)
    put("causal", np.concatenate([np.zeros((P, P)), np.where(f <= p, 0.0, NEG)], 1))
    n_ = np.arange(NCMP)
    ok = np.concatenate([(16 * n_ + 31)[None, :] <= (i * P + p) for i in range(2)], 1)
    put("cmp_ok", ok)
    put("cmp_add", np.where(ok, 0.0, NEG))
    qc = p % 64
    kc = (t % 64)[None, :]
    c0 = np.clip(qc - 8, 0, 48)
    put("na_mask", np.where((kc >= c0) & (kc < c0 + 16), 0.0, NEG))
    inv2 = np.float32(10000.0) ** (-np.arange(0, 32, 2, dtype=np.float32) / np.float32(32))
    ang = np.zeros((P, S), np.float32)
    for h in (0, HD):
        for i in range(16):
            ang[h + i] = ang[h + i + 16] = (t // 64).astype(np.float32) * inv2[i]
            ang[h + 32 + i] = ang[h + 48 + i] = (t % 64).astype(np.float32) * inv2[i]
    put("cos2", np.cos(ang))
    put("sin2", np.sin(ang))
    pin = np.zeros((P, 2, S))
    for g, w in enumerate((2, 4, 8, 16)):
        lo = np.clip(t - w // 2, 0, S)
        hi = np.clip(t - w // 2 + w, 0, S)
        pin[(g % 2) * 64:(g % 2) * 64 + 64, g // 2] = 1.0 / (hi - lo)
    put("pool_inv", pin)
    return c


def vec_layout():
    names = [("norm_mix", 8), ("norm_ffn", 8), ("norm_final", 8), ("final_g", 8), ("norm_g", 48),
             ("mu", 15), ("w0", 4), ("a0", 4), ("k_k", 4), ("k_a", 4), ("r_k", 4), ("lnx_w", 4), ("lnx_b", 4),
             ("pe_k", 16), ("pe_v", 16), ("bk1", 2), ("bv1", 2), ("b_ada", 144), ("pool_scale", 4),
             ("q_g", 2), ("k_g", 2), ("c", 16)]
    at, n = {}, 0
    for name, w in names:
        at[name] = (n, w)
        n += w
    return at, n


CAT, CN = const_layout()
VAT, VN = vec_layout()
M_G2, M_G2T, M_LORA, M_CK2, M_CV2, M_POOL = 0, 512, 1024, 1536, 1792, 1920
MN = 1920 + 2 * 2 * P


def counts(names):
    return {n: i + 1 for i, n in enumerate(names)}


def one(ap):
    return ap.unsqueeze(1)


def wait(eng, sem, v):
    if not isinstance(v, int) or v > 0:
        eng.wait_ge(sem, v)


def chunk_loop(eng, base, n, body):
    lead = min(n, RING) if base == 0 else 0
    rest = (n - lead) // RING
    for i in range(lead):
        body(base + i, (base + i) // RING, (base + i) % RING, i)
    b = base + lead
    if rest > 1:
        with eng.Fori(0, rest) as r:
            for j in range(RING):
                body(b + j + RING * r, (b + j) // RING + r, (b + j) % RING, lead + j + RING * r)
    else:
        rest = 0
    for i in range(lead + rest * RING, n):
        body(base + i, (base + i) // RING, (base + i) % RING, i)


class Product:

    def __init__(self, base, name, n, kt, mt, tokens, kind, first=0, ahead=None):
        self.base, self.name, self.n, self.kt, self.mt = base, name, n, kt, mt
        self.tokens, self.kind, self.first, self.ahead = tokens, kind, first, ahead
        self.size = kt * mt * P
        self.end = base + n


def plan():
    out = []

    def add(name, n, kt, mt, tokens, kind, first=0):
        base = out[-1].end if out else 0
        out.append(Product(base, name, n, kt, mt, tokens, kind, first))
        return out[-1]

    add("w_in", 12, KT, 2, S, "proj1")
    add("w_tail", 1, KT, 1, S, "tail1")
    add("w_cmp", 4, KT, 2, 2 * NCMP, "cmp")
    add("w_out", 4, KT, 2, S, "res")
    for half in range(2):
        add("w_gu", FH, KT, 2, S, "gu", half * FH)
        add("w_dn", KT, FH, 1, S, "down", half * KT)
    for l in range(LAYERS):
        for half in range(2):
            add(f"w_gu1_{l}", FH, KT, 2, T2, "gu", half * FH)
            add(f"w_dn1_{l}", KT, FH, 1, T2, "down", half * KT)
        add(f"w_in_{l}", 7, KT, 2, T2, "proj2")
        t = T2 if l == 0 else S
        add(f"w_out_{l}", 4, KT, 2, t, "res")
        for half in range(2):
            add(f"w_gu2_{l}", FH, KT, 2, t, "gu", half * FH)
            add(f"w_dn2_{l}", KT, FH, 1, t, "down", half * KT)
    for a, b in zip(out, out[1:]):
        if a.kind not in ("cmp", "proj2"):
            a.ahead = b
    return out


def program(nc, dram, out):
    ctx = ExitStack()
    cursor = [16512]

    def place(name, shape, dt, off=None):
        n = int(np.prod(shape[1:])) * 4
        if off is None:
            off = cursor[0]
            cursor[0] += (n + 31) // 32 * 32
        return nc.alloc_sbuf_tensor_at(name, shape, dt, offset=off)

    def sem(name):
        return ctx.enter_context(nc.semaphore(name))

    h = place("h", [P, KT, T2], F32)
    at_a = cursor[0]
    a_hi = place("a_hi", [P, KT, T2], F32R)
    a_lo = place("a_lo", [P, KT, T2], F32R)
    at_f = cursor[0]
    ff_hi = place("ff_hi", [P, FH, T2], F32R)
    ff_lo = place("ff_lo", [P, FH, T2], F32R)
    raw = [place(f"raw{i}", [P, CH], F32) for i in range(RING)]
    at_w = cursor[0]
    w_hi = [place(f"w_hi{i}", [P, CH], F32R) for i in range(RING)]
    w_lo = [place(f"w_lo{i}", [P, CH], F32R) for i in range(RING)]
    consts = place("consts_sb", [P, CN], F32)
    vecs = place("vecs_sb", [P, VN], F32)
    mats = place("mats_sb", [P, MN], F32)
    mod = place("mod", [P, LAYERS, N_MOD * KT, 2], F32)
    gmod = place("gmod", [P, LAYERS, 3, KT, 2], F32)
    half_gate = place("half_gate", [P, LAYERS, 2, KT, 2], F32)
    silu_c = place("silu_c", [P, KT, 2], F32)
    eps = place("eps", [P, 4], F32)
    rt = place("rt", [P, T2], F32)
    rs = place("rs", [P, T2], F32)
    silu_g = place("silu_g", [P, T2], F32)
    gu = [place(f"gu{i}", [P, T2], F32) for i in range(RING)]
    sq = place("sq", [P, KT, T2], F32, at_f)
    nrm = place("nrm", [P, KT, T2], F32, at_f + 16384)
    p1 = place("p1", [P, 25, S], F32, at_f)
    ada_ring = [place(f"ada_ring{i}", [P, CH], F32, at_f + 27648 + 8192 * i) for i in range(2)]
    p2 = place("p2", [P, 14, T2], F32, at_f)
    ps = [ctx.enter_context(nc.psum_tensor(f"ps{i}", [P, 512], F32)) for i in range(8)]

    def con(name, lo=0, hi=None):
        o, w = CAT[name]
        return consts[:, o + lo:o + (w if hi is None else hi)]

    def vcol(name, i=0, n=1, rows=slice(0, P)):
        o = VAT[name][0] + i
        return vecs[rows, o:o + n]

    x_loaded = sem("x_loaded")
    consts_loaded = sem("consts_loaded")
    landed = [sem(f"landed{i}") for i in range(RING)]
    hi_ready = sem("hi_ready")
    lo_ready = sem("lo_ready")
    chunk_mult = sem("chunk_mult")
    chunk_drained = sem("chunk_drained")
    silu_ready = sem("silu_ready")
    ffhi_ready = sem("ffhi_ready")
    ff_ready = sem("ff_ready")
    sq_ready = sem("sq_ready")
    ssum_ready = sem("ssum_ready")
    ms_ready = sem("ms_ready")
    rt_ready = sem("rt_ready")
    nrm_ready = sem("nrm_ready")
    ahi_ready = sem("ahi_ready")
    a_ready = sem("a_ready")
    dve_step = sem("dve_step")
    act_step = sem("act_step")
    pe_phase = sem("pe_phase")
    act_phase = sem("act_phase")
    dve_phase = sem("dve_phase")
    ada_landed = [sem(f"ada_landed{i}") for i in range(2)]
    ada_mult = sem("ada_mult")
    silu_c_ready = sem("silu_c_ready")
    first_done = sem("first_done")
    out_ready = sem("out_ready")
    out_stored = sem("out_stored")

    products = plan()
    gu_before = {}
    n_gu = 0
    for pr in products:
        gu_before[pr.base] = n_gu
        if pr.kind == "gu":
            n_gu += pr.n
    product_at = {}
    for pr in products:
        product_at.setdefault(pr.name, []).append(pr)

    def source(pr, i):
        return dram[pr.name][bass.ds(pr.first + i, 1)].rearrange("a p f -> p (a f)") if not isinstance(i, int) \
            else dram[pr.name][pr.first + i]

    norms = {"mix": (0, S), "ffn": (1, S), "final1": (2, S)}
    for l in range(LAYERS):
        for n in range(3):
            norms[f"{l}.{n}"] = (3 + 3 * l + n, T2 if (l == 0 or n < 2) else S)
    norms["final2"] = (9, S)
    a_norms = [k for k in norms if k not in ("final1", "final2")]

    def split_hi(act, c, turn, slot, size):
        act.wait_ge(landed[slot], 16 * (turn + 1))
        wait(act, chunk_mult, c - RING + 1)
        nc.scalar.activation(w_hi[slot][:, 0:size], raw[slot][:, 0:size], ACT.Copy).then_inc(hi_ready, 1)

    def split_lo(dve, c, slot, size):
        dve.wait_ge(hi_ready, c + 1)
        nc.vector.tensor_tensor(w_lo[slot][:, 0:size], raw[slot][:, 0:size],
                                w_hi[slot][:, 0:size].bitcast(F32), ALU.subtract).then_inc(lo_ready, 1)

    def multiply(pe, pr, c, slot, banks, lhs, rhs, start=True, stop=True, before=None):
        pe.wait_ge(lo_ready, c + 1)
        wait(pe, chunk_drained, c - RING + 1)
        for m in range(pr.mt):
            for k in range(pr.kt):
                if before is not None and m == 0:
                    before(k)
                w1, w2 = lhs(slot, m, k)
                a1, a2 = rhs(k)
                nc.tensor.matmul(banks[m], w1, a1, start=start and k == 0, stop=False)
                nc.tensor.matmul(banks[m], w1, a2, start=False, stop=False)
                last = nc.tensor.matmul(banks[m], w2, a1, start=False, stop=stop and k == pr.kt - 1)
        last.then_inc(chunk_mult, 1)

    def by_cols(kt, width):
        def lhs(slot, m, k):
            o = k * width + m * P
            return w_hi[slot][:, o:o + P], w_lo[slot][:, o:o + P]
        return lhs

    def by_part(slot, m, k):
        o = (m * KT + k) * P
        return w_hi[slot][:, o:o + P], w_lo[slot][:, o:o + P]

    def bank(slot, m, n):
        return ps[2 * slot + m][:, 0:n]

    def pe_product(pe, pr, a_mark=None):
        t = pr.tokens
        lhs = by_part if pr.kind == "gu" else by_cols(pr.kt, pr.mt * P)
        if pr.kind == "down":
            pe.wait_ge(ff_ready, gu_before[pr.base])
            rhs = lambda k: (ff_hi[:, k, 0:t], ff_lo[:, k, 0:t])
        else:
            rhs = lambda k: (a_hi[:, k, 0:t], a_lo[:, k, 0:t])
        if a_mark is not None:
            pe.wait_ge(a_ready, a_mark)
        if pr.kind == "proj2":
            for i in range(pr.n):
                c = pr.base + i
                n = T2 if pr.name == "w_in_0" or i in (1, 2, 6) else S
                multiply(pe, pr, c, c % RING, [bank(c % RING, m, n) for m in range(2)], lhs,
                         lambda k: (a_hi[:, k, 0:n], a_lo[:, k, 0:n]))
            return
        chunk_loop(pe, pr.base, pr.n, lambda c, turn, slot, i: multiply(
            pe, pr, c, slot, [bank(slot, m, t) for m in range(pr.mt)], lhs, rhs))

    def staged(eng, pr, split, evac, chained):
        if not chained:
            split(pr.base, pr.base // RING, pr.base % RING, pr.size)

        def body(c, turn, slot, i):
            s1 = (slot + 1) % RING
            split(c + 1, turn + (slot + 1) // RING, s1, pr.size)
            evac(c, turn, slot, i)

        chunk_loop(eng, pr.base, pr.n - 1, body)
        c = pr.end - 1
        if pr.ahead is not None:
            split(c + 1, (c + 1) // RING, (c + 1) % RING, pr.ahead.size)
        evac(c, c // RING, c % RING, pr.n - 1)

    chained = {pr.base: (n > 0 and products[n - 1].ahead is pr) for n, pr in enumerate(products)}

    def act_product(act, pr):
        t = pr.tokens

        def split(c, turn, slot, size):
            split_hi(act, c, turn, slot, size)

        def evac(c, turn, slot, i):
            if pr.kind != "gu":
                return
            act.wait_ge(chunk_mult, c + 1)
            nc.scalar.activation(silu_g[:, 0:t], ps[2 * slot][:, 0:t], ACT.Silu).then_inc(silu_ready, 1)
            act.wait_ge(chunk_drained, c + 1)
            nc.scalar.activation(ff_hi[:, bass.ds(i, 1), 0:t], one(gu[slot][:, 0:t]), ACT.Copy).then_inc(ffhi_ready, 1)

        staged(act, pr, split, evac, chained[pr.base])

    def dve_product(dve, pr, gate=None):
        t = pr.tokens

        def split(c, turn, slot, size):
            split_lo(dve, c, slot, size)

        def evac(c, turn, slot, i):
            if pr.kind == "gu":
                u = gu_before[pr.base] + i
                dve.wait_ge(silu_ready, u + 1)
                nc.vector.tensor_tensor(gu[slot][:, 0:t], ps[2 * slot + 1][:, 0:t], silu_g[:, 0:t],
                                        ALU.mult).then_inc(chunk_drained, 1)
                dve.wait_ge(ffhi_ready, u + 1)
                nc.vector.tensor_tensor(ff_lo[:, bass.ds(i, 1), 0:t], one(gu[slot][:, 0:t]),
                                        ff_hi[:, bass.ds(i, 1), 0:t].bitcast(F32),
                                        ALU.subtract).then_inc(ff_ready, 1)
                return
            dve.wait_ge(chunk_mult, c + 1)
            for m in range(pr.mt):
                j = pr.mt * i + m
                b = ps[2 * slot + m]
                if pr.kind in ("proj1", "tail1"):
                    dst = p1[:, bass.ds(j + (24 if pr.kind == "tail1" else 0), 1), :]
                    last = nc.vector.tensor_copy(dst, one(b[:, 0:t]))
                elif pr.kind == "proj2":
                    n = T2 if pr.name == "w_in_0" or i in (1, 2, 6) else S
                    last = nc.vector.tensor_copy(p2[:, j, 0:n], b[:, 0:n])
                elif gate is None:
                    hk = h[:, bass.ds(j, 1), 0:t]
                    last = nc.vector.tensor_tensor(hk, one(b[:, 0:t]), hk, ALU.add)
                else:
                    for w in range(t // S):
                        hk = h[:, bass.ds(j, 1), w * S:(w + 1) * S]
                        last = nc.vector.scalar_tensor_tensor(hk, one(b[:, w * S:(w + 1) * S]),
                                                              gate(j, w), hk, ALU.mult, ALU.add)
            last.then_inc(chunk_drained, 1)

        if pr.kind == "proj2":
            if not chained[pr.base]:
                split(pr.base, 0, pr.base % RING, pr.size)
            for i in range(pr.n):
                c = pr.base + i
                if i + 1 < pr.n:
                    split(c + 1, 0, (c + 1) % RING, pr.size)
                evac(c, 0, c % RING, i)
            return
        staged(dve, pr, split, evac, chained[pr.base])

    def norm_serial(key, a=False):
        keys = a_norms if a else list(norms)
        return keys.index(key)

    def gain(key, k, w):
        if "." not in key:
            name, i = {"mix": ("norm_mix", k), "ffn": ("norm_ffn", k), "final1": ("norm_final", k),
                       "final2": ("final_g", k)}[key]
            return vcol(name, i)
        l, n = int(key[0]), int(key[2])
        return gmod[:, l, n, k, w:w + 1]

    def halves(key):
        t = norms[key][1]
        if "." not in key:
            return [(0, slice(0, t))]
        return [(w, slice(w * S, (w + 1) * S)) for w in range(t // S)]

    def shift(key, k, w):
        return mod[:, int(key[0]), 3 * int(key[2]) * KT + k, w:w + 1]

    def act_norm(act, key):
        n, t = norm_serial(key), norms[key][1]
        for k in range(KT):
            nc.scalar.activation(sq[:, k, 0:t], h[:, k, 0:t], ACT.Square).then_inc(sq_ready, 1)
        act.wait_ge(ms_ready, n + 1)
        nc.scalar.activation(rt[:, 0:t], ps[7][:, 0:t], ACT.Sqrt, bias=eps[:, 0:1]).then_inc(rt_ready, 1)
        if key.startswith("final"):
            return
        na = norm_serial(key, True)
        for k in range(KT):
            act.wait_ge(nrm_ready, KT * na + k + 1)
            if "." in key:
                for w, c in halves(key):
                    last = nc.scalar.activation(a_hi[:, k, c], nrm[:, k, c], ACT.Identity, bias=shift(key, k, w))
            else:
                last = nc.scalar.activation(a_hi[:, k, 0:t], nrm[:, k, 0:t], ACT.Copy)
            last.then_inc(ahi_ready, 1)

    def pe_norm(pe, key):
        n, t = norm_serial(key), norms[key][1]
        pe.wait_ge(ssum_ready, n + 1)
        nc.tensor.matmul(ps[7][:, 0:t], con("ones"), sq[:, 0, 0:t], start=True, stop=True).then_inc(ms_ready, 1)

    def dve_norm(dve, key, step):
        n, t = norm_serial(key), norms[key][1]
        for k in range(1, KT):
            dve.wait_ge(sq_ready, KT * n + k + 1)
            ins = nc.vector.tensor_tensor(sq[:, 0, 0:t], sq[:, 0, 0:t], sq[:, k, 0:t], ALU.add)
            if k < KT - 1:
                step(ins)
        ins.then_inc(ssum_ready, 1)
        dve.wait_ge(rt_ready, n + 1)
        step(nc.vector.reciprocal(rs[:, 0:t], rt[:, 0:t]))
        if key.startswith("final"):
            for k in range(KT):
                ins = nc.vector.scalar_tensor_tensor(h[:, k, 0:t], h[:, k, 0:t], gain(key, k, 0), rs[:, 0:t],
                                                     ALU.mult, ALU.mult)
                if k < KT - 1:
                    step(ins)
            ins.then_inc(out_ready if key == "final2" else first_done, 1)
            return
        na = norm_serial(key, True)

        def lower(k):
            dve.wait_ge(ahi_ready, KT * na + k + 1)
            if "." in key:
                for w, c in halves(key):
                    last = nc.vector.scalar_tensor_tensor(a_lo[:, k, c], nrm[:, k, c], shift(key, k, w),
                                                          a_hi[:, k, c].bitcast(F32), ALU.add, ALU.subtract)
            else:
                last = nc.vector.tensor_tensor(a_lo[:, k, 0:t], nrm[:, k, 0:t], a_hi[:, k, 0:t].bitcast(F32),
                                               ALU.subtract)
            last.then_inc(a_ready, 1)

        for k in range(KT):
            for w, c in halves(key):
                last = nc.vector.scalar_tensor_tensor(nrm[:, k, c], h[:, k, c], gain(key, k, w), rs[:, c],
                                                      ALU.mult, ALU.mult)
            last.then_inc(nrm_ready, 1)
            if k:
                lower(k - 1)
        lower(KT - 1)

    ADA = LAYERS * N_MOD * KT // 2

    def ada_feed(pool, c0, c1):
        for c in range(c0, c1):
            if c >= 2:
                pool.wait_ge(ada_mult, c - 1)
            pool.dma_start(ada_ring[c % 2][:], dram["w_ada"][c]).then_inc(ada_landed[c % 2], 16)

    ada_done = [0]

    def pe_ada(pe, n):
        for c in range(ada_done[0], min(ada_done[0] + n, ADA)):
            pe.wait_ge(ada_landed[c % 2], 16 * (c // 2 + 1))
            for m in range(2):
                col = 2 * (2 * c + m)
                for k in range(KT):
                    o = k * 2 * P + m * P
                    last = nc.tensor.matmul(ps[6][:, col:col + 2], ada_ring[c % 2][:, o:o + P], silu_c[:, k, :],
                                            start=k == 0, stop=k == KT - 1)
            last.then_inc(ada_mult, 1)
            ada_done[0] = c + 1

    def dve_mods(dve, step):
        dve.wait_ge(ada_mult, ADA)
        nt = N_MOD * KT
        for l in range(LAYERS):
            bias = vcol("b_ada", nt * l, nt).unsqueeze(2).to_broadcast([P, nt, 2])
            step(nc.vector.tensor_tensor(mod[:, l], ps[6][:, 2 * nt * l:2 * nt * (l + 1)]
                                         .rearrange("p (j w) -> p j w", w=2), bias, ALU.add))
            for n in range(3):
                g = vcol("norm_g", (3 * l + n) * KT, KT).unsqueeze(2).to_broadcast([P, KT, 2])
                j = (3 * n + 1) * KT
                last = nc.vector.scalar_tensor_tensor(gmod[:, l, n], mod[:, l, j:j + KT, :], 1.0, g, ALU.add, ALU.mult)
            for i, j in enumerate((2, 8)):
                last = nc.vector.tensor_scalar(half_gate[:, l, i], mod[:, l, j * KT:(j + 1) * KT, :], 0.5, None,
                                               ALU.mult)
        step(last)

    def temp(name, shape, off, dt=F32):
        return place(name, shape, dt, off)

    K1 = 1024
    ar = temp("ar", [P, 4, 2, S], at_a)
    bt = temp("bt", [P, 4, S], at_a + 8 * K1)
    kt_ = temp("kt_", [P, 4, S], at_a + 12 * K1)
    a_tok = temp("a_tok", [P, 2, 512], at_a + 16 * K1)
    b_tok = temp("b_tok", [P, 2, 512], at_a + 20 * K1)
    k_tok = temp("k_tok", [P, 2, 512], at_a + 24 * K1)
    v_tok = temp("v_tok", [P, 2, 512], at_a + 28 * K1)
    t2b = temp("t2b", [P, 2, 2, S], at_a)
    xf = temp("xf", [P, 2, 16, 2 * NCMP], at_a + 4 * K1)
    x_hi = temp("x_hi", [P, 2, 16, 2 * NCMP], at_a + 8 * K1, F32R)
    x_lo = temp("x_lo", [P, 2, 16, 2 * NCMP], at_a + 12 * K1, F32R)
    hc = place("hc", [P, 4, 2 * NCMP], F32)
    kc = place("kc", [P, 2 * NCMP], F32)
    vct = place("vct", [P, 2, HD], F32)
    cos1 = place("cos1", [P, S], F32)
    sin1 = place("sin1", [P, S], F32)
    pos_i = place("pos_i", [P, S], I32)
    def slot4(name, i, shape=(P, 4, S)):
        return temp(name, list(shape), at_w + 4 * K1 * i)
    dsh = temp("dsh", [P, 15, S], at_w)
    sig = slot4("sig", 0)
    cum = slot4("cum", 1)
    ei = slot4("ei", 2)
    em = slot4("em", 3)
    aa = slot4("aa", 4)
    kk = slot4("kk", 5)
    kr = slot4("kr", 6)
    km = slot4("km", 7)
    rin = slot4("rin", 8)
    bb = slot4("bb", 9)
    tmp2 = slot4("tmp2", 10)
    el = slot4("el", 11)
    th = temp("th", [P, 4, S], at_w + 32 * K1)
    def slot2(name, i, shape=(P, 4, P)):
        return temp(name, list(shape), at_w + 2 * K1 * i)
    a16 = slot2("a16", 0)
    a16t = slot2("a16t", 1)
    aoff = slot2("aoff", 2)
    ak = slot2("ak", 3)
    pw2 = slot2("pw2", 4)
    pw2t = slot2("pw2t", 5)
    pw4 = slot2("pw4", 6)
    pw4t = slot2("pw4t", 7)
    pw8t = slot2("pw8t", 8)
    tinv = slot2("tinv", 9)
    w1t = slot2("w1t", 10, (P, 256))
    rb = temp("rb", [P, 8, P], at_w + 22 * K1)
    rk = temp("rk", [P, 8, P], at_w + 26 * K1)
    pp = temp("pp", [P, 4, P], at_w + 30 * K1)
    qq = temp("qq", [P, 512], at_w + 32 * K1)
    ut = temp("ut", [P, 512], at_w + 34 * K1)
    st = [temp(f"st{i}", [P, 4, P], at_w + (36 + 2 * i) * K1) for i in range(3)]
    ss = [temp(f"ss{i}", [P, 512], at_w + 2 * K1 * i) for i in range(2)]
    ee = [temp(f"ee{i}", [P, 512], at_w + (4 + 2 * i) * K1) for i in range(3)]
    pt = [temp(f"pt{i}", [P, 512], at_w + (10 + 2 * i) * K1) for i in range(2)]
    prep = temp("prep", [P, 5, T2], at_w)
    vt = temp("vt", [P, 3, 4, P], at_w + 14 * K1)
    ksw = temp("ksw", [P, 2, T2], at_w + 20 * K1)
    nb = temp("nb", [P, 4, 2, S], at_w + 24 * K1)
    pu = [temp(f"pu{i}", [P, 2, S + 32], at_w + 32 * K1 + 2304 * i) for i in range(5)]
    yp = temp("yp", [P, 2, S], at_w + 44 * K1)
    yp2 = temp("yp2", [P, 2, S], at_w + 46 * K1)
    nbt = temp("nbt", [P, 8, HD], at_w)
    gt = temp("gt", [P, 2, 24], at_w + 32 * K1)
    sgt = temp("sgt", [P, S], at_w + 33 * K1)
    cs = temp("cs", [P, 16, NCMP], at_w + 34 * K1)
    cst = temp("cst", [P, 8, 2, P], at_w + 36 * K1)
    cmx = temp("cmx", [P, 16], at_w + 46 * K1)
    csum = temp("csum", [P, 16], at_w + 46 * K1 + 64)
    cfac = temp("cfac", [P, 16], at_w + 46 * K1 + 128)
    NJ = 24
    mx = place("mx", [P, 2 * NJ, 2], F32)
    nm = place("nm", [P, 2 * NJ, 2], F32)
    sm = place("sm", [P, 2 * NJ, 2], F32)
    fac = place("fac", [P, 2 * NJ, 2], F32)

    def half_tiles(t, m):
        return ps[t + m // 2][:, (m % 2) * S:(m % 2) * S + S]

    def bc(ap, n):
        return ap.unsqueeze(1).to_broadcast([ap.shape[0], n, ap.shape[1]])

    pos_loaded = sem("pos_loaded")
    angle_ready = sem("angle_ready")
    sines_ready = sem("sines_ready")
    TWO_PI_HI, TWO_PI_MID = 6.28125, 2029.0 / 2 ** 20
    TWO_PI_LO = 2 * math.pi - TWO_PI_HI - TWO_PI_MID
    MAGIC = 1.5 * 2 ** 23

    def dve_tables(dve, step):
        dve.wait_ge(pos_loaded, 16)
        step(nc.vector.tensor_copy(cos1[:], pos_i[:]))
        step(nc.vector.tensor_scalar(cos1[:], cos1[:], con("freq"), None, ALU.mult))
        step(nc.vector.tensor_scalar(sin1[:], cos1[:], 1.0 / (2 * math.pi), MAGIC, ALU.mult, ALU.add))
        step(nc.vector.tensor_scalar(sin1[:], sin1[:], MAGIC, None, ALU.subtract))
        for part in (TWO_PI_HI, TWO_PI_MID, TWO_PI_LO):
            step(nc.vector.scalar_tensor_tensor(cos1[:], sin1[:], -part, cos1[:], ALU.mult, ALU.add))
        nc.vector.tensor_scalar(cos1[:], cos1[:], 3.1415925, -3.1415925, ALU.min, ALU.max).then_inc(angle_ready, 1)
        dve.wait_ge(sines_ready, 2)
        step(nc.vector.tensor_tensor(cos1[:], rt[:, 0:S], rt[:, 0:S], ALU.mult))
        step(nc.vector.tensor_scalar(cos1[:], cos1[:], -2.0, 1.0, ALU.mult, ALU.add))

    def act_tables(act):
        act.wait_ge(angle_ready, 1)
        nc.scalar.activation(sin1[:], cos1[:], ACT.Sin).then_inc(sines_ready, 1)
        nc.scalar.activation(rt[:, 0:S], cos1[:], ACT.Sin, scale=0.5).then_inc(sines_ready, 1)

    x_ready = sem("x_ready")
    xhi_ready = sem("xhi_ready")
    hc_ready = sem("hc_ready")
    kc_mult = sem("kc_mult")
    cmp_pr = product_at["w_cmp"][0]

    def dve_cmp(dve, step):
        for kv in range(2):
            for g in range(2):
                src = p1[g * HD:(g + 1) * HD, 18 + kv, :]
                nc.vector.tensor_copy(t2b[0:HD, kv, g, :], src)
                last = nc.vector.tensor_copy(t2b[HD:P, kv, g, 0:S - 1], src[:, 1:S])
        step(last)
        for kv in range(2):
            pe_cols = vcol("pe_v" if kv else "pe_k", 0, 16)
            for g in range(2):
                v = t2b[:, kv, g, :].rearrange("p (n s) -> p n s", s=16)
                for hf in range(2):
                    src = v[:, hf:hf + NCMP, 0:16:2].rearrange("p n j -> p j n")
                    b = pe_cols[:, 8 * hf:8 * hf + 8].unsqueeze(2).to_broadcast([P, 8, NCMP])
                    last = nc.vector.tensor_tensor(xf[:, kv, 8 * hf:8 * hf + 8, g * NCMP:(g + 1) * NCMP], src, b,
                                                   ALU.add)
        last.then_inc(x_ready, 1)
        dve.wait_ge(xhi_ready, 1)
        nc.vector.tensor_tensor(x_lo[:], xf[:], x_hi[:].bitcast(F32), ALU.subtract).then_inc(x_ready, 1)
        pr = cmp_pr
        for c in range(pr.base + 1, pr.end):
            split_lo(dve, c, c % RING, pr.size)
        dve.wait_ge(hc_ready, 1)
        nc.vector.memset(eps[:, 3:4], 0.0).then_inc(chunk_drained, pr.n)
        dve.wait_ge(kc_mult, 1)
        step(nc.vector.tensor_copy(kc[:], ps[7][:, 0:2 * NCMP]))
        nc.vector.tensor_copy(vct[0:NCMP], ps[5][0:NCMP, 0:P].rearrange("p (g d) -> p g d", g=2)).then_inc(x_ready, 1)

    def act_cmp(act):
        act.wait_ge(x_ready, 1)
        nc.scalar.activation(x_hi[:], xf[:], ACT.Copy).then_inc(xhi_ready, 1)
        pr = cmp_pr
        for c in range(pr.base + 1, pr.end):
            split_hi(act, c, c // RING, c % RING, pr.size)
        act.wait_ge(chunk_mult, pr.end)
        for kv in range(2):
            for m in range(2):
                last = nc.scalar.activation(hc[:, 2 * kv + m, :], ps[2 * kv + m][:, 0:2 * NCMP], ACT.Silu,
                                            bias=vcol("bv1" if kv else "bk1", m))
        last.then_inc(hc_ready, 1)

    def pe_cmp(pe):
        pr = cmp_pr
        pe.wait_ge(x_ready, 2)
        pe.wait_ge(chunk_drained, pr.base)
        for i in range(pr.n):
            kv, hf = i // 2, i % 2
            c = pr.base + i
            pe.wait_ge(lo_ready, c + 1)
            for m in range(2):
                for k in range(KT):
                    w1, w2 = by_cols(KT, 2 * P)(c % RING, m, k)
                    a1, a2 = x_hi[:, kv, 8 * hf + k, :], x_lo[:, kv, 8 * hf + k, :]
                    o = ps[2 * kv + m][:, 0:2 * NCMP]
                    nc.tensor.matmul(o, w1, a1, start=hf == 0 and k == 0, stop=False)
                    nc.tensor.matmul(o, w1, a2, start=False, stop=False)
                    last = nc.tensor.matmul(o, w2, a1, start=False, stop=hf == 1 and k == KT - 1)
            last.then_inc(chunk_mult, 1)
        pe.wait_ge(hc_ready, 1)
        for m in range(2):
            nc.tensor.matmul(ps[7][:, 0:2 * NCMP], mats[:, M_CK2 + m * P:M_CK2 + (m + 1) * P], hc[:, m, :],
                             start=m == 0, stop=m == 1)
        for g in range(2):
            for m in range(2):
                last = nc.tensor.matmul(ps[5][0:NCMP, g * HD:(g + 1) * HD], hc[:, 2 + m, g * NCMP:(g + 1) * NCMP],
                                        mats[:, M_CV2 + m * HD:M_CV2 + (m + 1) * HD], start=m == 0, stop=m == 1)
        last.then_inc(kc_mult, 1)

    rw_dve = sem("rw_dve")
    rw_act = sem("rw_act")
    rw_pe = sem("rw_pe")
    GR = range(4)
    RD = counts(["shift", "cum", "kr", "brk", "tokin"] + [f"tok{e}" for e in (1, 3, 5, 7)] + ["bonus"]
                + [n for t in range(2) for n in
                   [f"{n}.{2 * t + q}" for q in range(2) for n in
                    ("gram", "t0", "pw2t", "t1", "t2", "td", "n2t", "x1", "tinv", "qv")]
                   + [f"{n}.{2 * t + c}" for c in range(2) for n in ("u", "s")] + [f"y.{t}"]]
                + ["yc"])
    RA = counts(["lat", "sigw", "aa", "exps", "krsq", "kksqrt", "gcopy"] + [f"tok{e}" for e in (0, 2, 4, 6)]
                + [f"{n}.{g}" for g in GR for n in ("w1", "pw2", "pw4", "pw4t", "pw8t", "tdt", "n", "nt", "p")]
                + ["ysq", "ysd"])
    RP = counts(["zw", "za", "g", "kkss", "bonus"] + [f"tok{e}" for e in range(8)]
                + [n for t in range(2) for n in
                   [f"{n}.{2 * t + q}" for q in range(2) for n in
                    ("gram", "w1", "pw2", "pw2t", "pw4", "pw4t", "t1", "pw8t", "t2", "td", "tdt", "n", "nt", "n2t",
                     "x1", "tinv", "p", "qv")]
                   + [f"{n}.{2 * t + c}" for c in range(2) for n in ("u", "s")] + [f"y.{t}"]]
                + ["ymean", "yvar"])
    TOKB = (0, 1, 7)
    r_t, k_t, v_t = p1[:, 0:4, :], p1[:, 4:8, :], p1[:, 8:12, :]

    def flat(ap):
        return ap.rearrange("p a b -> p (a b)")

    def heads_of(par):
        return slice(par, 4, 2)

    def dve_rwkv(dve, step):
        V = nc.vector
        V.tensor_tensor(dsh[:, 0:14, 1:S], p1[:, 0:14, 0:S - 1], p1[:, 0:14, 1:S], ALU.subtract)
        V.tensor_scalar(dsh[:, 0:14, 0:1], p1[:, 0:14, 0:1], -1.0, None, ALU.mult)
        V.tensor_tensor(dsh[0:32, 14, 1:S], p1[0:32, 24, 0:S - 1], p1[0:32, 24, 1:S], ALU.subtract)
        step(V.tensor_scalar(dsh[0:32, 14, 0:1], p1[0:32, 24, 0:1], -1.0, None, ALU.mult))
        for m in (12, 13, 0, 1, 2, 3, 4, 5, 6, 7, 8, 9, 10, 11):
            V.scalar_tensor_tensor(p1[:, m, :], dsh[:, m, :], vcol("mu", m), p1[:, m, :], ALU.mult, ALU.add)
        V.scalar_tensor_tensor(p1[0:32, 24, :], dsh[0:32, 14, :], vcol("mu", 14, rows=slice(0, 32)), p1[0:32, 24, :],
                               ALU.mult, ALU.add).then_inc(rw_dve, 1)
        dve.wait_ge(rw_dve, RD["shift"])
        dve.wait_ge(rw_act, RA["sigw"])
        for m in range(4):
            last = V.tensor_tensor_scan(cum[:, m, :], con("scan0"), sig[:, m, :], 0.0, ALU.mult, ALU.add)
        step(last)
        V.tensor_tensor(em[:], cum[:], sig[:], ALU.subtract).then_inc(rw_dve, 1)
        for m in range(4):
            last = V.tensor_scalar(kr[:, m, :], k_t[:, m, :], vcol("k_k", m), None, ALU.mult)
        last.then_inc(rw_dve, 1)
        dve.wait_ge(rw_act, RA["aa"])
        for m in range(4):
            last = V.tensor_scalar(tmp2[:, m, :], aa[:, m, :], 1.0, vcol("k_a", m), ALU.subtract, ALU.mult)
        step(last)
        step(V.scalar_tensor_tensor(km[:], tmp2[:], 1.0, k_t, ALU.add, ALU.mult))
        dve.wait_ge(rw_act, RA["kksqrt"])
        step(V.tensor_scalar(rin[:], rin[:], 1e-12, None, ALU.max))
        step(V.reciprocal(rin[:], rin[:]))
        step(V.tensor_tensor(kk[:], kr[:], rin[:], ALU.mult))
        for m in range(4):
            last = V.scalar_tensor_tensor(kr[:, m, :], r_t[:, m, :], vcol("r_k", m), km[:, m, :], ALU.mult, ALU.mult)
        last.then_inc(rw_dve, 1)
        step(V.tensor_tensor(bb[:], kk[:], aa[:], ALU.mult))
        V.scalar_tensor_tensor(ar[:, :, 0, :], kk[:], -1.0, em[:], ALU.mult, ALU.mult)
        V.tensor_tensor(ar[:, :, 1, :], r_t, el[:], ALU.mult)
        V.tensor_tensor(bt[:], bb[:], ei[:], ALU.mult)
        step(V.tensor_tensor(kt_[:], km[:], ei[:], ALU.mult))
        for m in range(4):
            end = el[:, m, CHUNK - 1:S:CHUNK].unsqueeze(2).to_broadcast([P, S // CHUNK, CHUNK])
            V.tensor_tensor(kk[:, m, :].rearrange("p (c t) -> p c t", t=CHUNK),
                            bt[:, m, :].rearrange("p (c t) -> p c t", t=CHUNK), end, ALU.mult)
            last = V.tensor_tensor(aa[:, m, :].rearrange("p (c t) -> p c t", t=CHUNK),
                                   kt_[:, m, :].rearrange("p (c t) -> p c t", t=CHUNK), end, ALU.mult)
        last.then_inc(rw_dve, 1)
        toks = [(d, i) for d in (v_tok, a_tok, b_tok, k_tok) for i in range(2)]
        for e in (1, 3, 5, 7):
            dve.wait_ge(rw_pe, RP[f"tok{e}"])
            V.tensor_copy(toks[e][0][:, toks[e][1], :], ps[TOKB[e % 3]][:]).then_inc(rw_dve, 1)
        for m in range(2):
            last = V.tensor_tensor(v_t[:, 2 * m:2 * m + 2, :], ps[2 + m][:].rearrange("p (a b) -> p a b", a=2),
                                   v_t[:, 2 * m:2 * m + 2, :], ALU.mult)
        last.then_inc(rw_dve, 1)
        step(V.memset(st[0][:], 0.0))
        for i in range(2):
            for q in range(2):
                g = 2 * i + q
                dve.wait_ge(rw_pe, RP[f"gram.{g}"])
                if g:
                    dve.wait_ge(rw_pe, RP[f"qv.{g - 1}"])
                for par in range(2):
                    b = ps[par][:].rearrange("p (a b) -> p a b", a=2)
                    hs = heads_of(par)
                    gs = slice(4 * q + par, 4 * q + 4, 2)
                    V.tensor_tensor(a16[:, hs, :], b[:, :, 0:P], bc(con("m16"), 2), ALU.mult)
                    V.tensor_tensor(aoff[:, hs, :], b[:, :, 0:P], bc(con("moff"), 2), ALU.mult)
                    V.tensor_tensor(rb[:, gs, :], b[:, :, P:2 * P], bc(con("m_u"), 2), ALU.mult)
                    b = ps[2 + par][:].rearrange("p (a b) -> p a b", a=2)
                    V.tensor_tensor(ak[:, hs, :], b[:, :, 0:P], bc(con("m_su"), 2), ALU.mult)
                    V.tensor_tensor(rk[:, gs, :], b[:, :, P:2 * P], bc(con("m_u"), 2), ALU.mult)
                    b = ps[4 + par][:, 0:2 * P].rearrange("p (a b) -> p a b", a=2)
                    last = V.tensor_tensor(a16t[:, hs, :], b, bc(con("m16t"), 2), ALU.mult)
                last.then_inc(rw_dve, 1)
                dve.wait_ge(rw_dve, RD[f"gram.{g}"])
                V.tensor_tensor(tinv[:], a16[:], bc(con("ident"), 4), ALU.add).then_inc(rw_dve, 1)
                dve.wait_ge(rw_pe, RP[f"pw2t.{g}"])
                V.tensor_copy(flat(pw2t[:]), ps[0][:]).then_inc(rw_dve, 1)
                for n, bk in (("t1", 3), ("t2", 5), ("td", 7)):
                    dve.wait_ge(rw_pe, RP[f"{n}.{g}"])
                    dve.wait_ge(rw_dve, RD[f"{n}.{g}"] - 1)
                    V.tensor_tensor(flat(tinv[:]), ps[bk][:], flat(tinv[:]), ALU.add).then_inc(rw_dve, 1)
                dve.wait_ge(rw_pe, RP[f"n2t.{g}"])
                V.tensor_copy(flat(pw4[:]), ps[3][:]).then_inc(rw_dve, 1)
                for n, bk in (("x1", 4), ("tinv", 5)):
                    dve.wait_ge(rw_pe, RP[f"{n}.{g}"])
                    dve.wait_ge(rw_dve, RD[f"{n}.{g}"] - 1)
                    V.tensor_tensor(flat(tinv[:]), ps[bk][:], flat(tinv[:]), ALU.add).then_inc(rw_dve, 1)
                dve.wait_ge(rw_pe, RP[f"qv.{g}"])
                V.tensor_copy(qq[:, q * 256:(q + 1) * 256], ps[1][:, 0:256]).then_inc(rw_dve, 1)
            dve.wait_ge(rw_dve, RD[f"qv.{2 * i + 1}"])
            for c in range(2):
                s = 2 * i + c
                rows = slice(c * HD, (c + 1) * HD)
                dve.wait_ge(rw_pe, RP[f"u.{s}"])
                V.tensor_tensor(ut[rows, :], ps[2][rows, :], qq[rows, :], ALU.add).then_inc(rw_dve, 1)
                old, new = st[s % 3], st[(s + 1) % 3]
                end = el[:, :, s * CHUNK + CHUNK - 1:s * CHUNK + CHUNK].to_broadcast([P, 4, P])
                step(V.tensor_tensor(new[:], old[:], end, ALU.mult))
                dve.wait_ge(rw_pe, RP[f"s.{s}"])
                step(V.tensor_tensor(a16[:], ps[3][:].rearrange("p (a b) -> p a b", a=4), bc(con("bdmask"), 4),
                                     ALU.mult))
                V.tensor_tensor(new[:], new[:], a16[:], ALU.add).then_inc(rw_dve, 1)
                dve.wait_ge(rw_dve, RD[f"s.{s}"])
            dve.wait_ge(rw_pe, RP[f"y.{i}"])
            for m in range(2):
                last = V.tensor_copy(r_t[:, 2 * m:2 * m + 2, i * P:(i + 1) * P],
                                     ps[4 + m][:, 0:2 * P].rearrange("p (a b) -> p a b", a=2))
            last.then_inc(rw_dve, 1)
        dve.wait_ge(rw_pe, RP["ymean"])
        dve.wait_ge(rw_dve, RD["y.1"])
        for m in range(2):
            last = V.scalar_tensor_tensor(r_t[:, 2 * m:2 * m + 2, :], ps[m][:].rearrange("p (a b) -> p a b", a=2),
                                          -1.0 / HD, r_t[:, 2 * m:2 * m + 2, :], ALU.mult, ALU.add)
        last.then_inc(rw_dve, 1)
        dve.wait_ge(rw_act, RA["ysd"])
        step(V.reciprocal(cum[:], cum[:]))
        dve.wait_ge(rw_dve, RD["yc"])
        step(V.tensor_tensor(r_t, r_t, cum[:], ALU.mult))
        for m in range(4):
            last = V.tensor_scalar(r_t[:, m, :], r_t[:, m, :], vcol("lnx_w", m), vcol("lnx_b", m), ALU.mult, ALU.add)
        step(last)
        step(V.tensor_tensor(r_t, r_t, v_t, ALU.add))
        step(V.tensor_tensor(r_t, r_t, k_t, ALU.mult))

    def act_rwkv(act):
        A = nc.scalar.activation
        act.wait_ge(rw_dve, RD["shift"])
        A(th[0:HD, 0, :], p1[0:HD, 12, :], ACT.Tanh)
        A(th[:, 1, :], p1[:, 13, :], ACT.Sigmoid)
        A(th[0:32, 2, :], p1[0:32, 24, :], ACT.Sigmoid).then_inc(rw_act, 1)
        act.wait_ge(rw_pe, RP["zw"])
        for m in range(4):
            last = A(sig[:, m, :], half_tiles(0, m), ACT.Sigmoid, bias=vcol("w0", m))
        last.then_inc(rw_act, 1)
        act.wait_ge(rw_pe, RP["za"])
        for m in range(4):
            last = A(aa[:, m, :], half_tiles(2, m), ACT.Sigmoid, bias=vcol("a0", m))
        last.then_inc(rw_act, 1)
        act.wait_ge(rw_dve, RD["cum"])
        A(el[:], cum[:], ACT.Exp, scale=-DECAY)
        A(ei[:], cum[:], ACT.Exp, scale=DECAY)
        A(em[:], em[:], ACT.Exp, scale=-DECAY).then_inc(rw_act, 1)
        act.wait_ge(rw_pe, RP["g"])
        act.wait_ge(rw_dve, RD["kr"])
        A(rin[:], kr[:], ACT.Square).then_inc(rw_act, 1)
        act.wait_ge(rw_pe, RP["kkss"])
        for m in range(2):
            last = A(flat(rin[:, 2 * m:2 * m + 2, :]), ps[m][:], ACT.Sqrt)
        last.then_inc(rw_act, 1)
        act.wait_ge(rw_dve, RD["tokin"])
        for m in range(2):
            last = A(flat(k_t[:, 2 * m:2 * m + 2, :]), ps[4 + m][:], ACT.Copy)
        last.then_inc(rw_act, 1)
        toks = [(d, i) for d in (v_tok, a_tok, b_tok, k_tok) for i in range(2)]
        for e in (0, 2, 4, 6):
            act.wait_ge(rw_pe, RP[f"tok{e}"])
            A(toks[e][0][:, toks[e][1], :], ps[TOKB[e % 3]][:], ACT.Copy).then_inc(rw_act, 1)
        for g in GR:
            for n, dst, bk in (("w1", w1t, 3), ("pw2", pw2, 7), ("pw4", pw4, 1), ("pw4t", pw4t, 2), ("pw8t", pw8t, 4),
                               ("tdt", a16t, 0), ("n", pw2, 1), ("nt", pw2t, 2), ("p", pp, 0)):
                act.wait_ge(rw_pe, RP[f"{n}.{g}"])
                if n == "w1":
                    A(w1t[:], ps[bk][:, 0:256], ACT.Copy).then_inc(rw_act, 1)
                elif n == "p":
                    q = g % 2
                    A(flat(pp[:, 2 * q:2 * q + 2, :]), ps[0][:, 0:256], ACT.Copy).then_inc(rw_act, 1)
                else:
                    A(flat(dst[:]), ps[bk][:], ACT.Copy).then_inc(rw_act, 1)
        act.wait_ge(rw_dve, RD["yc"])
        A(sig[:], r_t, ACT.Square).then_inc(rw_act, 1)
        act.wait_ge(rw_pe, RP["yvar"])
        for m in range(2):
            last = A(flat(cum[:, 2 * m:2 * m + 2, :]), ps[2 + m][:], ACT.Sqrt, scale=1.0 / HD, bias=eps[:, 1:2])
        last.then_inc(rw_act, 1)

    def pe_rwkv(pe):
        M = nc.tensor.matmul
        T = nc.tensor.transpose
        ident = con("ident")
        pe.wait_ge(rw_dve, RD["shift"])
        pe.wait_ge(rw_act, RA["lat"])
        for m in range(4):
            w = mats[0:HD, M_LORA + m * P:M_LORA + (m + 1) * P]
            last = M(half_tiles(0, m), w, th[0:HD, 0, :], start=True, stop=True)
        last.then_inc(rw_pe, 1)
        for m in range(4):
            w = mats[HD:P, M_LORA + m * P:M_LORA + (m + 1) * P]
            last = M(half_tiles(2, m), w, p1[HD:P, 12, :], start=True, stop=True)
        last.then_inc(rw_pe, 1)
        for m in range(4):
            M(half_tiles(4, m), mats[:, M_G2 + m * P:M_G2 + (m + 1) * P], th[:, 1, :], start=True, stop=False)
            last = M(half_tiles(4, m), mats[0:32, M_G2T + m * P:M_G2T + (m + 1) * P], th[0:32, 2, :],
                     start=False, stop=True)
        last.then_inc(rw_pe, 1)
        pe_ada(pe, 8)
        pe.wait_ge(rw_act, RA["krsq"])
        for m in range(2):
            last = M(ps[m][:], con("bd"), flat(rin[:, 2 * m:2 * m + 2, :]), start=True, stop=True)
        last.then_inc(rw_pe, 1)
        pe_ada(pe, 4)
        pe.wait_ge(rw_dve, RD["brk"])
        for m in range(2):
            last = M(ps[2 + m][:], con("bd"), flat(kr[:, 2 * m:2 * m + 2, :]), start=True, stop=True)
        last.then_inc(rw_pe, 1)
        pe_ada(pe, 4)
        pe.wait_ge(rw_dve, RD["tokin"])
        pe.wait_ge(rw_act, RA["kksqrt"])
        e = 0
        for src in (v_t, ar[:, :, 0, :], kk[:], aa[:]):
            for i in range(2):
                if e >= 3:
                    pe.wait_ge(rw_dve if (e - 3) % 2 else rw_act, (RD if (e - 3) % 2 else RA)[f"tok{e - 3}"])
                for m in range(4):
                    last = T(ps[TOKB[e % 3]][:, m * P:(m + 1) * P], src[:, m, i * P:(i + 1) * P], ident)
                last.then_inc(rw_pe, 1)
                e += 1
        pe.wait_ge(rw_dve, RD["bonus"])
        pe.wait_ge(rw_act, RA["tok6"])
        for i in range(2):
            tok = slice(i * P, (i + 1) * P)
            for q in range(2):
                g = 2 * i + q
                if q == 0 and i:
                    pe.wait_ge(rw_dve, RD["y.0"])
                if g:
                    pe.wait_ge(rw_dve, RD[f"qv.{g - 1}"])
                    pe.wait_ge(rw_act, RA[f"p.{g - 1}"])
                for j in range(4):
                    par, ix = j % 2, j // 2
                    rows = slice(par * HD, (par + 1) * HD)
                    m = 2 * q + ix
                    b = ps[par][:, ix * 256:ix * 256 + 256].rearrange("p (a b) -> p a b", a=2)
                    M(b, bt[rows, m, tok], ar[rows, m, :, tok], start=True, stop=True)
                    b = ps[2 + par][:, ix * 256:ix * 256 + 256].rearrange("p (a b) -> p a b", a=2)
                    M(b, kt_[rows, m, tok], ar[rows, m, :, tok], start=True, stop=True)
                    last = M(ps[4 + par][:, ix * P:(ix + 1) * P], ar[rows, m, 0, tok], bt[rows, m, tok],
                             start=True, stop=True)
                last.then_inc(rw_pe, 1)
                pe_ada(pe, 3)

                def four(bk, lhs, rhs, n=P):
                    for j in range(4):
                        last = M(ps[bk][:, j * n:(j + 1) * n], lhs[:, j, :], rhs(j), start=True, stop=True)
                    last.then_inc(rw_pe, 1)

                pe.wait_ge(rw_dve, RD[f"t0.{g}"])
                four(3, ak, lambda j: v_tok[:, i, (4 * q + j) * HD:(4 * q + j + 1) * HD], HD)
                four(7, a16t, lambda j: a16[:, j, :])
                four(0, a16, lambda j: a16t[:, j, :])
                pe.wait_ge(rw_dve, RD[f"pw2t.{g}"])
                pe.wait_ge(rw_act, RA[f"pw2.{g}"])
                four(1, pw2t, lambda j: pw2[:, j, :])
                four(2, pw2, lambda j: pw2t[:, j, :])
                pe.wait_ge(rw_act, RA[f"w1.{g}"])
                four(3, pw2t, lambda j: tinv[:, j, :])
                pe_ada(pe, 2)
                pe.wait_ge(rw_act, RA[f"pw4t.{g}"])
                four(4, pw4, lambda j: pw4t[:, j, :])
                pe.wait_ge(rw_dve, RD[f"t1.{g}"])
                four(5, pw4t, lambda j: tinv[:, j, :])
                pe.wait_ge(rw_act, RA[f"pw8t.{g}"])
                pe.wait_ge(rw_dve, RD[f"t2.{g}"])
                four(7, pw8t, lambda j: tinv[:, j, :])
                pe_ada(pe, 1)
                pe.wait_ge(rw_dve, RD[f"td.{g}"])
                for j in range(4):
                    last = T(ps[0][:, j * P:(j + 1) * P], tinv[:, j, :], ident)
                last.then_inc(rw_pe, 1)
                pe.wait_ge(rw_act, RA[f"tdt.{g}"])
                four(1, a16t, lambda j: aoff[:, j, :])
                four(2, aoff, lambda j: a16t[:, j, :])
                pe.wait_ge(rw_act, RA[f"nt.{g}"])
                four(3, pw2, lambda j: pw2t[:, j, :])
                pe.wait_ge(rw_dve, RD[f"n2t.{g}"])
                four(4, pw4, lambda j: tinv[:, j, :])
                pe.wait_ge(rw_dve, RD[f"x1.{g}"])
                four(5, pw2t, lambda j: tinv[:, j, :])
                pe_ada(pe, 2)
                pe.wait_ge(rw_dve, RD[f"tinv.{g}"])
                for j in range(4):
                    par, ix = j % 2, j // 2
                    last = M(ps[0][par * HD:(par + 1) * HD, ix * P:(ix + 1) * P],
                             a_tok[:, i, (4 * q + j) * HD:(4 * q + j + 1) * HD], tinv[:, j, :], start=True, stop=True)
                last.then_inc(rw_pe, 1)
                for j in range(4):
                    last = M(ps[1][:, j * HD:(j + 1) * HD], tinv[:, j, :], w1t[:, j * HD:(j + 1) * HD],
                             start=True, stop=True)
                last.then_inc(rw_pe, 1)
            pe.wait_ge(rw_act, RA[f"p.{2 * i + 1}"])
            for c in range(2):
                s = 2 * i + c
                rows = slice(c * HD, (c + 1) * HD)
                pe.wait_ge(rw_dve, RD[f"u.{s}"] - 1)
                for m in range(4):
                    last = M(ps[2][rows, m * P:(m + 1) * P], pp[:, m, c * HD:(c + 1) * HD], st[s % 3][:, m, :],
                             start=True, stop=True)
                last.then_inc(rw_pe, 1)
                pe.wait_ge(rw_dve, RD[f"u.{s}"])
                for m in range(4):
                    cols = slice(m * P, (m + 1) * P)
                    M(ps[3][:, cols], b_tok[rows, i, cols], ut[rows, cols], start=True, stop=False)
                    last = M(ps[3][:, cols], k_tok[rows, i, cols], v_tok[rows, i, cols], start=False, stop=True)
                last.then_inc(rw_pe, 1)
                pe_ada(pe, 1)
            for m in range(4):
                o = ps[4 + m // 2]
                for par in range(2):
                    hh = 2 * m + par
                    dst = o[par * HD:(par + 1) * HD, (m % 2) * P:(m % 2) * P + P]
                    hc_ = slice(hh * HD, (hh + 1) * HD)
                    M(dst, v_tok[:, i, hc_], rk[:, hh, :], start=True, stop=False, skip_group_check=True)
                    M(dst, ut[:, hc_], rb[:, hh, :], start=False, stop=False, skip_group_check=True)
                for c in range(2):
                    col = (m % 2) * P + c * HD
                    t0 = i * P + c * CHUNK
                    last = M(o[:, col:col + HD], st[(2 * i + c) % 3][:, m, :], ar[:, m, 1, t0:t0 + CHUNK],
                             start=False, stop=True, skip_group_check=True)
            last.then_inc(rw_pe, 1)
        pe.wait_ge(rw_dve, RD["y.1"])
        for m in range(2):
            last = M(ps[m][:], con("bd"), flat(r_t[:, 2 * m:2 * m + 2, :]), start=True, stop=True)
        last.then_inc(rw_pe, 1)
        pe_ada(pe, 4)
        pe.wait_ge(rw_act, RA["ysq"])
        for m in range(2):
            last = M(ps[2 + m][:], con("bd"), flat(sig[:, 2 * m:2 * m + 2, :]), start=True, stop=True)
        last.then_inc(rw_pe, 1)
        pe_ada(pe, ADA)

    at_scores = sem("at_scores")
    at_max = sem("at_max")
    at_exp = sem("at_exp")
    at_norm = sem("at_norm")
    at_trans = sem("at_trans")
    at_pt = sem("at_pt")
    at_pv = sem("at_pv")
    at_ohi = sem("at_ohi")
    at_olo = sem("at_olo")
    pr_dve = sem("pr_dve")
    pr_act = sem("pr_act")
    pr_pe = sem("pr_pe")
    pool_step = sem("pool_step")
    pool_ready = sem("pool_ready")
    nb_loaded = sem("nb_loaded")

    class Job:
        pass

    def jobs_first():
        out_ = []
        for hh in range(8):
            for i in range(2):
                j = Job()
                par, g, n = hh % 2, hh // 4, P * (i + 1)
                rows = slice(par * HD, (par + 1) * HD)
                j.q = p1[rows, 14 + hh // 2, i * P:(i + 1) * P]
                j.keys = [((p1[rows, 20 + 2 * b, 0:n] if par == g else ksw[rows, b, 0:n]), b * S, n) for b in range(2)]
                j.segs, j.seg, j.width = 2, S, n
                j.masks = [(con("causal", P if i == 0 else 0), n)]
                j.scaled = True
                j.gates = gt[:, i, 3 * hh + 1:3 * hh + 3]
                j.values = [(vt[:, b, k, g * HD:(g + 1) * HD], b * S + k * P) for b in range(2) for k in range(i + 1)]
                j.cmp = (vct[0:NCMP, g, :], cst[0:NCMP, hh, i, :])
                j.rows, j.col, j.tile, j.tok = rows, i * P, 4 + hh // 2, 0
                out_.append(j)
        return out_

    def jobs_second(l):
        out_ = []
        for w in range(2 if l == 0 else 1):
            for hh in range(12):
                for i in range(2):
                    j = Job()
                    na = hh < 4
                    hq = hh if na else hh - 4
                    par = hq % 2
                    rows = slice(par * HD, (par + 1) * HD)
                    k0, n = (0, T2) if w == 0 else (S, S)
                    g = hq // 4
                    j.q = p2[rows, (0 if na else 8) + hq // 2, w * S + i * P:w * S + (i + 1) * P]
                    if na:
                        key = p2[rows, 2 + hq // 2, k0:k0 + n]
                    else:
                        key = p2[rows, 12, k0:k0 + n] if par == g else ksw[rows, 0, k0:k0 + n]
                    j.keys = [(key, 0, n)]
                    j.segs, j.seg, j.width = 1, n, n
                    j.scaled = na and w == 0
                    j.masks = [(nb[:, hq, i, :], S)] if j.scaled else []
                    j.gates = None
                    v, d = (hq // 2, par) if na else (2, g)
                    j.values = [(vt[:, v, (k0 // P) + k, d * HD:(d + 1) * HD], k * P) for k in range(n // P)]
                    j.cmp = None
                    j.rows, j.col, j.tok = rows, i * P, w * S
                    j.tile = hq // 2 if na else 4 + hq // 2
                    out_.append(j)
        return out_

    SB, TB, OB = (0, 1, 2), (3, 4), (5, 7)
    stages = [("first", jobs_first(), 0)]
    for l in range(LAYERS):
        stages.append((l, jobs_second(l), stages[-1][2] + len(stages[-1][1])))
    stage_of = {s[0]: s for s in stages}

    def pe_attend(pe, key):
        _, jobs, j0 = stage_of[key]

        def scores(j, x):
            wait(pe, at_exp, j - 2)
            for kx, off, n in x.keys:
                last = nc.tensor.matmul(ps[SB[j % 3]][:, off:off + n], x.q, kx, start=True, stop=True)
            last.then_inc(at_scores, 1)

        def turn(j, x):
            pe.wait_ge(at_norm, j + 1)
            wait(pe, at_pt, j - 1)
            for _, off in x.values:
                last = nc.tensor.transpose(ps[TB[j % 2]][:, off:off + P], ee[j % 3][:, off:off + P], con("ident"))
            last.then_inc(at_trans, 1)

        def pv(j, x):
            pair = j // 4
            pe.wait_ge(at_pt, j + 1)
            if j % 4 == 0:
                wait(pe, at_olo, pair - 1)
            o = ps[OB[pair % 2]][x.rows, x.col:x.col + P]
            for n, (v, off) in enumerate(x.values):
                last = nc.tensor.matmul(o, v, pt[j % 2][:, off:off + P], start=n == 0,
                                        stop=x.cmp is None and n == len(x.values) - 1)
            if x.cmp is not None:
                last = nc.tensor.matmul(o, x.cmp[0], x.cmp[1], start=False, stop=True)
            last.then_inc(at_pv, 1)

        n = len(jobs)
        for t in range(n + 3):
            if t < n:
                scores(j0 + t, jobs[t])
            if 2 <= t < n + 2:
                turn(j0 + t - 2, jobs[t - 2])
            if t >= 3:
                pv(j0 + t - 3, jobs[t - 3])

    def act_attend(act, key):
        _, jobs, j0 = stage_of[key]
        n = len(jobs)
        for t in range(n + 7):
            if t < n:
                j, x = j0 + t, jobs[t]
                act.wait_ge(at_max, j + 1)
                wait(act, at_trans, j - 2)
                for s in range(x.segs):
                    c = slice(s * S, s * S + x.width)
                    src = (ss[j % 2] if x.scaled else ps[SB[j % 3]])[:, c]
                    last = nc.scalar.activation(ee[j % 3][:, c], src, ACT.Exp, bias=nm[:, t, s:s + 1],
                                                scale=1.0 if x.scaled else SCALE, accum_out=sm[:, t, s:s + 1])
                last.then_inc(at_exp, 1)
            if 2 <= t < n + 2:
                j, x = j0 + t - 2, jobs[t - 2]
                act.wait_ge(at_trans, j + 1)
                wait(act, at_pv, j - 1)
                src, dst = ps[TB[j % 2]], pt[j % 2]
                for s in range(x.segs):
                    c = slice(s * S, s * S + x.width)
                    last = nc.scalar.activation(dst[:, c], src[:, c], ACT.Copy)
                last.then_inc(at_pt, 1)
            if 6 <= t < n + 6 and (t - 6) % 4 == 0:
                pair, x = (j0 + t - 6) // 4, jobs[t - 6]
                act.wait_ge(at_pv, j0 + t - 2)
                nc.scalar.activation(a_hi[:, x.tile, x.tok:x.tok + S], ps[OB[pair % 2]][:, 0:S],
                                     ACT.Copy).then_inc(at_ohi, 1)

    def dve_attend(dve, key, step):
        _, jobs, j0 = stage_of[key]
        n = len(jobs)
        for t in range(n + 7):
            if t < n:
                j, x = j0 + t, jobs[t]
                dve.wait_ge(at_scores, j + 1)
                b = ps[SB[j % 3]]
                if x.scaled:
                    wait(dve, at_exp, j - 1)
                    src = ss[j % 2]
                    mask, w = x.masks[0]
                    if x.segs == 2:
                        dst = src[:].rearrange("p (b c) -> p b c", b=2)[:, :, 0:w]
                        step(nc.vector.scalar_tensor_tensor(
                            dst, b[:].rearrange("p (b c) -> p b c", b=2)[:, :, 0:w], SCALE,
                            bc(mask[:, 0:w], 2), ALU.mult, ALU.add))
                    else:
                        flip = mask.rearrange("p (r c) -> p r c", c=64)
                        nc.vector.scalar_tensor_tensor(src[:, 0:w].rearrange("p (r c) -> p r c", c=64),
                                                       b[:, 0:w].rearrange("p (r c) -> p r c", c=64), SCALE,
                                                       flip, ALU.mult, ALU.add)
                        step(nc.vector.tensor_scalar(src[:, w:T2], b[:, w:T2], SCALE, None, ALU.mult))
                else:
                    src = b
                view = src[:].rearrange("p (b c) -> p b c", b=2)[:, :, 0:x.width] if x.segs == 2 else src[:, 0:x.width]
                step(nc.vector.tensor_reduce(mx[:, t, 0:x.segs], view, AX_X, ALU.max))
                nc.vector.tensor_scalar(nm[:, t, 0:x.segs], mx[:, t, 0:x.segs], -1.0 if x.scaled else -SCALE, None,
                                        ALU.mult).then_inc(at_max, 1)
            if 1 <= t < n + 1:
                j, x = j0 + t - 1, jobs[t - 1]
                u = t - 1
                dve.wait_ge(at_exp, j + 1)
                step(nc.vector.reciprocal(fac[:, u, 0:x.segs], sm[:, u, 0:x.segs]))
                if x.gates is not None:
                    step(nc.vector.tensor_tensor(fac[:, u, :], fac[:, u, :], x.gates, ALU.mult))
                for s in range(x.segs):
                    c = slice(s * S, s * S + x.width)
                    last = nc.vector.tensor_scalar(ee[j % 3][:, c], ee[j % 3][:, c], fac[:, u, s:s + 1], None,
                                                   ALU.mult)
                last.then_inc(at_norm, 1)
            if 6 <= t < n + 6 and (t - 6) % 4 == 0:
                pair, x = (j0 + t - 6) // 4, jobs[t - 6]
                dve.wait_ge(at_ohi, pair + 1)
                c = slice(x.tok, x.tok + S)
                nc.vector.tensor_tensor(a_lo[:, x.tile, c], ps[OB[pair % 2]][:, 0:S],
                                        a_hi[:, x.tile, c].bitcast(F32), ALU.subtract).then_inc(at_olo, 1)

    PD = counts(["rot", "ksw", "vt", "cmax", "cnorm", "cst0", "cst1", "cst2", "cst3"])
    PA = counts(["gate", "gt", "cexp", "rhi"])
    PP = counts(["rot", "krot", "vt", "gt", "cs", "ct0", "ct1", "ct2", "ct3"])
    ROT = (14, 16, 20, 22)

    def pe_first(pe):
        for e, t in enumerate(ROT):
            last = nc.tensor.matmul(ps[e][:], con("rot1"), flat(p1[:, t:t + 2, :]), start=True, stop=True)
        last.then_inc(pr_pe, 1)
        nc.tensor.matmul(ps[4][:, 0:2 * NCMP], con("rot1"), kc[:], start=True, stop=True).then_inc(pr_pe, 1)
        pe.wait_ge(pr_dve, PD["ksw"])
        for b in range(2):
            for i in range(2):
                o = (2 * b + i) * P
                last = nc.tensor.transpose(ps[5][:, o:o + P], p1[:, 21 + 2 * b, i * P:(i + 1) * P], con("ident"))
        last.then_inc(pr_pe, 1)
        pe.wait_ge(pr_act, PA["gate"])
        for i in range(2):
            last = nc.tensor.transpose(ps[0][:, i * 24:(i + 1) * 24], sgt[0:24, i * P:(i + 1) * P],
                                       consts[0:24, CAT["ident"][0]:CAT["ident"][0] + 24])
        last.then_inc(pr_pe, 1)
        for hh in range(8):
            par, g = hh % 2, hh // 4
            rows = slice(par * HD, (par + 1) * HD)
            for i in range(2):
                o = ((hh // 2) * 2 + i) * NCMP
                last = nc.tensor.matmul(ps[1 + par][:, o:o + NCMP], p1[rows, 14 + hh // 2, i * P:(i + 1) * P],
                                        kc[rows, g * NCMP:(g + 1) * NCMP], start=True, stop=True)
        last.then_inc(pr_pe, 1)
        pe.wait_ge(pr_dve, PD["cnorm"])
        for e in range(4):
            if e >= 2:
                pe.wait_ge(pr_dve, PD[f"cst{e - 2}"])
            for q in range(4):
                n = 4 * e + q
                hh, i = n // 2, n % 2
                last = nc.tensor.transpose(ps[3 + e % 2][0:NCMP, q * P:(q + 1) * P],
                                           cs[:, ((hh % 2) * 4 + hh // 2) * 2 + i, :], con("ident"))
            last.then_inc(pr_pe, 1)

    def act_first(act):
        nc.scalar.activation(sgt[0:24, :], p1[32:56, 24, :], ACT.Sigmoid).then_inc(pr_act, 1)
        act.wait_ge(pr_pe, PP["gt"])
        nc.scalar.activation(gt[:], ps[0][:, 0:48].rearrange("p (i c) -> p i c", i=2), ACT.Copy).then_inc(pr_act, 1)
        act.wait_ge(pr_dve, PD["cmax"])
        nc.scalar.activation(cs[:], cs[:], ACT.Exp).then_inc(pr_act, 1)
        nc.scalar.activation(a_hi[:, 0:4, 0:S], r_t, ACT.Copy).then_inc(pr_act, 1)

    def dve_first(dve, step):
        V = nc.vector
        dve.wait_ge(pr_pe, PP["rot"])
        t1 = prep[:, 0, :].rearrange("p (a b) -> p a b", a=2)
        t2 = prep[:, 1, :].rearrange("p (a b) -> p a b", a=2)
        for e, t in enumerate(ROT):
            V.tensor_tensor(t1, p1[:, t:t + 2, :], bc(cos1[:], 2), ALU.mult)
            step(V.tensor_tensor(t2, ps[e][:].rearrange("p (a b) -> p a b", a=2), bc(sin1[:], 2), ALU.mult))
            last = V.tensor_tensor(p1[:, t:t + 2, :], t1, t2, ALU.add)
            if e < 3:
                step(last)
        last.then_inc(pr_dve, 1)
        dve.wait_ge(pr_pe, PP["krot"])
        k3 = kc[:].rearrange("p (g n) -> p g n", g=2)
        u1 = prep[:, 2, 0:2 * NCMP].rearrange("p (g n) -> p g n", g=2)
        u2 = prep[:, 3, 0:2 * NCMP].rearrange("p (g n) -> p g n", g=2)
        V.tensor_tensor(u1, k3, bc(cos1[:, 31:S:16], 2), ALU.mult)
        step(V.tensor_tensor(u2, ps[4][:, 0:2 * NCMP].rearrange("p (g n) -> p g n", g=2),
                             bc(sin1[:, 31:S:16], 2), ALU.mult))
        V.tensor_tensor(k3, u1, u2, ALU.add)
        dve.wait_ge(pr_dve, PD["rot"])
        for b in range(2):
            V.tensor_copy(ksw[0:HD, b, 0:S], p1[HD:P, 20 + 2 * b, :])
            last = V.tensor_copy(ksw[HD:P, b, 0:S], p1[0:HD, 20 + 2 * b, :])
        last.then_inc(pr_dve, 1)
        dve.wait_ge(pr_pe, PP["vt"])
        V.tensor_copy(vt[:, 0:2, 0:2, :], ps[5][:].rearrange("p (b i f) -> p b i f", b=2, i=2)).then_inc(pr_dve, 1)
        dve.wait_ge(pr_pe, PP["cs"])
        c4 = cs[:].rearrange("p (a h i) n -> p a h i n", a=2, i=2)
        for par in range(2):
            for i in range(2):
                m = bc(con("cmp_add", i * NCMP, (i + 1) * NCMP), 4)
                last = V.scalar_tensor_tensor(
                    c4[:, par, :, i, :], ps[1 + par][:, 0:120].rearrange("p (h i n) -> p h i n", i=2, n=NCMP)[:, :, i, :],
                    SCALE, m, ALU.mult, ALU.add)
        step(last)
        step(V.tensor_reduce(cmx[:], cs[:], AX_X, ALU.max))
        V.tensor_tensor(cs[:], cs[:], cmx[:].unsqueeze(2).to_broadcast([P, 16, NCMP]), ALU.subtract).then_inc(pr_dve, 1)
        dve.wait_ge(pr_act, PA["cexp"])
        step(V.tensor_reduce(csum[:], cs[:], AX_X, ALU.add))
        step(V.reciprocal(csum[:], csum[:]))
        for par in range(2):
            for i in range(2):
                g3 = gt[:, i, 3 * par:24:6]
                last = V.tensor_tensor(cfac[:].rearrange("p (a h i) -> p a h i", a=2, i=2)[:, par, :, i],
                                       csum[:].rearrange("p (a h i) -> p a h i", a=2, i=2)[:, par, :, i], g3, ALU.mult)
        step(last)
        for i in range(2):
            v = cs[:].rearrange("p (a i) n -> p a i n", i=2)[:, :, i, :]
            last = V.tensor_tensor(v, v, bc(con("cmp_ok", i * NCMP, (i + 1) * NCMP), 8), ALU.mult)
        step(last)
        V.tensor_tensor(cs[:], cs[:], cfac[:].unsqueeze(2).to_broadcast([P, 16, NCMP]), ALU.mult).then_inc(pr_dve, 1)
        for e in range(4):
            dve.wait_ge(pr_pe, PP[f"ct{e}"])
            V.tensor_copy(cst[0:NCMP, 2 * e:2 * e + 2, :, :],
                          ps[3 + e % 2][0:NCMP, :].rearrange("p (h i q) -> p h i q", h=2, i=2)).then_inc(pr_dve, 1)
        dve.wait_ge(pr_act, PA["rhi"])
        step(V.tensor_tensor(a_lo[:, 0:4, 0:S], r_t, a_hi[:, 0:4, 0:S].bitcast(F32), ALU.subtract))

    n1 = len(PP)
    QD = counts(["nrm", "rot", "vt0", "vt2"])
    QA = counts(["sq", "sqrt", "vt1", "pool"])
    QP = counts(["ss", "rot", "vt0", "vt1", "vt2", "pool"])
    base_d, base_a, base_p = len(PD), len(PA), len(PP)

    def qd(l, n):
        return base_d + l * len(QD) + QD[n]

    def qa(l, n):
        return base_a + l * len(QA) + QA[n]

    def qp(l, n):
        return base_p + l * len(QP) + QP[n]

    def width(l, t):
        return T2 if l == 0 or t == 4 else S

    def pe_second(pe, l):
        pe.wait_ge(pr_act, qa(l, "sq"))
        for t in range(5):
            w = width(l, t)
            last = nc.tensor.matmul(ps[t][:, 0:w], con("bd"), prep[:, t, 0:w], start=True, stop=True)
        last.then_inc(pr_pe, 1)
        pe.wait_ge(pr_dve, qd(l, "nrm"))
        for t in range(5):
            last = nc.tensor.matmul(ps[t][:, 0:S], con("rot2"), p2[:, 8 + t, 0:S], start=True, stop=True)
        last.then_inc(pr_pe, 1)
        for v, (tile, b) in enumerate(((4, 5), (5, 6), (13, 7))):
            for k in range(4):
                last = nc.tensor.transpose(ps[b][:, k * P:(k + 1) * P], p2[:, tile, k * P:(k + 1) * P], con("ident"))
            last.then_inc(pr_pe, 1)
        nw = 2 if l == 0 else 1
        pe.wait_ge(pr_dve, qd(l, "rot"))
        for w in range(nw):
            pe.wait_ge(pool_ready, 1 + w if l == 0 else 3)
            for t in range(2):
                o = M_POOL + (2 * l + t) * P
                last = nc.tensor.matmul(ps[2 * w + t][:, 0:S], mats[:, o:o + P], yp[:, t, :] if w == 0 else yp2[:, t, :],
                                        start=True, stop=True)
        last.then_inc(pr_pe, 1)

    def act_second(act, l):
        for t in range(5):
            w = width(l, t)
            last = nc.scalar.activation(prep[:, t, 0:w], p2[:, 8 + t, 0:w], ACT.Square)
        last.then_inc(pr_act, 1)
        act.wait_ge(pr_pe, qp(l, "ss"))
        for t in range(5):
            w = width(l, t)
            last = nc.scalar.activation(prep[:, t, 0:w], ps[t][:, 0:w], ACT.Sqrt, scale=1.0 / HD, bias=eps[:, 0:1])
        last.then_inc(pr_act, 1)
        act.wait_ge(pr_pe, qp(l, "vt1"))
        nc.scalar.activation(vt[:, 1], ps[6][:].rearrange("p (a b) -> p a b", a=4), ACT.Copy).then_inc(pr_act, 1)
        act.wait_ge(pr_pe, qp(l, "pool"))
        for w in range(2 if l == 0 else 1):
            for t in range(2):
                last = nc.scalar.activation(a_hi[:, 2 + t, w * S:(w + 1) * S], ps[2 * w + t][:, 0:S], ACT.Copy,
                                            scale=vcol("pool_scale", 2 * l + t))
        last.then_inc(pr_act, 1)

    def dve_second(dve, l, step):
        V = nc.vector
        dve.wait_ge(pr_act, qa(l, "sqrt"))
        for t in range(5):
            w = width(l, t)
            last = V.reciprocal(prep[:, t, 0:w], prep[:, t, 0:w])
        step(last)
        for t in range(5):
            w = width(l, t)
            g = vcol("k_g" if t == 4 else "q_g", l)
            last = V.scalar_tensor_tensor(p2[:, 8 + t, 0:w], p2[:, 8 + t, 0:w], g, prep[:, t, 0:w], ALU.mult, ALU.mult)
        last.then_inc(pr_dve, 1)
        dve.wait_ge(pr_dve, qd(l, "nrm"))
        dve.wait_ge(pr_pe, qp(l, "rot"))
        for t in range(5):
            V.tensor_tensor(prep[:, t, 0:S], p2[:, 8 + t, 0:S], con("cos2"), ALU.mult)
            last = V.tensor_tensor(prep[:, t, S:T2], ps[t][:, 0:S], con("sin2"), ALU.mult)
        step(last)
        last = V.tensor_tensor(p2[:, 8:13, 0:S], prep[:, :, 0:S], prep[:, :, S:T2], ALU.add)
        last.then_inc(pr_dve, 1)
        dve.wait_ge(pr_dve, qd(l, "rot"))
        V.tensor_copy(ksw[0:HD, 0, :], p2[HD:P, 12, :])
        V.tensor_copy(ksw[HD:P, 0, :], p2[0:HD, 12, :])
        for v, b in ((0, 5), (2, 7)):
            dve.wait_ge(pr_pe, qp(l, f"vt{v}"))
            V.tensor_copy(vt[:, v], ps[b][:].rearrange("p (a b) -> p a b", a=4)).then_inc(pr_dve, 1)
        dve.wait_ge(pr_act, qa(l, "pool"))
        for w in range(2 if l == 0 else 1):
            for t in range(2):
                c = slice(w * S, (w + 1) * S)
                last = V.scalar_tensor_tensor(a_lo[:, 2 + t, c], ps[2 * w + t][:, 0:S], vcol("pool_scale", 2 * l + t),
                                              a_hi[:, 2 + t, c].bitcast(F32), ALU.mult, ALU.subtract)
        step(last)
        dve.wait_ge(nb_loaded, 256 * (l + 1))
        for q in range(4):
            v = nb[:, q].rearrange("p i (r c) -> p (i r) c", c=64)
            tq = nbt[:, 0:8, :]
            step(V.tensor_copy(tq, v[:, :, ::-1]))
            m = con("na_mask").rearrange("p (r c) -> p r c", c=64)
            for i in range(2):
                last = V.tensor_tensor(v[:, 4 * i:4 * i + 4, :], tq[:, 4 * i:4 * i + 4, :], m, ALU.add)
            step(last)

    def pool_bias(pool, l):
        for q in range(4):
            for i in range(2):
                for r in range(2):
                    base = (4 * l + q) * 15 * 31 + (7 - (2 * i + r)) * 31 - 48
                    src = bass.AP(dram["rpb"].tensor, base, [[1, HD], [31, 4], [1, HD]])
                    dst = nb[r * HD:(r + 1) * HD, q, i, :].rearrange("p (r c) -> p r c", c=HD)
                    pool.dma_start(dst, src).then_inc(nb_loaded, 16)

    pool_count = [0]

    def pool_mix(pool, l):
        G = nc.gpsimd

        def pstep(ins):
            pool_count[0] += 1
            ins.then_inc(pool_step, 1)
            pool.wait_ge(pool_step, pool_count[0])

        for w in range(2 if l == 0 else 1):
            dst = yp if w == 0 else yp2
            for b in pu:
                last = G.memset(b[:], 0.0)
            pstep(last)
            pstep(G.tensor_copy(pu[0][:, :, 16:16 + S], p2[:, 6:8, w * S:(w + 1) * S]))
            for n, (d0, d1) in enumerate(((1, 0), (1, 1), (2, 2), (4, 4))):
                lo, hi = 8, S + 24
                pstep(G.tensor_tensor(pu[n + 1][:, :, lo:hi], pu[n][:, :, lo - d0:hi - d0],
                                      pu[n][:, :, lo + d1:hi + d1], ALU.add))
            inv = con("pool_inv").rearrange("p (a b) -> p a b", a=2)
            for g in range(4):
                rows = slice((g % 2) * HD, (g % 2 + 1) * HD)
                last = G.tensor_tensor(dst[rows, g // 2, :], pu[g + 1][rows, g // 2, 16:16 + S], inv[rows, g // 2, :],
                                       ALU.mult)
            pstep(last)
            G.tensor_tensor(dst[:], dst[:], pu[0][:, :, 16:16 + S], ALU.subtract).then_inc(pool_ready, 1)
            pool.wait_ge(pool_ready, w + 1 if l == 0 else 3)

    def meet(eng, mine, others, k):
        eng.drain().then_inc(mine, 1)
        for o in others:
            eng.wait_ge(o, k)

    flow = []
    it = iter(products)
    flow += [("norm", "mix"), ("product", next(it)), ("product", next(it)), ("cmp", next(it)), ("rwkv", None),
             ("meet", 1), ("first", None), ("meet", 2), ("attend", "first"), ("meet", 3), ("product", next(it)),
             ("norm", "ffn")]
    flow += [("product", next(it)) for _ in range(4)] + [("norm", "final1")]
    k_meet = 3
    for l in range(LAYERS):
        flow += [("norm", f"{l}.0")] + [("product", next(it)) for _ in range(4)]
        flow += [("norm", f"{l}.1"), ("product", next(it)), ("meet", k_meet + 1), ("second", l), ("meet", k_meet + 2),
                 ("attend", l), ("meet", k_meet + 3), ("product", next(it)), ("norm", f"{l}.2")]
        flow += [("product", next(it)) for _ in range(4)]
        k_meet += 3
    flow += [("norm", "final2")]

    a_serial = {}
    for k in a_norms:
        a_serial[k] = KT * (a_norms.index(k) + 1)
    block = ctx.enter_context(nc.Block())

    @block.sync
    def _(sp):
        sp.dma_start(h[:], dram["x"]).then_inc(x_loaded, 16)
        for t, n in ((consts, "consts"), (vecs, "vecs"), (mats, "mats")):
            sp.dma_start(t[:], dram[n]).then_inc(consts_loaded, 16)
        sp.dma_start(pos_i[:], dram["positions"].to_broadcast([P, S])).then_inc(pos_loaded, 16)
        for pr in products:
            def load(c, turn, slot, i, pr=pr):
                wait(sp, lo_ready, c - RING + 1)
                sp.dma_start(raw[slot][:, 0:pr.size], source(pr, i)).then_inc(landed[slot], 16)
            chunk_loop(sp, pr.base, pr.n, load)
        sp.wait_ge(out_ready, 1)
        sp.dma_start(out, h[:, :, 0:S]).then_inc(out_stored, 16)
        sp.wait_ge(out_stored, 16)

    @block.gpsimd
    def _(pool):
        pool.wait_ge(a_ready, KT)
        ada_feed(pool, 0, ADA)
        for l in range(LAYERS):
            pool.wait_ge(dve_phase, 4 + 3 * l)
            pool.wait_ge(pe_phase, 4 + 3 * l)
            pool.wait_ge(act_phase, 4 + 3 * l)
            pool_bias(pool, l)
            pool_mix(pool, l)
            pool.wait_ge(nb_loaded, 256 * (l + 1))

    @block.tensor
    def _(pe):
        pe.wait_ge(consts_loaded, 48)
        pe.wait_ge(silu_c_ready, 1)
        mark = None
        for kind, x in flow:
            if kind == "norm":
                pe_norm(pe, x)
                mark = a_serial.get(x)
            elif kind == "product":
                pe_product(pe, x, mark)
                mark = None
            elif kind == "cmp":
                pe_cmp(pe)
            elif kind == "rwkv":
                pe_rwkv(pe)
            elif kind == "meet":
                meet(pe, pe_phase, (act_phase, dve_phase), x)
            elif kind == "first":
                pe_first(pe)
            elif kind == "second":
                pe_second(pe, x)
            elif kind == "attend":
                pe_attend(pe, x)

    @block.scalar
    def _(act):
        act.wait_ge(consts_loaded, 48)
        nc.scalar.activation(silu_c[:], vcol("c", 0, 16).rearrange("p (k w) -> p k w", w=2),
                             ACT.Silu).then_inc(silu_c_ready, 1)
        act_tables(act)
        act.wait_ge(x_loaded, 16)
        drained = 0
        for kind, x in flow:
            if kind == "norm":
                if drained:
                    act.wait_ge(chunk_drained, drained)
                if x == "0.0":
                    act.wait_ge(first_done, 1)
                act_norm(act, x)
            elif kind == "product":
                act_product(act, x)
                drained = x.end
            elif kind == "cmp":
                act_cmp(act)
            elif kind == "rwkv":
                act_rwkv(act)
            elif kind == "meet":
                meet(act, act_phase, (pe_phase, dve_phase), x)
            elif kind == "first":
                act_first(act)
            elif kind == "second":
                act_second(act, x)
            elif kind == "attend":
                act_attend(act, x)

    @block.vector
    def _(dve):
        made = [0]

        def step(ins):
            made[0] += 1
            ins.then_inc(dve_step, 1)
            dve.wait_ge(dve_step, made[0])

        for i, v in enumerate((1e-6, 64e-5)):
            last = nc.vector.memset(eps[:, i:i + 1], v)
        step(last)
        dve.wait_ge(consts_loaded, 48)
        dve_tables(dve, step)
        dve.wait_ge(x_loaded, 16)
        for kind, x in flow:
            if kind == "norm":
                if x == "0.0":
                    dve.wait_ge(first_done, 1)
                dve_norm(dve, x, step)
            elif kind == "product":
                gate = None
                if x.name.startswith("w_dn1"):
                    l = int(x.name[-1])
                    gate = lambda j, w, l=l: half_gate[:, l, 0, bass.ds(j, 1), w:w + 1].rearrange("p a b -> p (a b)")
                elif x.name.startswith("w_dn2"):
                    l = int(x.name[-1])
                    gate = lambda j, w, l=l: half_gate[:, l, 1, bass.ds(j, 1), w:w + 1].rearrange("p a b -> p (a b)")
                elif x.name in ("w_out_0", "w_out_1"):
                    l = int(x.name[-1])
                    gate = lambda j, w, l=l: mod[:, l, bass.ds(5 * KT + j, 1), w:w + 1].rearrange("p a b -> p (a b)")
                dve_product(dve, x, gate)
            elif kind == "cmp":
                dve_cmp(dve, step)
            elif kind == "rwkv":
                dve_rwkv(dve, step)
                dve_mods(dve, step)
            elif kind == "meet":
                meet(dve, dve_phase, (pe_phase, act_phase), x)
            elif kind == "first":
                dve_first(dve, step)
            elif kind == "second":
                dve_second(dve, x, step)
            elif kind == "attend":
                dve_attend(dve, x, step)


def kernel(**inputs):
    import numpy as _np
    import concourse.bacc as _bacc
    from concourse.bass_utils import run_bass_kernel_spmd as _run

    g = {k: _np.asarray(v) for k, v in inputs.items()}

    def cols(v):
        return v.reshape(-1, P).T

    def chunks(w, m):
        k, n = w.shape
        return w.reshape(k // P, P, n // m, m).transpose(2, 1, 0, 3).reshape(n // m, P, (k // P) * m)

    def ffn(gate, up):
        return _np.concatenate([chunks(gate, P), chunks(up, P)], axis=2)

    def down(w):
        return _np.concatenate([chunks(w[:FH * P], P), chunks(w[FH * P:], P)], axis=0)

    w_in = g["w_in"][0]
    tail = _np.zeros((D, P), w_in.dtype)
    tail[:, 0:32] = w_in[:, 1792:R_COLS]
    tail[:, 32:56] = w_in[:, R_COLS + 1280:]
    vec = _np.zeros((P, VN), _np.float32)

    def put(name, a, o=0, rows=P):
        vec[:rows, VAT[name][0] + o:VAT[name][0] + o + a.shape[1]] = a

    put("norm_mix", cols(g["norm_mix"]))
    put("norm_ffn", cols(g["norm_ffn"]))
    put("norm_final", cols(g["norm_final"]))
    put("final_g", cols(g["final_g_2"]))
    put("norm_g", cols(g["norm_g_2"]))
    put("mu", cols(g["mu_shift"][0, :1792]))
    put("mu", g["mu_shift"][0, 1792:].reshape(32, 1), 14, 32)
    for n in ("w0", "a0", "k_k", "k_a", "r_k", "lnx_w", "lnx_b", "pe_k", "pe_v", "bk1", "bv1"):
        put(n, cols(g[n]))
    put("b_ada", cols(g["b_ada_2"]))
    put("pool_scale", cols(g["pool_scale_2"]))
    for n, s in (("q_g", "q_norm_g_2"), ("k_g", "k_norm_g_2")):
        put(n, _np.concatenate([g[s].T, g[s].T], axis=0))
    put("c", _np.stack([cols(g["c_2"]), cols(g["c_ctx_2"])], axis=2).reshape(P, 16))
    mats = _np.zeros((P, MN), _np.float32)
    mats[:, M_G2:M_G2 + 512] = g["g2"][0, :128]
    mats[:32, M_G2T:M_G2T + 512] = g["g2"][0, 128:]
    mats[:64, M_LORA:M_LORA + 512] = g["w2"][0]
    mats[64:, M_LORA:M_LORA + 512] = g["a2"][0]
    k2 = g["wk2"][0].reshape(2, P, HD).transpose(1, 0, 2)
    mats[:, M_CK2:M_CK2 + 256] = _np.concatenate([k2, k2], axis=2).reshape(P, 256)
    mats[:, M_CV2:M_CV2 + 128] = g["wv2"][0].reshape(2, P, HD).transpose(1, 0, 2).reshape(P, 128)
    for l in range(LAYERS):
        for q in range(4):
            o = M_POOL + (2 * l + q // 2) * P + (q % 2) * HD
            mats[(q % 2) * HD:(q % 2) * HD + HD, o:o + HD] = g["pool_w_2"][l, q]
    up1 = [ffn(g["ffn1_up_2"][l][:, :FF], g["ffn1_up_2"][l][:, FF:]) for l in range(LAYERS)]
    up2 = [ffn(g["ffn2_up_2"][l][:, :FF], g["ffn2_up_2"][l][:, FF:]) for l in range(LAYERS)]
    rpb = g["na_rpb_2"]
    arrays = {
        "x": _np.concatenate([g["x"][0].T.reshape(KT, P, S), g["ctx_2"][0].T.reshape(KT, P, S)], axis=2)
                .transpose(1, 0, 2),
        "positions": g["positions"],
        "consts": const_array(),
        "vecs": vec,
        "mats": mats,
        "rpb": rpb[..., ::-1].reshape(1, -1),
        "w_in": _np.concatenate([chunks(w_in[:, :1792], 2 * P), chunks(w_in[:, R_COLS:R_COLS + 1280], 2 * P)]),
        "w_tail": chunks(tail, P),
        "w_cmp": _np.concatenate([chunks(g[n][0][h * D:(h + 1) * D], 2 * P) for n in ("wk1", "wv1") for h in (0, 1)]),
        "w_out": chunks(g["w_out"][0], 2 * P),
        "w_gu": ffn(g["w_gate"][0], g["w_up"][0]),
        "w_dn": down(g["w_down"][0]),
        "w_ada": _np.concatenate([chunks(g["w_ada_2"][l], 2 * P) for l in range(LAYERS)]),
    }
    for l in range(LAYERS):
        arrays[f"w_gu1_{l}"] = up1[l]
        arrays[f"w_dn1_{l}"] = down(g["ffn1_down_2"][l])
        arrays[f"w_gu2_{l}"] = up2[l]
        arrays[f"w_dn2_{l}"] = down(g["ffn2_down_2"][l])
        arrays[f"w_in_{l}"] = chunks(g["w_in_2"][l], 2 * P)
        arrays[f"w_out_{l}"] = chunks(g["w_out_2"][l], 2 * P)
    arrays = {f"in_{k}": _np.ascontiguousarray(v) for k, v in arrays.items()}

    nc = _bacc.Bacc("TRN2", target_bir_lowering=False, num_devices=1)
    dram = {k[3:]: nc.dram_tensor(k, v.shape, mybir.dt.from_np(v.dtype), kind="ExternalInput").ap()
            for k, v in arrays.items()}
    out = nc.dram_tensor("out_h", (P, KT, S), F32, kind="ExternalOutput").ap()
    program(nc, dram, out)
    r = _run(nc, [arrays], core_ids=[0])
    got = r.results[0]["out_h"]
    return got.transpose(2, 1, 0).reshape(1, S, D)
```

```python
from contextlib import ExitStack
import math

import numpy as np
import concourse.bass as bass
from concourse import mybir

F32 = mybir.dt.float32
F32R = mybir.dt.float32r
I32 = mybir.dt.int32
ALU = mybir.AluOpType
ACT = mybir.ActivationFunctionType
AX_X = mybir.AxisListType.X

P = 128
D = 1024
KT = D // P
S = 256
T2 = 2 * S
FF = 2816
FT = FF // P
FH = FT // 2
R_COLS, N_COLS = 1824, 1304
LAYERS = 2
N_MOD = 9
HD = 64
NEG = -1e30
RING = 3
HEAD_K = KT // 2
CH = KT * 2 * P
DECAY = math.exp(-0.5)
SCALE = HD ** -0.5
CHUNK = 64
NCMP = 15


def const_layout():
    names = [("ident", P), ("ones", P), ("bd", P), ("rot1", P), ("rot2", P), ("bdmask", P),
             ("m_su", P), ("m_u", P), ("m16", P), ("moff", P), ("m16t", P),
             ("scan0", S), ("freq", 1), ("causal", 2 * P), ("cmp_add", 2 * NCMP), ("cmp_ok", 2 * NCMP),
             ("na_mask", S), ("cos2", S), ("sin2", S), ("pool_inv", 2 * S), ("pair", 2), ("heads", 50)]
    at, n = {}, 0
    for name, w in names:
        at[name] = (n, w)
        n += w
    return at, n


def const_array():
    at, n = const_layout()
    c = np.zeros((P, n), np.float32)

    def put(name, a):
        o, w = at[name]
        c[:, o:o + w] = np.asarray(a, np.float32).reshape(P, w)

    p = np.arange(P)[:, None]
    f = np.arange(P)[None, :]
    put("ident", p == f)
    put("ones", np.full((P, P), 1.0 / D))
    put("heads", [[float(j % 10 == 2 * (j // 10) + (q >= HD)) for j in range(50)] for q in range(P)])
    put("pair", p % 2 == f[:, 0:2])
    put("bd", p // HD == f // HD)
    put("bdmask", p // HD == f // HD)
    r1 = np.zeros((P, P))
    r2 = np.zeros((P, P))
    for h in (0, HD):
        for i in range(8):
            r1[h + i + 8, h + i] = -1.0
            r1[h + i, h + i + 8] = 1.0
        for q in (0, 32):
            for i in range(16):
                r2[h + q + i + 16, h + q + i] = -1.0
                r2[h + q + i, h + q + i + 16] = 1.0
    put("rot1", r1)
    put("rot2", r2)
    same = p // CHUNK == f // CHUNK
    same16 = p // 16 == f // 16
    put("m_su", same & (p < f))
    put("m_u", same & (p <= f))
    put("m16", same16 & (p < f))
    put("moff", same & (p < f) & ~same16)
    put("m16t", same16 & (f < p))
    t = np.arange(S)
    put("scan0", np.broadcast_to((t % CHUNK != 0), (P, S)))
    inv = np.power(np.float32(500000.0), -np.arange(8, dtype=np.float32) * np.float32(2.0) / np.float32(16))
    fr = np.zeros(P, np.float32)
    for h in (0, HD):
        fr[h:h + 8] = inv
        fr[h + 8:h + 16] = inv
    put("freq", fr)
    put("causal", np.concatenate([np.zeros((P, P)), np.where(f <= p, 0.0, NEG)], 1))
    n_ = np.arange(NCMP)
    ok = np.concatenate([(16 * n_ + 31)[None, :] <= (i * P + p) for i in range(2)], 1)
    put("cmp_ok", ok)
    put("cmp_add", np.where(ok, 0.0, NEG))
    qc = p % 64
    kc = (t % 64)[None, :]
    c0 = np.clip(qc - 8, 0, 48)
    put("na_mask", np.where((kc >= c0) & (kc < c0 + 16), 0.0, NEG))
    inv2 = np.float32(10000.0) ** (-np.arange(0, 32, 2, dtype=np.float32) / np.float32(32))
    ang = np.zeros((P, S), np.float32)
    for h in (0, HD):
        for i in range(16):
            ang[h + i] = ang[h + i + 16] = (t // 64).astype(np.float32) * inv2[i]
            ang[h + 32 + i] = ang[h + 48 + i] = (t % 64).astype(np.float32) * inv2[i]
    put("cos2", np.cos(ang))
    put("sin2", np.sin(ang))
    pin = np.zeros((P, 2, S))
    for g, w in enumerate((2, 4, 8, 16)):
        lo = np.clip(t - w // 2, 0, S)
        hi = np.clip(t - w // 2 + w, 0, S)
        pin[(g % 2) * 64:(g % 2) * 64 + 64, g // 2] = 1.0 / (hi - lo)
    put("pool_inv", pin)
    return c


def head_rows():
    r = np.zeros((10, 5 * P), np.float32)
    for t in range(5):
        for h in range(2):
            r[2 * t + h, t * P + h * HD:t * P + (h + 1) * HD] = 1.0
    return r


def vec_layout():
    names = [("norm_mix", 8), ("norm_ffn", 8), ("norm_final", 8), ("final_g", 8), ("norm_g", 48),
             ("mu", 15), ("w0", 4), ("a0", 4), ("k_k", 4), ("k_a", 4), ("r_k", 4), ("lnx_w", 4), ("lnx_b", 4),
             ("pe_k", 16), ("pe_v", 16), ("bk1", 2), ("bv1", 2), ("b_ada", 144), ("pool_scale", 4),
             ("q_g", 2), ("k_g", 2), ("c", 16)]
    at, n = {}, 0
    for name, w in names:
        at[name] = (n, w)
        n += w
    return at, n


CAT, CN = const_layout()
VAT, VN = vec_layout()
M_G2, M_G2T, M_LORA, M_CK2, M_CV2, M_POOL = 0, 512, 1024, 1536, 1792, 1920
MN = 1920 + 2 * 2 * P


def counts(names):
    return {n: i + 1 for i, n in enumerate(names)}


def one(ap):
    return ap.unsqueeze(1)


def wait(eng, sem, v):
    if not isinstance(v, int) or v > 0:
        eng.wait_ge(sem, v)


def chunk_loop(eng, base, n, body, stride=1):
    lead = min(n, RING) if base == 0 else 0
    rest = (n - lead) // RING
    for i in range(lead):
        body(base + i, (base + i) // RING, (base + i) % RING, i)
    assert lead == 0 or stride == 1
    b = base + lead
    if rest > 1:
        with eng.Fori(0, rest) as r:
            for j in range(RING):
                c = b + stride * j
                body(c + stride * RING * r, c // RING + stride * r, c % RING, lead + j + RING * r)
    else:
        rest = 0
    for i in range(lead + rest * RING, n):
        c = base + stride * i
        body(c, c // RING, c % RING, i)


ADA = N_MOD * KT // 2


class Product:

    def __init__(self, base, name, n, kt, mt, tokens, kind, first=0, tile0=0, ada=None):
        self.base, self.name, self.n, self.kt, self.mt = base, name, n, kt, mt
        self.tokens, self.kind, self.first = tokens, kind, first
        self.ahead = None
        self.norm = None
        self.squares = None
        self.tile0 = tile0
        self.ada = ada
        self.size = kt * mt * P
        self.stride = 1 if ada is None else 2
        self.lead_size = self.size if ada is None else CH
        self.end = base + n * self.stride


def plan():
    out = []
    n_ada = [0]

    def add(name, n, kt, mt, tokens, kind, first=0, tile0=0, ada=False):
        base = out[-1].end if out else 0
        out.append(Product(base, name, n, kt, mt, tokens, kind, first, tile0, n_ada[0] if ada else None))
        n_ada[0] += n if ada else 0

    def add_gu(name, tokens, half, ada=False):
        head = RING if ada and half == 0 else 0
        if head:
            add(name, head, KT, 2, tokens, "gu")
        add(name, FH - head, KT, 2, tokens, "gu", half * FH + head, head, ada)

    add("w_in", 12, KT, 2, S, "proj1")
    add("w_tail", 1, KT, 1, S, "tail1", ada=True)
    add("w_out", 4, KT, 2, S, "res", ada=True)
    for half in range(2):
        add_gu("w_gu", S, half, ada=True)
        add("w_dn", KT, FH, 1, S, "down", half * KT, ada=True)
    for l in range(LAYERS):
        for half in range(2):
            add_gu(f"w_gu1_{l}", T2, half, ada=l == 0 and half == 0)
            add(f"w_dn1_{l}", KT, FH, 1, T2, "down", half * KT, ada=l == 0)
        add(f"w_in_{l}", 7, KT, 2, T2, "proj2")
        t = T2 if l == 0 else S
        add(f"w_out_{l}", 4, KT, 2, t, "res")
        for half in range(2):
            add_gu(f"w_gu2_{l}", t, half)
            add(f"w_dn2_{l}", KT, FH, 1, t, "down", half * KT, ada=l == 0 and half == 0)
    assert n_ada[0] == LAYERS * ADA
    for a, b in zip(out, out[1:]):
        if a.kind not in ("tail1", "proj2"):
            a.ahead = b
    gus = [p for p in out if p.kind == "gu" and p.first == 0]
    downs = [p for p in out if p.kind == "down" and p.first]
    projs = [p for p in out if p.kind == "proj2"]
    ress = [p for p in out if p.kind == "res"]
    out[0].norm = "mix"
    for p, n in zip(gus, ["ffn", "0.0", "0.2", "1.0", "1.2"]):
        p.norm = n
    for p, n in zip(projs, ["0.1", "1.1"]):
        p.norm = n
    for p, n in zip(downs, ["final1", "0.1", "1.0", "1.1", "final2"]):
        p.squares = n
    for p, n in zip(ress, ["ffn", "0.2", "1.2"]):
        p.squares = n
    return out


def program(nc, dram, out):
    ctx = ExitStack()
    cursor = [16512]

    def place(name, shape, dt, off=None):
        n = int(np.prod(shape[1:])) * 4
        if off is None:
            off = cursor[0]
            cursor[0] += (n + 31) // 32 * 32
        return nc.alloc_sbuf_tensor_at(name, shape, dt, offset=off)

    def sem(name):
        return ctx.enter_context(nc.semaphore(name))

    h = place("h", [P, KT, T2], F32)
    at_a = cursor[0]
    a_hi = place("a_hi", [P, KT, T2], F32R)
    a_lo = place("a_lo", [P, KT, T2], F32R)
    at_f = cursor[0]
    ff_hi = place("ff_hi", [P, FH, T2], F32R)
    ff_lo = place("ff_lo", [P, FH, T2], F32R)
    raw = [place(f"raw{i}", [P, CH], F32) for i in range(RING)]
    at_w = cursor[0]
    w_hi = [place(f"w_hi{i}", [P, CH], F32R) for i in range(RING)]
    w_lo = [place(f"w_lo{i}", [P, CH], F32R) for i in range(RING)]
    consts = place("consts_sb", [P, CN], F32)
    vecs = place("vecs_sb", [P, VN], F32)
    mats = place("mats_sb", [P, MN], F32)
    mod = place("mod", [P, LAYERS, N_MOD * KT, 2], F32)
    gmod = place("gmod", [P, LAYERS, 3, KT, 2], F32)
    half_gate = place("half_gate", [P, LAYERS, 2, KT, 2], F32)
    silu_c = place("silu_c", [P, KT, 2], F32)
    c_split = place("c_split", [P, KT, 4], F32R)
    eps = place("eps", [P, 4], F32)
    warm = place("warm", [P, 1], F32)
    rt = place("rt", [P, T2], F32)
    rs = place("rs", [P, T2], F32)
    silu_g = place("silu_g", [P, T2], F32)
    gu = [place(f"gu{i}", [P, T2], F32) for i in range(RING)]
    nrm = place("nrm", [P, KT, T2], F32, at_f)
    p1 = place("p1", [P, 25, S], F32, at_f)
    direct = [place(f"direct{i}", [P, CH], F32, at_f + 28672 + 4 * CH * i) for i in range(2)]
    p2 = place("p2", [P, 14, T2], F32, at_f)
    ps = [ctx.enter_context(nc.psum_tensor(f"ps{i}", [P, 512], F32)) for i in range(8)]

    def con(name, lo=0, hi=None):
        o, w = CAT[name]
        return consts[:, o + lo:o + (w if hi is None else hi)]

    def vcol(name, i=0, n=1, rows=slice(0, P)):
        o = VAT[name][0] + i
        return vecs[rows, o:o + n]

    x_loaded = sem("x_loaded")
    consts_loaded = sem("consts_loaded")
    mats_loaded = sem("mats_loaded")
    landed = [sem(f"landed{i}") for i in range(RING)]
    hi_ready = sem("hi_ready")
    lo_ready = sem("lo_ready")
    chunk_mult = sem("chunk_mult")
    chunk_drained = sem("chunk_drained")
    silu_ready = sem("silu_ready")
    ffhi_ready = sem("ffhi_ready")
    ff_ready = sem("ff_ready")
    sq_ready = sem("sq_ready")
    sq_added = sem("sq_added")
    sq_cleared = sem("sq_cleared")
    ms_ready = sem("ms_ready")
    rt_ready = sem("rt_ready")
    nrm_ready = sem("nrm_ready")
    ahi_ready = sem("ahi_ready")
    a_ready = sem("a_ready")
    dve_step = sem("dve_step")
    pe_phase = sem("pe_phase")
    act_phase = sem("act_phase")
    dve_phase = sem("dve_phase")
    direct_landed = [sem(f"direct_landed{i}") for i in range(2)]
    direct_mult = sem("direct_mult")
    silu_c_ready = sem("silu_c_ready")
    c_split_ready = sem("c_split_ready")
    ada_folded = sem("ada_folded")
    first_done = sem("first_done")
    out_ready = sem("out_ready")
    out_stored = sem("out_stored")

    products = plan()
    gu_before = {}
    n_gu = 0
    for pr in products:
        gu_before[pr.base] = n_gu
        if pr.kind == "gu":
            n_gu += pr.n

    def source(pr, i):
        return dram[pr.name][bass.ds(pr.first + i, 1)].rearrange("a p f -> p (a f)") if not isinstance(i, int) \
            else dram[pr.name][pr.first + i]

    norms = {"mix": (0, S), "ffn": (1, S), "final1": (2, S)}
    for l in range(LAYERS):
        for n in range(3):
            norms[f"{l}.{n}"] = (3 + 3 * l + n, T2 if (l == 0 or n < 2) else S)
    norms["final2"] = (9, S)
    a_norms = [k for k in norms if k not in ("final1", "final2")]

    def split_hi(act, c, turn, slot, size):
        act.wait_ge(landed[slot], 16 * (turn + 1))
        wait(act, chunk_mult, c - RING + 1)
        nc.scalar.activation(w_hi[slot][:, 0:size], raw[slot][:, 0:size], ACT.Copy).then_inc(hi_ready, 1)

    def split_lo(dve, c, slot, size):
        dve.wait_ge(hi_ready, c + 1)
        nc.vector.tensor_tensor(w_lo[slot][:, 0:size], raw[slot][:, 0:size],
                                w_hi[slot][:, 0:size].bitcast(F32), ALU.subtract).then_inc(lo_ready, 1)

    def multiply(pe, pr, c, slot, banks, lhs, rhs, start=True, stop=True, before=None):
        pe.wait_ge(lo_ready, c + 1)
        wait(pe, chunk_drained, c - RING + 1)
        for m in range(pr.mt):
            for k in range(pr.kt):
                if before is not None and m == 0:
                    before(k)
                w1, w2 = lhs(slot, m, k)
                a1, a2 = rhs(k)
                nc.tensor.matmul(banks[m], w1, a1, start=start and k == 0, stop=False)
                nc.tensor.matmul(banks[m], w1, a2, start=False, stop=False)
                last = nc.tensor.matmul(banks[m], w2, a1, start=False, stop=stop and k == pr.kt - 1)
        last.then_inc(chunk_mult, 1)

    def by_cols(kt, width):
        def lhs(slot, m, k):
            o = k * width + m * P
            return w_hi[slot][:, o:o + P], w_lo[slot][:, o:o + P]
        return lhs

    def by_part(slot, m, k):
        o = (m * KT + k) * P
        return w_hi[slot][:, o:o + P], w_lo[slot][:, o:o + P]

    def bank(slot, m, n):
        return ps[2 * slot + m][:, 0:n]

    def multiply_ada(pe, c, slot):
        pe.wait_ge(lo_ready, c + 1)
        wait(pe, chunk_drained, c - RING + 1)
        for k in range(KT):
            w = slice(k * 2 * P, (k + 1) * 2 * P)
            nc.tensor.matmul(ps[2 * slot][0:4, 0:2 * P], c_split[:, k, :], w_hi[slot][:, w], start=k == 0, stop=False)
            last = nc.tensor.matmul(ps[2 * slot][0:4, 0:2 * P], c_split[:, k, :], w_lo[slot][:, w],
                                    start=False, stop=k == KT - 1)
        last.then_inc(chunk_mult, 1)

    def drain_ada(dve, c, slot):
        dve.wait_ge(chunk_mult, c + 1)
        nc.vector.tensor_copy(rt[0:4, 0:2 * P], ps[2 * slot][0:4, 0:2 * P]).then_inc(chunk_drained, 1)

    def fold_ada(pe, c, i):
        pe.wait_ge(chunk_drained, c + 1)
        for m in range(2):
            col = bass.ds(4 * i + 2 * m, 2)
            last = nc.tensor.matmul(ps[6][:, col], rt[0:4, m * P:(m + 1) * P], con("pair")[0:4, :],
                                    start=True, stop=True)
        last.then_inc(ada_folded, 1)

    def tokens_of(pr, i):
        if pr.kind == "proj2" and pr.name != "w_in_0" and i not in (1, 2, 6):
            return S
        return pr.tokens

    def pe_product(pe, pr):
        t = pr.tokens
        lhs = by_part if pr.kind == "gu" else by_cols(pr.kt, pr.mt * P)
        if pr.kind == "down":
            pe.wait_ge(ff_ready, gu_before[pr.base])
            rhs = lambda k: (ff_hi[:, k, 0:t], ff_lo[:, k, 0:t])
        else:
            rhs = lambda k: (a_hi[:, k, 0:t], a_lo[:, k, 0:t])
        first = 0
        if pr.norm is not None:
            first = RING
            pe.wait_ge(lo_ready, pr.base + 2)
            wait(pe, chunk_drained, pr.base)
            serial = KT * a_norms.index(pr.norm)
            for i, ks in [(i, [k]) for k in range(HEAD_K) for i in (0, 1)] + [(2, range(HEAD_K))] \
                    + [(i, range(HEAD_K, KT)) for i in range(RING)]:
                if i == 2 and ks[0] == 0:
                    pe.wait_ge(lo_ready, pr.base + RING)
                slot = (pr.base + i) % RING
                n = tokens_of(pr, i)
                for m in range(pr.mt):
                    for k in ks:
                        if i == 0 and m == 0:
                            pe.wait_ge(a_ready, serial + k + 1)
                        a1, a2 = a_hi[:, k, 0:n], a_lo[:, k, 0:n]
                        w1, w2 = lhs(slot, m, k)
                        o = bank(slot, m, n)
                        nc.tensor.matmul(o, w1, a1, start=k == 0, stop=False)
                        nc.tensor.matmul(o, w1, a2, start=False, stop=False)
                        last = nc.tensor.matmul(o, w2, a1, start=False, stop=k == KT - 1)
                if ks[-1] == KT - 1:
                    last.then_inc(chunk_mult, 1)
        if pr.kind == "proj2":
            for i in range(first, pr.n):
                c = pr.base + i
                n = tokens_of(pr, i)
                multiply(pe, pr, c, c % RING, [bank(c % RING, m, n) for m in range(2)], lhs,
                         lambda k: (a_hi[:, k, 0:n], a_lo[:, k, 0:n]))
            return

        def body(c, turn, slot, i):
            if pr.ada is not None:
                multiply_ada(pe, c, slot)
                c, slot = c + 1, (slot + 1) % RING
            multiply(pe, pr, c, slot, [bank(slot, m, t) for m in range(pr.mt)], lhs, rhs)
            if pr.ada is not None:
                fold_ada(pe, c - 1, pr.ada + i)

        chunk_loop(pe, pr.base + first, pr.n - first, body, pr.stride)

    def staged(eng, pr, split, evac, chained, evac_ada=None):
        def split_next(c, turn, slot, of):
            split(c, turn, slot, of.lead_size)
            if of.ada is not None:
                split(c + 1, turn + (slot + 1) // RING, (slot + 1) % RING, of.size)

        head = 0
        if pr.norm is not None:
            head = RING - 1
            for i in range(head):
                c = pr.base + i
                evac(c, c // RING, c % RING, i)
        elif not chained:
            split_next(pr.base, pr.base // RING, pr.base % RING, pr)

        def body(c, turn, slot, i):
            after = (c + pr.stride, turn + (slot + pr.stride) // RING, (slot + pr.stride) % RING, pr)
            if pr.ada is not None:
                if evac_ada is not None:
                    evac_ada(c, slot)
                split_next(*after)
                evac(c + 1, turn + (slot + 1) // RING, (slot + 1) % RING, i)
            else:
                split_next(*after)
                evac(c, turn, slot, i + head)

        chunk_loop(eng, pr.base + head, pr.n - 1 - head, body, pr.stride)
        c = pr.end - 1
        if pr.ada is not None and evac_ada is not None:
            evac_ada(c - 1, (c - 1) % RING)
        if pr.ahead is not None:
            split_next(c + 1, (c + 1) // RING, (c + 1) % RING, pr.ahead)
            if pr.ahead.norm:
                split_next(c + 2, (c + 2) // RING, (c + 2) % RING, pr.ahead)
        evac(c, c // RING, c % RING, pr.n - 1)

    def square_buffer(pr, slot, m):
        i = (slot - (pr.end - 1) % RING + pr.n * RING + pr.stride * (pr.n - 1)) * pr.stride % RING
        return gu[(pr.mt * i + m) % RING]

    chained = {pr.base: (n > 0 and products[n - 1].ahead is pr) for n, pr in enumerate(products)}

    def act_product(act, pr):
        t = pr.tokens

        def split(c, turn, slot, size):
            split_hi(act, c, turn, slot, size)

        def evac(c, turn, slot, i):
            if pr.squares is not None:
                act.wait_ge(chunk_drained, c + 1)
                for m in range(pr.mt):
                    q = pr.mt * i + m
                    b = square_buffer(pr, slot, m)
                    act.wait_ge(sq_added, KT * norm_serial(pr.squares) + q - RING + 1)
                    nc.scalar.activation(one(b[:, 0:t]), h[:, bass.ds(q, 1), 0:t], ACT.Square).then_inc(sq_ready, 1)
                return
            if pr.kind != "gu":
                return
            act.wait_ge(chunk_mult, c + 1)
            nc.scalar.activation(silu_g[:, 0:t], ps[2 * slot][:, 0:t], ACT.Silu).then_inc(silu_ready, 1)
            act.wait_ge(chunk_drained, c + 1)
            nc.scalar.activation(ff_hi[:, bass.ds(pr.tile0 + i, 1), 0:t], one(gu[slot][:, 0:t]), ACT.Copy).then_inc(ffhi_ready, 1)

        staged(act, pr, split, evac, chained[pr.base])

    def add_square(dve, n, q, b, t):
        dve.wait_ge(sq_ready, KT * n + q + 1)
        wait(dve, sq_added, KT * n + q)
        nc.vector.tensor_tensor(silu_g[:, 0:t], silu_g[:, 0:t], b[:, 0:t], ALU.add).then_inc(sq_added, 1)

    def dve_product(dve, pr, gate=None):
        t = pr.tokens

        def split(c, turn, slot, size):
            split_lo(dve, c, slot, size)

        def evac(c, turn, slot, i):
            if pr.kind == "gu":
                u = gu_before[pr.base] + i
                dve.wait_ge(silu_ready, u + 1)
                nc.vector.tensor_tensor(gu[slot][:, 0:t], ps[2 * slot + 1][:, 0:t], silu_g[:, 0:t],
                                        ALU.mult).then_inc(chunk_drained, 1)
                dve.wait_ge(ffhi_ready, u + 1)
                nc.vector.tensor_tensor(ff_lo[:, bass.ds(pr.tile0 + i, 1), 0:t], one(gu[slot][:, 0:t]),
                                        ff_hi[:, bass.ds(pr.tile0 + i, 1), 0:t].bitcast(F32),
                                        ALU.subtract).then_inc(ff_ready, 1)
                return
            dve.wait_ge(chunk_mult, c + 1)
            for m in range(pr.mt):
                j = pr.mt * i + m
                b = ps[2 * slot + m]
                if pr.kind in ("proj1", "tail1"):
                    dst = p1[:, bass.ds(j + (24 if pr.kind == "tail1" else 0), 1), :]
                    last = nc.vector.tensor_copy(dst, one(b[:, 0:t]))
                elif pr.kind == "proj2":
                    n = tokens_of(pr, i)
                    last = nc.vector.tensor_copy(p2[:, j, 0:n], b[:, 0:n])
                elif gate is None:
                    hk = h[:, bass.ds(j, 1), 0:t]
                    last = nc.vector.tensor_tensor(hk, one(b[:, 0:t]), hk, ALU.add)
                else:
                    for w in range(t // S):
                        hk = h[:, bass.ds(j, 1), w * S:(w + 1) * S]
                        last = nc.vector.scalar_tensor_tensor(hk, one(b[:, w * S:(w + 1) * S]),
                                                              gate(j, w), hk, ALU.mult, ALU.add)
            last.then_inc(chunk_drained, 1)
            if pr.squares is not None:
                for m in range(pr.mt):
                    add_square(dve, norm_serial(pr.squares), pr.mt * i + m, square_buffer(pr, slot, m), t)

        if pr.kind == "proj2":
            for i in range(pr.n):
                c = pr.base + i
                if RING <= i + 1 < pr.n:
                    split(c + 1, 0, (c + 1) % RING, pr.size)
                evac(c, 0, c % RING, i)
            return
        if pr.squares is not None:
            nc.vector.memset(silu_g[:, 0:t], 0.0).then_inc(sq_cleared, 1)
            dve.wait_ge(sq_cleared, norm_serial(pr.squares) + 1)
        staged(dve, pr, split, evac, chained[pr.base], lambda c, slot: drain_ada(dve, c, slot))

    def norm_serial(key, a=False):
        keys = a_norms if a else list(norms)
        return keys.index(key)

    def gain(key, k, w):
        if "." not in key:
            name, i = {"mix": ("norm_mix", k), "ffn": ("norm_ffn", k), "final1": ("norm_final", k),
                       "final2": ("final_g", k)}[key]
            return vcol(name, i)
        l, n = int(key[0]), int(key[2])
        return gmod[:, l, n, k, w:w + 1]

    def halves(key):
        t = norms[key][1]
        if "." not in key:
            return [(0, slice(0, t))]
        return [(w, slice(w * S, (w + 1) * S)) for w in range(t // S)]

    def shift(key, k, w):
        return mod[:, int(key[0]), 3 * int(key[2]) * KT + k, w:w + 1]

    own_squares = ("mix", "0.0")
    feeds = {pr.norm: pr for pr in products if pr.norm is not None}

    def splits_left(key):
        pr = feeds.get(key)
        if pr is None:
            return []
        done = 2 if any(p.ahead is pr for p in products) else 0
        return [(c, c // RING, c % RING, pr.size) for c in range(pr.base + done, pr.base + RING)]

    def act_norm(act, key):
        n, t = norm_serial(key), norms[key][1]
        if key in own_squares:
            for k in range(KT):
                wait(act, sq_added, KT * n + k - RING + 1)
                nc.scalar.activation(gu[k % RING][:, 0:t], h[:, k, 0:t], ACT.Square).then_inc(sq_ready, 1)
        left = splits_left(key)
        for c, turn, slot, size in left[:-1]:
            split_hi(act, c, turn, slot, size)
        nc.scalar.activation(warm[:], eps[:, 0:1], ACT.Sqrt)
        act.wait_ge(ms_ready, n + 1)
        nc.scalar.activation(rt[:, 0:t], ps[7][:, 0:t], ACT.Sqrt, bias=eps[:, 0:1]).then_inc(rt_ready, 1)
        for c, turn, slot, size in left[-1:]:
            split_hi(act, c, turn, slot, size)
        if key.startswith("final"):
            return
        na = norm_serial(key, True)
        for k in range(KT):
            act.wait_ge(nrm_ready, KT * na + k + 1)
            if "." in key:
                for w, c in halves(key):
                    last = nc.scalar.activation(a_hi[:, k, c], nrm[:, k, c], ACT.Identity, bias=shift(key, k, w))
            else:
                last = nc.scalar.activation(a_hi[:, k, 0:t], nrm[:, k, 0:t], ACT.Copy)
            last.then_inc(ahi_ready, 1)

    def pe_norm(pe, key):
        n, t = norm_serial(key), norms[key][1]
        pe.wait_ge(sq_added, KT * (n + 1))
        nc.tensor.matmul(ps[7][:, 0:t], con("ones"), silu_g[:, 0:t], start=True, stop=True).then_inc(ms_ready, 1)

    def dve_norm(dve, key, step):
        n, t = norm_serial(key), norms[key][1]
        if key in own_squares:
            nc.vector.memset(silu_g[:, 0:t], 0.0).then_inc(sq_cleared, 1)
            dve.wait_ge(sq_cleared, n + 1)
            for k in range(KT):
                add_square(dve, n, k, gu[k % RING], t)
        left = splits_left(key)
        for c, turn, slot, size in left[:-1]:
            split_lo(dve, c, slot, size)
        dve.wait_ge(rt_ready, n + 1)
        step(nc.vector.reciprocal(rs[:, 0:t], rt[:, 0:t]))
        if key.startswith("final"):
            for k in range(KT):
                ins = nc.vector.scalar_tensor_tensor(h[:, k, 0:t], h[:, k, 0:t], gain(key, k, 0), rs[:, 0:t],
                                                     ALU.mult, ALU.mult)
                if k < KT - 1:
                    step(ins)
            ins.then_inc(out_ready if key == "final2" else first_done, 1)
            return
        na = norm_serial(key, True)

        def lower(k):
            dve.wait_ge(ahi_ready, KT * na + k + 1)
            if "." in key:
                for w, c in halves(key):
                    last = nc.vector.scalar_tensor_tensor(a_lo[:, k, c], nrm[:, k, c], shift(key, k, w),
                                                          a_hi[:, k, c].bitcast(F32), ALU.add, ALU.subtract)
            else:
                last = nc.vector.tensor_tensor(a_lo[:, k, 0:t], nrm[:, k, 0:t], a_hi[:, k, 0:t].bitcast(F32),
                                               ALU.subtract)
            last.then_inc(a_ready, 1)

        for k in range(KT):
            for w, c in halves(key):
                last = nc.vector.scalar_tensor_tensor(nrm[:, k, c], h[:, k, c], gain(key, k, w), rs[:, c],
                                                      ALU.mult, ALU.mult)
            last.then_inc(nrm_ready, 1)
            if k:
                lower(k - 1)
            if k == HEAD_K:
                for c, turn, slot, size in left[-1:]:
                    split_lo(dve, c, slot, size)
        lower(KT - 1)

    def feed_direct(sp, d0, d1):
        for d in range(d0, d1):
            if d >= 2:
                sp.wait_ge(direct_mult, d // 2)
            sp.dma_start(direct[d % 2][:], dram["w_cmp"][d]).then_inc(direct_landed[d % 2], 16)

    def dve_mods(dve, step, l):
        dve.wait_ge(ada_folded, sum(pr.n for pr in products if pr.ada is not None and (l == 1 or pr.tokens == S)))
        nt = N_MOD * KT
        bias = vcol("b_ada", nt * l, nt).unsqueeze(2).to_broadcast([P, nt, 2])
        step(nc.vector.tensor_tensor(mod[:, l], ps[6][:, 2 * nt * l:2 * nt * (l + 1)]
                                     .rearrange("p (j w) -> p j w", w=2), bias, ALU.add))
        for n in range(3):
            g = vcol("norm_g", (3 * l + n) * KT, KT).unsqueeze(2).to_broadcast([P, KT, 2])
            j = (3 * n + 1) * KT
            last = nc.vector.scalar_tensor_tensor(gmod[:, l, n], mod[:, l, j:j + KT, :], 1.0, g, ALU.add, ALU.mult)
        for i, j in enumerate((2, 8)):
            last = nc.vector.tensor_scalar(half_gate[:, l, i], mod[:, l, j * KT:(j + 1) * KT, :], 0.5, None,
                                           ALU.mult)
        step(last)

    def temp(name, shape, off, dt=F32):
        return place(name, shape, dt, off)

    K1 = 1024
    ar = temp("ar", [P, 4, 2, S], at_a)
    bt = temp("bt", [P, 4, S], at_a + 8 * K1)
    kt_ = temp("kt_", [P, 4, S], at_a + 12 * K1)
    a_tok = temp("a_tok", [P, 2, 512], at_a + 16 * K1)
    b_tok = temp("b_tok", [P, 2, 512], at_a + 20 * K1)
    k_tok = temp("k_tok", [P, 2, 512], at_a + 24 * K1)
    v_tok = temp("v_tok", [P, 2, 512], at_a + 28 * K1)
    t2b = temp("t2b", [P, 2, 2, S], at_a)
    xf = temp("xf", [P, 2, 16, 2 * NCMP], at_a + 16 * K1)
    hc = place("hc", [P, 4, 2 * NCMP], F32)
    kc = place("kc", [P, 2 * NCMP], F32)
    vct = place("vct", [P, 2, HD], F32)
    at_rope = cursor[0]
    cos1 = place("cos1", [P, S], F32)
    sin1 = place("sin1", [P, S], F32)
    pos_i = place("pos_i", [P, S], I32)
    rows10 = place("rows10", [P, 5 * P], F32, at_rope)
    def slot4(name, i, shape=(P, 4, S)):
        return temp(name, list(shape), at_w + 4 * K1 * i)
    dsh = temp("dsh", [P, 15, S], at_w)
    sig = slot4("sig", 0)
    cum = slot4("cum", 1)
    ei = slot4("ei", 2)
    em = slot4("em", 3)
    aa = slot4("aa", 4)
    kk = slot4("kk", 5)
    kr = slot4("kr", 6)
    km = slot4("km", 7)
    rin = slot4("rin", 8)
    bb = slot4("bb", 9)
    tmp2 = slot4("tmp2", 10)
    el = slot4("el", 11)
    th = temp("th", [P, 4, S], at_w + 32 * K1)
    def slot2(name, i, shape=(P, 4, P)):
        return temp(name, list(shape), at_w + 2 * K1 * i)
    a16 = slot2("a16", 0)
    a16t = slot2("a16t", 1)
    aoff = slot2("aoff", 2)
    ak = slot2("ak", 3)
    pw2 = slot2("pw2", 4)
    pw2t = slot2("pw2t", 5)
    pw4 = slot2("pw4", 6)
    pw4t = slot2("pw4t", 7)
    pw8t = slot2("pw8t", 8)
    tinv = slot2("tinv", 9)
    w1t = slot2("w1t", 10, (P, 256))
    rb = temp("rb", [P, 8, P], at_w + 22 * K1)
    rk = temp("rk", [P, 8, P], at_w + 26 * K1)
    pp = temp("pp", [P, 4, P], at_w + 30 * K1)
    qq = temp("qq", [P, 512], at_w + 32 * K1)
    ut = temp("ut", [P, 512], at_w + 34 * K1)
    st = [temp(f"st{i}", [P, 4, P], at_w + (36 + 2 * i) * K1) for i in range(3)]
    qn = temp("qn", [P, T2], at_f + 30 * K1)
    ysq = temp("ysq", [P, 4, S], at_w + 24 * K1)
    ysd = temp("ysd", [P, 4, S], at_w + 28 * K1)
    ss = [temp(f"ss{i}", [P, 512], at_w + 2 * K1 * i) for i in range(2)]
    ee = [temp(f"ee{i}", [P, 512], at_w + (4 + 2 * i) * K1) for i in range(3)]
    pt = [temp(f"pt{i}", [P, 512], at_w + (10 + 2 * i) * K1) for i in range(2)]
    prep = temp("prep", [P, 5, T2], at_w)
    vt = temp("vt", [P, 3, 4, P], at_w + 14 * K1)
    ksw = temp("ksw", [P, 2, T2], at_w + 20 * K1)
    nb = temp("nb", [P, 4, 2, S], at_w + 24 * K1)
    pu = [temp(f"pu{i}", [P, 2, S + 32], at_w + 32 * K1 + 2304 * i) for i in range(5)]
    yp = temp("yp", [P, 2, S], at_w + 44 * K1)
    yp2 = temp("yp2", [P, 2, S], at_w + 46 * K1)
    nbt = temp("nbt", [P, 8, HD], at_f + 28 * K1)
    gt = temp("gt", [P, 2, 24], at_w + 32 * K1)
    sgt = temp("sgt", [P, S], at_w + 33 * K1)
    cs = temp("cs", [P, 16, NCMP], at_w + 34 * K1)
    cst = temp("cst", [P, 8, 2, P], at_w + 36 * K1)
    cmx = temp("cmx", [P, 16], at_w + 46 * K1)
    csum = temp("csum", [P, 16], at_w + 46 * K1 + 64)
    cfac = temp("cfac", [P, 16], at_w + 46 * K1 + 128)
    NJ = 24
    mx = place("mx", [P, 2 * NJ, 2], F32)
    nm = place("nm", [P, 2 * NJ, 2], F32)
    sm = place("sm", [P, 2 * NJ, 2], F32)
    fac = place("fac", [P, 2 * NJ, 2], F32)

    def half_tiles(t, m):
        return ps[t + m // 2][:, (m % 2) * S:(m % 2) * S + S]

    def bc(ap, n):
        return ap.unsqueeze(1).to_broadcast([ap.shape[0], n, ap.shape[1]])

    pos_loaded = sem("pos_loaded")
    angle_ready = sem("angle_ready")
    sines_ready = sem("sines_ready")
    TWO_PI_HI, TWO_PI_MID = 6.28125, 2029.0 / 2 ** 20
    TWO_PI_LO = 2 * math.pi - TWO_PI_HI - TWO_PI_MID
    MAGIC = 1.5 * 2 ** 23

    def dve_tables(dve, step):
        dve.wait_ge(pos_loaded, 16)
        step(nc.vector.tensor_copy(cos1[:], pos_i[:]))
        step(nc.vector.tensor_scalar(cos1[:], cos1[:], con("freq"), None, ALU.mult))
        step(nc.vector.tensor_scalar(sin1[:], cos1[:], 1.0 / (2 * math.pi), MAGIC, ALU.mult, ALU.add))
        step(nc.vector.tensor_scalar(sin1[:], sin1[:], MAGIC, None, ALU.subtract))
        for part in (TWO_PI_HI, TWO_PI_MID, TWO_PI_LO):
            step(nc.vector.scalar_tensor_tensor(cos1[:], sin1[:], -part, cos1[:], ALU.mult, ALU.add))
        nc.vector.tensor_scalar(cos1[:], cos1[:], 3.1415925, -3.1415925, ALU.min, ALU.max).then_inc(angle_ready, 1)
        dve.wait_ge(sines_ready, 2)
        step(nc.vector.tensor_tensor(cos1[:], rt[:, 0:S], rt[:, 0:S], ALU.mult))
        step(nc.vector.tensor_scalar(cos1[:], cos1[:], -2.0, 1.0, ALU.mult, ALU.add))

    def act_tables(act):
        act.wait_ge(angle_ready, 1)
        nc.scalar.activation(sin1[:], cos1[:], ACT.Sin).then_inc(sines_ready, 1)
        nc.scalar.activation(rt[:, 0:S], cos1[:], ACT.Sin, scale=0.5).then_inc(sines_ready, 1)

    x_ready = sem("x_ready")
    hc_ready = sem("hc_ready")
    kc_mult = sem("kc_mult")

    def dve_cmp(dve, step):
        for kv in range(2):
            for g in range(2):
                src = p1[g * HD:(g + 1) * HD, 18 + kv, :]
                nc.vector.tensor_copy(t2b[0:HD, kv, g, :], src)
                last = nc.vector.tensor_copy(t2b[HD:P, kv, g, 0:S - 1], src[:, 1:S])
        step(last)
        for kv in range(2):
            pe_cols = vcol("pe_v" if kv else "pe_k", 0, 16)
            for g in range(2):
                v = t2b[:, kv, g, :].rearrange("p (n s) -> p n s", s=16)
                for hf in range(2):
                    src = v[:, hf:hf + NCMP, 0:16:2].rearrange("p n j -> p j n")
                    b = pe_cols[:, 8 * hf:8 * hf + 8].unsqueeze(2).to_broadcast([P, 8, NCMP])
                    last = nc.vector.tensor_tensor(xf[:, kv, 8 * hf:8 * hf + 8, g * NCMP:(g + 1) * NCMP], src, b,
                                                   ALU.add)
        last.then_inc(x_ready, 1)

    def dve_cmp_out(dve):
        dve.wait_ge(kc_mult, 1)
        nc.vector.tensor_copy(kc[:], ps[7][:, P:P + 2 * NCMP])
        nc.vector.tensor_copy(vct[0:NCMP], ps[7][0:NCMP, 2 * P:3 * P].rearrange("p (g d) -> p g d", g=2))

    def act_cmp(act):
        act.wait_ge(direct_mult, 2)
        for kv in range(2):
            for m in range(2):
                last = nc.scalar.activation(hc[:, 2 * kv + m, :], cmp_bank(kv, m), ACT.Silu,
                                            bias=vcol("bv1" if kv else "bk1", m))
        last.then_inc(hc_ready, 1)

    def cmp_bank(kv, m):
        n = 2 * kv + m
        return ps[7][:, n * 2 * NCMP:(n + 1) * 2 * NCMP]

    def pe_cmp(pe, kv):
        pe.wait_ge(x_ready, 1)
        for hf in range(2):
            pe.wait_ge(direct_landed[hf], 16 * (kv + 1))
        for m in range(2):
            for hf in range(2):
                for k in range(KT):
                    o = k * 2 * P + m * P
                    last = nc.tensor.matmul(cmp_bank(kv, m), direct[hf][:, o:o + P], xf[:, kv, 8 * hf + k, :],
                                            start=hf == 0 and k == 0, stop=hf == 1 and k == KT - 1)
        last.then_inc(direct_mult, 1)

    def pe_cmp_out(pe):
        pe.wait_ge(hc_ready, 1)
        for m in range(2):
            nc.tensor.matmul(ps[7][:, P:P + 2 * NCMP], mats[:, M_CK2 + m * P:M_CK2 + (m + 1) * P], hc[:, m, :],
                             start=m == 0, stop=m == 1)
        for g in range(2):
            for m in range(2):
                last = nc.tensor.matmul(ps[7][0:NCMP, 2 * P + g * HD:2 * P + (g + 1) * HD],
                                        hc[:, 2 + m, g * NCMP:(g + 1) * NCMP],
                                        mats[:, M_CV2 + m * HD:M_CV2 + (m + 1) * HD], start=m == 0, stop=m == 1)
        last.then_inc(kc_mult, 1)

    rw_dve = sem("rw_dve")
    rw_act = sem("rw_act")
    rw_pe = sem("rw_pe")
    GR = range(4)
    RD = counts(["shift", "cum", "kr", "brk", "tokin"] + [f"tok{e}" for e in (1, 3, 5, 7)] + ["bonus"]
                + [n for t in range(2) for n in
                   [f"{n}.{2 * t + q}" for q in range(2) for n in
                    ("gram", "t0", "pw2t", "t1", "t2", "td", "n2t", "x1", "tinv", "qv")]
                   + [f"{n}.{2 * t + c}" for c in range(2) for n in ("u", "s")] + [f"y.{t}"]]
                + ["yc", "yout"])
    RA = counts(["lat", "sigw", "aa", "exps", "krsq", "kksqrt", "gcopy"] + [f"tok{e}" for e in (0, 2, 4, 6)]
                + [f"{n}.{g}" for g in GR for n in ("w1", "pw2", "pw4", "pw4t", "pw8t", "tdt", "n", "nt", "p")]
                + ["ysq", "ysd"])
    RP = counts(["zw", "za", "g", "kkss", "bonus"] + [f"tok{e}" for e in range(8)]
                + [n for t in range(2) for n in
                   [f"{n}.{2 * t + q}" for q in range(2) for n in
                    ("gram", "w1", "pw2", "pw2t", "pw4", "pw4t", "t1", "pw8t", "t2", "td", "tdt", "n", "nt", "n2t",
                     "x1", "tinv", "p", "qv")]
                   + [f"{n}.{2 * t + c}" for c in range(2) for n in ("u", "s")] + [f"y.{t}"]]
                + ["ymean", "yvar"])
    TOKB = (0, 1, 7)
    YB = (5, 7)
    r_t, k_t, v_t = p1[:, 0:4, :], p1[:, 4:8, :], p1[:, 8:12, :]

    def flat(ap):
        return ap.rearrange("p a b -> p (a b)")

    def heads_of(par):
        return slice(par, 4, 2)

    def dve_rwkv(dve, step):
        V = nc.vector
        V.tensor_tensor(dsh[:, 0:14, 1:S], p1[:, 0:14, 0:S - 1], p1[:, 0:14, 1:S], ALU.subtract)
        V.tensor_scalar(dsh[:, 0:14, 0:1], p1[:, 0:14, 0:1], -1.0, None, ALU.mult)
        V.tensor_tensor(dsh[0:32, 14, 1:S], p1[0:32, 24, 0:S - 1], p1[0:32, 24, 1:S], ALU.subtract)
        step(V.tensor_scalar(dsh[0:32, 14, 0:1], p1[0:32, 24, 0:1], -1.0, None, ALU.mult))
        for m in (12, 13, 0, 1, 2, 3, 4, 5, 6, 7, 8, 9, 10, 11):
            V.scalar_tensor_tensor(p1[:, m, :], dsh[:, m, :], vcol("mu", m), p1[:, m, :], ALU.mult, ALU.add)
        V.scalar_tensor_tensor(p1[0:32, 24, :], dsh[0:32, 14, :], vcol("mu", 14, rows=slice(0, 32)), p1[0:32, 24, :],
                               ALU.mult, ALU.add).then_inc(rw_dve, 1)
        dve.wait_ge(rw_dve, RD["shift"])
        dve.wait_ge(rw_act, RA["sigw"])
        for m in range(4):
            last = V.tensor_tensor_scan(cum[:, m, :], con("scan0"), sig[:, m, :], 0.0, ALU.mult, ALU.add)
        step(last)
        V.tensor_tensor(em[:], cum[:], sig[:], ALU.subtract).then_inc(rw_dve, 1)
        for m in range(4):
            last = V.tensor_scalar(kr[:, m, :], k_t[:, m, :], vcol("k_k", m), None, ALU.mult)
        last.then_inc(rw_dve, 1)
        dve.wait_ge(rw_act, RA["aa"])
        for m in range(4):
            last = V.tensor_scalar(tmp2[:, m, :], aa[:, m, :], 1.0, vcol("k_a", m), ALU.subtract, ALU.mult)
        step(last)
        step(V.scalar_tensor_tensor(km[:], tmp2[:], 1.0, k_t, ALU.add, ALU.mult))
        dve.wait_ge(rw_act, RA["kksqrt"])
        step(V.tensor_scalar(rin[:], rin[:], 1e-12, None, ALU.max))
        step(V.reciprocal(rin[:], rin[:]))
        step(V.tensor_tensor(kk[:], kr[:], rin[:], ALU.mult))
        for m in range(4):
            last = V.scalar_tensor_tensor(kr[:, m, :], r_t[:, m, :], vcol("r_k", m), km[:, m, :], ALU.mult, ALU.mult)
        last.then_inc(rw_dve, 1)
        step(V.tensor_tensor(bb[:], kk[:], aa[:], ALU.mult))
        V.scalar_tensor_tensor(ar[:, :, 0, :], kk[:], -1.0, em[:], ALU.mult, ALU.mult)
        V.tensor_tensor(ar[:, :, 1, :], r_t, el[:], ALU.mult)
        V.tensor_tensor(bt[:], bb[:], ei[:], ALU.mult)
        step(V.tensor_tensor(kt_[:], km[:], ei[:], ALU.mult))
        dve_cmp_out(dve)
        for m in range(4):
            end = el[:, m, CHUNK - 1:S:CHUNK].unsqueeze(2).to_broadcast([P, S // CHUNK, CHUNK])
            V.tensor_tensor(kk[:, m, :].rearrange("p (c t) -> p c t", t=CHUNK),
                            bt[:, m, :].rearrange("p (c t) -> p c t", t=CHUNK), end, ALU.mult)
            last = V.tensor_tensor(aa[:, m, :].rearrange("p (c t) -> p c t", t=CHUNK),
                                   kt_[:, m, :].rearrange("p (c t) -> p c t", t=CHUNK), end, ALU.mult)
        last.then_inc(rw_dve, 1)
        toks = [(d, i) for d in (v_tok, a_tok, b_tok, k_tok) for i in range(2)]
        for e in (1, 3, 5, 7):
            dve.wait_ge(rw_pe, RP[f"tok{e}"])
            V.tensor_copy(toks[e][0][:, toks[e][1], :], ps[TOKB[e % 3]][:]).then_inc(rw_dve, 1)
        for m in range(2):
            last = V.tensor_tensor(v_t[:, 2 * m:2 * m + 2, :], ps[2 + m][:].rearrange("p (a b) -> p a b", a=2),
                                   v_t[:, 2 * m:2 * m + 2, :], ALU.mult)
        last.then_inc(rw_dve, 1)
        step(V.memset(st[0][:], 0.0))
        for i in range(2):
            for q in range(2):
                g = 2 * i + q
                dve.wait_ge(rw_pe, RP[f"gram.{g}"])
                if g:
                    dve.wait_ge(rw_pe, RP[f"qv.{g - 1}"])
                for par in range(2):
                    b = ps[par][:].rearrange("p (a b) -> p a b", a=2)
                    hs = heads_of(par)
                    gs = slice(4 * q + par, 4 * q + 4, 2)
                    V.tensor_tensor(a16[:, hs, :], b[:, :, 0:P], bc(con("m16"), 2), ALU.mult)
                    V.tensor_tensor(aoff[:, hs, :], b[:, :, 0:P], bc(con("moff"), 2), ALU.mult)
                    V.tensor_tensor(rb[:, gs, :], b[:, :, P:2 * P], bc(con("m_u"), 2), ALU.mult)
                    b = ps[2 + par][:].rearrange("p (a b) -> p a b", a=2)
                    V.tensor_tensor(ak[:, hs, :], b[:, :, 0:P], bc(con("m_su"), 2), ALU.mult)
                    V.tensor_tensor(rk[:, gs, :], b[:, :, P:2 * P], bc(con("m_u"), 2), ALU.mult)
                    b = ps[4 + par][:, 0:2 * P].rearrange("p (a b) -> p a b", a=2)
                    last = V.tensor_tensor(a16t[:, hs, :], b, bc(con("m16t"), 2), ALU.mult)
                last.then_inc(rw_dve, 1)
                dve.wait_ge(rw_dve, RD[f"gram.{g}"])
                V.tensor_tensor(tinv[:], a16[:], bc(con("ident"), 4), ALU.add).then_inc(rw_dve, 1)
                dve.wait_ge(rw_pe, RP[f"pw2t.{g}"])
                V.tensor_copy(flat(pw2t[:]), ps[0][:]).then_inc(rw_dve, 1)
                for n, bk in (("t1", 3), ("t2", 5), ("td", 7)):
                    dve.wait_ge(rw_pe, RP[f"{n}.{g}"])
                    dve.wait_ge(rw_dve, RD[f"{n}.{g}"] - 1)
                    V.tensor_tensor(flat(tinv[:]), ps[bk][:], flat(tinv[:]), ALU.add).then_inc(rw_dve, 1)
                dve.wait_ge(rw_pe, RP[f"n2t.{g}"])
                V.tensor_copy(flat(pw4[:]), ps[3][:]).then_inc(rw_dve, 1)
                for n, bk in (("x1", 4), ("tinv", 5)):
                    dve.wait_ge(rw_pe, RP[f"{n}.{g}"])
                    dve.wait_ge(rw_dve, RD[f"{n}.{g}"] - 1)
                    V.tensor_tensor(flat(tinv[:]), ps[bk][:], flat(tinv[:]), ALU.add).then_inc(rw_dve, 1)
                dve.wait_ge(rw_pe, RP[f"qv.{g}"])
                V.tensor_copy(qq[:, q * 256:(q + 1) * 256], ps[1][:, 0:256]).then_inc(rw_dve, 1)
            dve.wait_ge(rw_dve, RD[f"qv.{2 * i + 1}"])
            for c in range(2):
                s = 2 * i + c
                rows = slice(c * HD, (c + 1) * HD)
                dve.wait_ge(rw_pe, RP[f"u.{s}"])
                V.tensor_tensor(ut[rows, :], ps[2][rows, :], qq[rows, :], ALU.add).then_inc(rw_dve, 1)
                old, new = st[s % 3], st[(s + 1) % 3]
                end = el[:, :, s * CHUNK + CHUNK - 1:s * CHUNK + CHUNK].to_broadcast([P, 4, P])
                step(V.tensor_tensor(new[:], old[:], end, ALU.mult))
                dve.wait_ge(rw_pe, RP[f"s.{s}"])
                step(V.tensor_tensor(a16[:], ps[3][:].rearrange("p (a b) -> p a b", a=4), bc(con("bdmask"), 4),
                                     ALU.mult))
                V.tensor_tensor(new[:], new[:], a16[:], ALU.add).then_inc(rw_dve, 1)
                dve.wait_ge(rw_dve, RD[f"s.{s}"])
            dve.wait_ge(rw_pe, RP[f"y.{i}"])
            for m in range(2):
                last = V.tensor_copy(r_t[:, 2 * m:2 * m + 2, i * P:(i + 1) * P],
                                     ps[4 + m][:, 0:2 * P].rearrange("p (a b) -> p a b", a=2))
            last.then_inc(rw_dve, 1)

    def dve_mean(dve):
        dve.wait_ge(rw_pe, RP["ymean"])
        for m in range(2):
            last = nc.vector.scalar_tensor_tensor(r_t[:, 2 * m:2 * m + 2, :],
                                                  ps[YB[m]][:].rearrange("p (a b) -> p a b", a=2), -1.0 / HD,
                                                  r_t[:, 2 * m:2 * m + 2, :], ALU.mult, ALU.add)
        last.then_inc(rw_dve, 1)

    def dve_out(dve, step):
        V = nc.vector
        dve.wait_ge(rw_act, RA["ysd"])
        step(V.reciprocal(ysd[:], ysd[:]))
        dve.wait_ge(rw_dve, RD["yc"])
        step(V.tensor_tensor(r_t, r_t, ysd[:], ALU.mult))
        for m in range(4):
            last = V.tensor_scalar(r_t[:, m, :], r_t[:, m, :], vcol("lnx_w", m), vcol("lnx_b", m), ALU.mult, ALU.add)
        step(last)
        step(V.tensor_tensor(r_t, r_t, v_t, ALU.add))
        V.tensor_tensor(r_t, r_t, k_t, ALU.mult).then_inc(rw_dve, 1)

    def act_deviation(act):
        act.wait_ge(rw_dve, RD["yc"])
        nc.scalar.activation(ysq[:], r_t, ACT.Square).then_inc(rw_act, 1)
        act.wait_ge(rw_pe, RP["yvar"])
        for m in range(2):
            last = nc.scalar.activation(flat(ysd[:, 2 * m:2 * m + 2, :]), ps[YB[m]][:], ACT.Sqrt, scale=1.0 / HD,
                                        bias=eps[:, 1:2])
        last.then_inc(rw_act, 1)

    def pe_mean(pe):
        for m in range(2):
            last = nc.tensor.matmul(ps[YB[m]][:], con("bd"), flat(r_t[:, 2 * m:2 * m + 2, :]), start=True, stop=True)
        last.then_inc(rw_pe, 1)

    def pe_variance(pe):
        pe.wait_ge(rw_act, RA["ysq"])
        for m in range(2):
            last = nc.tensor.matmul(ps[YB[m]][:], con("bd"), flat(ysq[:, 2 * m:2 * m + 2, :]), start=True, stop=True)
        last.then_inc(rw_pe, 1)

    def act_rwkv(act):
        A = nc.scalar.activation
        act.wait_ge(rw_dve, RD["shift"])
        A(th[0:HD, 0, :], p1[0:HD, 12, :], ACT.Tanh)
        A(th[:, 1, :], p1[:, 13, :], ACT.Sigmoid)
        A(th[0:32, 2, :], p1[0:32, 24, :], ACT.Sigmoid).then_inc(rw_act, 1)
        act.wait_ge(rw_pe, RP["zw"])
        for m in range(4):
            last = A(sig[:, m, :], half_tiles(0, m), ACT.Sigmoid, bias=vcol("w0", m))
        last.then_inc(rw_act, 1)
        act.wait_ge(rw_pe, RP["za"])
        for m in range(4):
            last = A(aa[:, m, :], half_tiles(2, m), ACT.Sigmoid, bias=vcol("a0", m))
        last.then_inc(rw_act, 1)
        act.wait_ge(rw_dve, RD["cum"])
        A(el[:], cum[:], ACT.Exp, scale=-DECAY)
        A(ei[:], cum[:], ACT.Exp, scale=DECAY)
        A(em[:], em[:], ACT.Exp, scale=-DECAY).then_inc(rw_act, 1)
        act.wait_ge(rw_pe, RP["g"])
        act.wait_ge(rw_dve, RD["kr"])
        A(rin[:], kr[:], ACT.Square).then_inc(rw_act, 1)
        act.wait_ge(rw_pe, RP["kkss"])
        for m in range(2):
            last = A(flat(rin[:, 2 * m:2 * m + 2, :]), ps[m][:], ACT.Sqrt)
        last.then_inc(rw_act, 1)
        act_cmp(act)
        act.wait_ge(rw_dve, RD["tokin"])
        for m in range(2):
            last = A(flat(k_t[:, 2 * m:2 * m + 2, :]), ps[4 + m][:], ACT.Copy)
        last.then_inc(rw_act, 1)
        toks = [(d, i) for d in (v_tok, a_tok, b_tok, k_tok) for i in range(2)]
        for e in (0, 2, 4, 6):
            act.wait_ge(rw_pe, RP[f"tok{e}"])
            A(toks[e][0][:, toks[e][1], :], ps[TOKB[e % 3]][:], ACT.Copy).then_inc(rw_act, 1)
        for g in GR:
            for n, dst, bk in (("w1", w1t, 3), ("pw2", pw2, 7), ("pw4", pw4, 1), ("pw4t", pw4t, 2), ("pw8t", pw8t, 4),
                               ("tdt", a16t, 0), ("n", pw2, 1), ("nt", pw2t, 2), ("p", pp, 0)):
                act.wait_ge(rw_pe, RP[f"{n}.{g}"])
                if n == "w1":
                    A(w1t[:], ps[bk][:, 0:256], ACT.Copy).then_inc(rw_act, 1)
                elif n == "p":
                    q = g % 2
                    A(flat(pp[:, 2 * q:2 * q + 2, :]), ps[0][:, 0:256], ACT.Copy).then_inc(rw_act, 1)
                else:
                    A(flat(dst[:]), ps[bk][:], ACT.Copy).then_inc(rw_act, 1)

    def pe_rwkv(pe):
        M = nc.tensor.matmul
        T = nc.tensor.transpose
        ident = con("ident")
        pe_cmp(pe, 0)
        pe.wait_ge(rw_dve, RD["shift"])
        pe.wait_ge(rw_act, RA["lat"])
        for m in range(4):
            w = mats[0:HD, M_LORA + m * P:M_LORA + (m + 1) * P]
            last = M(half_tiles(0, m), w, th[0:HD, 0, :], start=True, stop=True)
        last.then_inc(rw_pe, 1)
        for m in range(4):
            w = mats[HD:P, M_LORA + m * P:M_LORA + (m + 1) * P]
            last = M(half_tiles(2, m), w, p1[HD:P, 12, :], start=True, stop=True)
        last.then_inc(rw_pe, 1)
        for m in range(4):
            M(half_tiles(4, m), mats[:, M_G2 + m * P:M_G2 + (m + 1) * P], th[:, 1, :], start=True, stop=False)
            last = M(half_tiles(4, m), mats[0:32, M_G2T + m * P:M_G2T + (m + 1) * P], th[0:32, 2, :],
                     start=False, stop=True)
        last.then_inc(rw_pe, 1)
        pe.wait_ge(rw_act, RA["krsq"])
        for m in range(2):
            last = M(ps[m][:], con("bd"), flat(rin[:, 2 * m:2 * m + 2, :]), start=True, stop=True)
        last.then_inc(rw_pe, 1)
        pe_cmp(pe, 1)
        pe_cmp_out(pe)
        pe.wait_ge(rw_dve, RD["brk"])
        for m in range(2):
            last = M(ps[2 + m][:], con("bd"), flat(kr[:, 2 * m:2 * m + 2, :]), start=True, stop=True)
        last.then_inc(rw_pe, 1)
        pe.wait_ge(rw_dve, RD["tokin"])
        pe.wait_ge(rw_act, RA["kksqrt"])
        e = 0
        for src in (v_t, ar[:, :, 0, :], kk[:], aa[:]):
            for i in range(2):
                if e >= 3:
                    pe.wait_ge(rw_dve if (e - 3) % 2 else rw_act, (RD if (e - 3) % 2 else RA)[f"tok{e - 3}"])
                for m in range(4):
                    last = T(ps[TOKB[e % 3]][:, m * P:(m + 1) * P], src[:, m, i * P:(i + 1) * P], ident)
                last.then_inc(rw_pe, 1)
                e += 1
        pe.wait_ge(rw_dve, RD["bonus"])
        pe.wait_ge(rw_act, RA["tok6"])
        for i in range(2):
            tok = slice(i * P, (i + 1) * P)
            for q in range(2):
                g = 2 * i + q
                if q == 0 and i:
                    pe.wait_ge(rw_dve, RD["y.0"])
                if g:
                    pe.wait_ge(rw_dve, RD[f"qv.{g - 1}"])
                    pe.wait_ge(rw_act, RA[f"p.{g - 1}"])
                for j in range(4):
                    par, ix = j % 2, j // 2
                    rows = slice(par * HD, (par + 1) * HD)
                    m = 2 * q + ix
                    b = ps[par][:, ix * 256:ix * 256 + 256].rearrange("p (a b) -> p a b", a=2)
                    M(b, bt[rows, m, tok], ar[rows, m, :, tok], start=True, stop=True)
                    b = ps[2 + par][:, ix * 256:ix * 256 + 256].rearrange("p (a b) -> p a b", a=2)
                    M(b, kt_[rows, m, tok], ar[rows, m, :, tok], start=True, stop=True)
                    last = M(ps[4 + par][:, ix * P:(ix + 1) * P], ar[rows, m, 0, tok], bt[rows, m, tok],
                             start=True, stop=True)
                last.then_inc(rw_pe, 1)

                def four(bk, lhs, rhs, n=P):
                    for j in range(4):
                        last = M(ps[bk][:, j * n:(j + 1) * n], lhs[:, j, :], rhs(j), start=True, stop=True)
                    last.then_inc(rw_pe, 1)

                pe.wait_ge(rw_dve, RD[f"t0.{g}"])
                four(3, ak, lambda j: v_tok[:, i, (4 * q + j) * HD:(4 * q + j + 1) * HD], HD)
                four(7, a16t, lambda j: a16[:, j, :])
                four(0, a16, lambda j: a16t[:, j, :])
                pe.wait_ge(rw_dve, RD[f"pw2t.{g}"])
                pe.wait_ge(rw_act, RA[f"pw2.{g}"])
                four(1, pw2t, lambda j: pw2[:, j, :])
                four(2, pw2, lambda j: pw2t[:, j, :])
                pe.wait_ge(rw_act, RA[f"w1.{g}"])
                four(3, pw2t, lambda j: tinv[:, j, :])
                pe.wait_ge(rw_act, RA[f"pw4t.{g}"])
                four(4, pw4, lambda j: pw4t[:, j, :])
                pe.wait_ge(rw_dve, RD[f"t1.{g}"])
                four(5, pw4t, lambda j: tinv[:, j, :])
                pe.wait_ge(rw_act, RA[f"pw8t.{g}"])
                pe.wait_ge(rw_dve, RD[f"t2.{g}"])
                four(7, pw8t, lambda j: tinv[:, j, :])
                pe.wait_ge(rw_dve, RD[f"td.{g}"])
                for j in range(4):
                    last = T(ps[0][:, j * P:(j + 1) * P], tinv[:, j, :], ident)
                last.then_inc(rw_pe, 1)
                pe.wait_ge(rw_act, RA[f"tdt.{g}"])
                four(1, a16t, lambda j: aoff[:, j, :])
                four(2, aoff, lambda j: a16t[:, j, :])
                pe.wait_ge(rw_act, RA[f"nt.{g}"])
                four(3, pw2, lambda j: pw2t[:, j, :])
                pe.wait_ge(rw_dve, RD[f"n2t.{g}"])
                four(4, pw4, lambda j: tinv[:, j, :])
                pe.wait_ge(rw_dve, RD[f"x1.{g}"])
                four(5, pw2t, lambda j: tinv[:, j, :])
                pe.wait_ge(rw_dve, RD[f"tinv.{g}"])
                for j in range(4):
                    par, ix = j % 2, j // 2
                    last = M(ps[0][par * HD:(par + 1) * HD, ix * P:(ix + 1) * P],
                             a_tok[:, i, (4 * q + j) * HD:(4 * q + j + 1) * HD], tinv[:, j, :], start=True, stop=True)
                last.then_inc(rw_pe, 1)
                for j in range(4):
                    last = M(ps[1][:, j * HD:(j + 1) * HD], tinv[:, j, :], w1t[:, j * HD:(j + 1) * HD],
                             start=True, stop=True)
                last.then_inc(rw_pe, 1)
            pe.wait_ge(rw_act, RA[f"p.{2 * i + 1}"])
            for c in range(2):
                s = 2 * i + c
                rows = slice(c * HD, (c + 1) * HD)
                pe.wait_ge(rw_dve, RD[f"u.{s}"] - 1)
                for m in range(4):
                    last = M(ps[2][rows, m * P:(m + 1) * P], pp[:, m, c * HD:(c + 1) * HD], st[s % 3][:, m, :],
                             start=True, stop=True)
                last.then_inc(rw_pe, 1)
                pe.wait_ge(rw_dve, RD[f"u.{s}"])
                for m in range(4):
                    cols = slice(m * P, (m + 1) * P)
                    M(ps[3][:, cols], b_tok[rows, i, cols], ut[rows, cols], start=True, stop=False)
                    last = M(ps[3][:, cols], k_tok[rows, i, cols], v_tok[rows, i, cols], start=False, stop=True)
                last.then_inc(rw_pe, 1)
            for m in range(4):
                o = ps[4 + m // 2]
                for par in range(2):
                    hh = 2 * m + par
                    dst = o[par * HD:(par + 1) * HD, (m % 2) * P:(m % 2) * P + P]
                    hc_ = slice(hh * HD, (hh + 1) * HD)
                    M(dst, v_tok[:, i, hc_], rk[:, hh, :], start=True, stop=False, skip_group_check=True)
                    M(dst, ut[:, hc_], rb[:, hh, :], start=False, stop=False, skip_group_check=True)
                for c in range(2):
                    col = (m % 2) * P + c * HD
                    t0 = i * P + c * CHUNK
                    last = M(o[:, col:col + HD], st[(2 * i + c) % 3][:, m, :], ar[:, m, 1, t0:t0 + CHUNK],
                             start=False, stop=True, skip_group_check=True)
            last.then_inc(rw_pe, 1)

    at_scores = sem("at_scores")
    at_max = sem("at_max")
    at_exp = sem("at_exp")
    at_norm = sem("at_norm")
    at_trans = sem("at_trans")
    at_pt = sem("at_pt")
    at_pv = sem("at_pv")
    at_ohi = sem("at_ohi")
    at_olo = sem("at_olo")
    pr_dve = sem("pr_dve")
    pr_act = sem("pr_act")
    pr_pe = sem("pr_pe")
    pool_step = sem("pool_step")
    pool_ready = sem("pool_ready")
    nb_loaded = sem("nb_loaded")
    rows_loaded = sem("rows_loaded")

    class Job:
        pass

    def jobs_first():
        out_ = []
        for hh in range(8):
            for i in range(2):
                j = Job()
                par, g, n = hh % 2, hh // 4, P * (i + 1)
                rows = slice(par * HD, (par + 1) * HD)
                j.q = p1[rows, 14 + hh // 2, i * P:(i + 1) * P]
                j.keys = [((p1[rows, 20 + 2 * b, 0:n] if par == g else ksw[rows, b, 0:n]), b * S, n) for b in range(2)]
                j.segs, j.seg, j.width = 2, S, n
                j.masks = [(con("causal", P if i == 0 else 0), n)]
                j.scaled = True
                j.gates = gt[:, i, 3 * hh + 1:3 * hh + 3]
                j.values = [(vt[:, b, k, g * HD:(g + 1) * HD], b * S + k * P) for b in range(2) for k in range(i + 1)]
                j.cmp = (vct[0:NCMP, g, :], cst[0:NCMP, hh, i, :])
                j.rows, j.col, j.tile, j.tok = rows, i * P, 4 + hh // 2, 0
                out_.append(j)
        return out_

    def jobs_second(l):
        out_ = []
        for w in range(2 if l == 0 else 1):
            for hh in range(12):
                for i in range(2):
                    j = Job()
                    na = hh < 4
                    hq = hh if na else hh - 4
                    par = hq % 2
                    rows = slice(par * HD, (par + 1) * HD)
                    k0, n = (0, T2) if w == 0 else (S, S)
                    g = hq // 4
                    j.q = p2[rows, (0 if na else 8) + hq // 2, w * S + i * P:w * S + (i + 1) * P]
                    if na:
                        key = p2[rows, 2 + hq // 2, k0:k0 + n]
                    else:
                        key = p2[rows, 12, k0:k0 + n] if par == g else ksw[rows, 0, k0:k0 + n]
                    j.keys = [(key, 0, n)]
                    j.segs, j.seg, j.width = 1, n, n
                    j.scaled = na and w == 0
                    j.masks = [(nb[:, hq, i, :], S)] if j.scaled else []
                    j.gates = None
                    v, d = (hq // 2, par) if na else (2, g)
                    j.values = [(vt[:, v, (k0 // P) + k, d * HD:(d + 1) * HD], k * P) for k in range(n // P)]
                    j.cmp = None
                    j.rows, j.col, j.tok = rows, i * P, w * S
                    j.tile = hq // 2 if na else 4 + hq // 2
                    out_.append(j)
        return out_

    SB, TB, OB = (0, 1, 2), (3, 4), (5, 7)
    stages = [("first", jobs_first(), 0)]
    for l in range(LAYERS):
        stages.append((l, jobs_second(l), stages[-1][2] + len(stages[-1][1])))
    stage_of = {s[0]: s for s in stages}

    def pe_attend(pe, key):
        _, jobs, j0 = stage_of[key]

        def scores(j, x):
            wait(pe, at_exp, j - 2)
            for kx, off, n in x.keys:
                last = nc.tensor.matmul(ps[SB[j % 3]][:, off:off + n], x.q, kx, start=True, stop=True)
            last.then_inc(at_scores, 1)

        def turn(j, x):
            pe.wait_ge(at_norm, j + 1)
            wait(pe, at_pt, j - 1)
            for _, off in x.values:
                last = nc.tensor.transpose(ps[TB[j % 2]][:, off:off + P], ee[j % 3][:, off:off + P], con("ident"))
            last.then_inc(at_trans, 1)

        def pv(j, x):
            pair = j // 4
            pe.wait_ge(at_pt, j + 1)
            if j % 4 == 0:
                wait(pe, at_olo, pair - 1)
            o = ps[OB[pair % 2]][x.rows, x.col:x.col + P]
            for n, (v, off) in enumerate(x.values):
                last = nc.tensor.matmul(o, v, pt[j % 2][:, off:off + P], start=n == 0,
                                        stop=x.cmp is None and n == len(x.values) - 1)
            if x.cmp is not None:
                last = nc.tensor.matmul(o, x.cmp[0], x.cmp[1], start=False, stop=True)
            last.then_inc(at_pv, 1)

        n = len(jobs)
        for t in range(n + 3):
            if t < n:
                scores(j0 + t, jobs[t])
            if 2 <= t < n + 2:
                turn(j0 + t - 2, jobs[t - 2])
            if t >= 3:
                pv(j0 + t - 3, jobs[t - 3])

    def act_attend(act, key):
        _, jobs, j0 = stage_of[key]
        n = len(jobs)
        for t in range(n + 7):
            if t < n:
                j, x = j0 + t, jobs[t]
                act.wait_ge(at_max, j + 1)
                wait(act, at_trans, j - 2)
                for s in range(x.segs):
                    c = slice(s * S, s * S + x.width)
                    src = (ss[j % 2] if x.scaled else ps[SB[j % 3]])[:, c]
                    last = nc.scalar.activation(ee[j % 3][:, c], src, ACT.Exp, bias=nm[:, t, s:s + 1],
                                                scale=1.0 if x.scaled else SCALE, accum_out=sm[:, t, s:s + 1])
                last.then_inc(at_exp, 1)
            if 2 <= t < n + 2:
                j, x = j0 + t - 2, jobs[t - 2]
                act.wait_ge(at_trans, j + 1)
                wait(act, at_pv, j - 1)
                src, dst = ps[TB[j % 2]], pt[j % 2]
                for s in range(x.segs):
                    c = slice(s * S, s * S + x.width)
                    last = nc.scalar.activation(dst[:, c], src[:, c], ACT.Copy)
                last.then_inc(at_pt, 1)
            if 6 <= t < n + 6 and (t - 6) % 4 == 0:
                pair, x = (j0 + t - 6) // 4, jobs[t - 6]
                act.wait_ge(at_pv, j0 + t - 2)
                nc.scalar.activation(a_hi[:, x.tile, x.tok:x.tok + S], ps[OB[pair % 2]][:, 0:S],
                                     ACT.Copy).then_inc(at_ohi, 1)

    def dve_attend(dve, key, step):
        _, jobs, j0 = stage_of[key]
        n = len(jobs)
        for t in range(n + 7):
            if t < n:
                j, x = j0 + t, jobs[t]
                dve.wait_ge(at_scores, j + 1)
                b = ps[SB[j % 3]]
                if x.scaled:
                    wait(dve, at_exp, j - 1)
                    src = ss[j % 2]
                    mask, w = x.masks[0]
                    if x.segs == 2:
                        dst = src[:].rearrange("p (b c) -> p b c", b=2)[:, :, 0:w]
                        step(nc.vector.scalar_tensor_tensor(
                            dst, b[:].rearrange("p (b c) -> p b c", b=2)[:, :, 0:w], SCALE,
                            bc(mask[:, 0:w], 2), ALU.mult, ALU.add))
                    else:
                        flip = mask.rearrange("p (r c) -> p r c", c=64)
                        nc.vector.scalar_tensor_tensor(src[:, 0:w].rearrange("p (r c) -> p r c", c=64),
                                                       b[:, 0:w].rearrange("p (r c) -> p r c", c=64), SCALE,
                                                       flip, ALU.mult, ALU.add)
                        step(nc.vector.tensor_scalar(src[:, w:T2], b[:, w:T2], SCALE, None, ALU.mult))
                else:
                    src = b
                view = src[:].rearrange("p (b c) -> p b c", b=2)[:, :, 0:x.width] if x.segs == 2 else src[:, 0:x.width]
                step(nc.vector.tensor_reduce(mx[:, t, 0:x.segs], view, AX_X, ALU.max))
                nc.vector.tensor_scalar(nm[:, t, 0:x.segs], mx[:, t, 0:x.segs], -1.0 if x.scaled else -SCALE, None,
                                        ALU.mult).then_inc(at_max, 1)
            if 1 <= t < n + 1:
                j, x = j0 + t - 1, jobs[t - 1]
                u = t - 1
                dve.wait_ge(at_exp, j + 1)
                step(nc.vector.reciprocal(fac[:, u, 0:x.segs], sm[:, u, 0:x.segs]))
                if x.gates is not None:
                    step(nc.vector.tensor_tensor(fac[:, u, :], fac[:, u, :], x.gates, ALU.mult))
                for s in range(x.segs):
                    c = slice(s * S, s * S + x.width)
                    last = nc.vector.tensor_scalar(ee[j % 3][:, c], ee[j % 3][:, c], fac[:, u, s:s + 1], None,
                                                   ALU.mult)
                last.then_inc(at_norm, 1)
            if 6 <= t < n + 6 and (t - 6) % 4 == 0:
                pair, x = (j0 + t - 6) // 4, jobs[t - 6]
                dve.wait_ge(at_ohi, pair + 1)
                c = slice(x.tok, x.tok + S)
                nc.vector.tensor_tensor(a_lo[:, x.tile, c], ps[OB[pair % 2]][:, 0:S],
                                        a_hi[:, x.tile, c].bitcast(F32), ALU.subtract).then_inc(at_olo, 1)

    PD = counts(["rot", "ksw", "vt", "cmax", "cnorm", "cst0", "cst1", "cst2", "cst3"])
    PA = counts(["gate", "gt", "cexp", "rhi"])
    PP = counts(["rot", "krot", "vt", "gt", "cs", "ct0", "ct1", "ct2", "ct3"])
    ROT = (14, 16, 20, 22)

    def pe_first(pe):
        pe_mean(pe)
        for e, t in enumerate(ROT):
            last = nc.tensor.matmul(ps[e][:], con("rot1"), flat(p1[:, t:t + 2, :]), start=True, stop=True)
        last.then_inc(pr_pe, 1)
        nc.tensor.matmul(ps[4][:, 0:2 * NCMP], con("rot1"), kc[:], start=True, stop=True).then_inc(pr_pe, 1)
        pe_variance(pe)
        pe.wait_ge(rw_act, RA["ysd"])
        pe.wait_ge(pr_dve, PD["ksw"])
        for b in range(2):
            for i in range(2):
                o = (2 * b + i) * P
                last = nc.tensor.transpose(ps[5][:, o:o + P], p1[:, 21 + 2 * b, i * P:(i + 1) * P], con("ident"))
        last.then_inc(pr_pe, 1)
        pe.wait_ge(pr_act, PA["gate"])
        for i in range(2):
            last = nc.tensor.transpose(ps[0][:, i * 24:(i + 1) * 24], sgt[0:24, i * P:(i + 1) * P],
                                       consts[0:24, CAT["ident"][0]:CAT["ident"][0] + 24])
        last.then_inc(pr_pe, 1)
        for hh in range(8):
            par, g = hh % 2, hh // 4
            rows = slice(par * HD, (par + 1) * HD)
            for i in range(2):
                o = ((hh // 2) * 2 + i) * NCMP
                last = nc.tensor.matmul(ps[1 + par][:, o:o + NCMP], p1[rows, 14 + hh // 2, i * P:(i + 1) * P],
                                        kc[rows, g * NCMP:(g + 1) * NCMP], start=True, stop=True)
        last.then_inc(pr_pe, 1)
        pe.wait_ge(pr_dve, PD["cnorm"])
        for e in range(4):
            if e >= 2:
                pe.wait_ge(pr_dve, PD[f"cst{e - 2}"])
            for q in range(4):
                n = 4 * e + q
                hh, i = n // 2, n % 2
                last = nc.tensor.transpose(ps[3 + e % 2][0:NCMP, q * P:(q + 1) * P],
                                           cs[:, ((hh % 2) * 4 + hh // 2) * 2 + i, :], con("ident"))
            last.then_inc(pr_pe, 1)

    def act_first(act):
        nc.scalar.activation(sgt[0:24, :], p1[32:56, 24, :], ACT.Sigmoid).then_inc(pr_act, 1)
        act_deviation(act)
        act.wait_ge(pr_pe, PP["gt"])
        nc.scalar.activation(gt[:], ps[0][:, 0:48].rearrange("p (i c) -> p i c", i=2), ACT.Copy).then_inc(pr_act, 1)
        act.wait_ge(pr_dve, PD["cmax"])
        nc.scalar.activation(cs[:], cs[:], ACT.Exp).then_inc(pr_act, 1)
        act.wait_ge(rw_dve, RD["yout"])
        nc.scalar.activation(a_hi[:, 0:4, 0:S], r_t, ACT.Copy).then_inc(pr_act, 1)

    def dve_first(dve, step):
        V = nc.vector
        dve_mean(dve)
        dve.wait_ge(pr_pe, PP["rot"])
        t1 = prep[:, 0, :].rearrange("p (a b) -> p a b", a=2)
        t2 = prep[:, 1, :].rearrange("p (a b) -> p a b", a=2)
        for e, t in enumerate(ROT):
            V.tensor_tensor(t1, p1[:, t:t + 2, :], bc(cos1[:], 2), ALU.mult)
            step(V.tensor_tensor(t2, ps[e][:].rearrange("p (a b) -> p a b", a=2), bc(sin1[:], 2), ALU.mult))
            last = V.tensor_tensor(p1[:, t:t + 2, :], t1, t2, ALU.add)
            if e < 3:
                step(last)
        last.then_inc(pr_dve, 1)
        dve.wait_ge(pr_pe, PP["krot"])
        k3 = kc[:].rearrange("p (g n) -> p g n", g=2)
        u1 = prep[:, 2, 0:2 * NCMP].rearrange("p (g n) -> p g n", g=2)
        u2 = prep[:, 3, 0:2 * NCMP].rearrange("p (g n) -> p g n", g=2)
        V.tensor_tensor(u1, k3, bc(cos1[:, 31:S:16], 2), ALU.mult)
        step(V.tensor_tensor(u2, ps[4][:, 0:2 * NCMP].rearrange("p (g n) -> p g n", g=2),
                             bc(sin1[:, 31:S:16], 2), ALU.mult))
        V.tensor_tensor(k3, u1, u2, ALU.add)
        dve.wait_ge(pr_dve, PD["rot"])
        for b in range(2):
            V.tensor_copy(ksw[0:HD, b, 0:S], p1[HD:P, 20 + 2 * b, :])
            last = V.tensor_copy(ksw[HD:P, b, 0:S], p1[0:HD, 20 + 2 * b, :])
        last.then_inc(pr_dve, 1)
        dve.wait_ge(pr_pe, PP["vt"])
        V.tensor_copy(vt[:, 0:2, 0:2, :], ps[5][:].rearrange("p (b i f) -> p b i f", b=2, i=2)).then_inc(pr_dve, 1)
        dve_out(dve, step)
        dve.wait_ge(pr_pe, PP["cs"])
        c4 = cs[:].rearrange("p (a h i) n -> p a h i n", a=2, i=2)
        for par in range(2):
            for i in range(2):
                m = bc(con("cmp_add", i * NCMP, (i + 1) * NCMP), 4)
                last = V.scalar_tensor_tensor(
                    c4[:, par, :, i, :], ps[1 + par][:, 0:120].rearrange("p (h i n) -> p h i n", i=2, n=NCMP)[:, :, i, :],
                    SCALE, m, ALU.mult, ALU.add)
        step(last)
        step(V.tensor_reduce(cmx[:], cs[:], AX_X, ALU.max))
        V.tensor_tensor(cs[:], cs[:], cmx[:].unsqueeze(2).to_broadcast([P, 16, NCMP]), ALU.subtract).then_inc(pr_dve, 1)
        dve.wait_ge(pr_act, PA["cexp"])
        step(V.tensor_reduce(csum[:], cs[:], AX_X, ALU.add))
        step(V.reciprocal(csum[:], csum[:]))
        for par in range(2):
            for i in range(2):
                g3 = gt[:, i, 3 * par:24:6]
                last = V.tensor_tensor(cfac[:].rearrange("p (a h i) -> p a h i", a=2, i=2)[:, par, :, i],
                                       csum[:].rearrange("p (a h i) -> p a h i", a=2, i=2)[:, par, :, i], g3, ALU.mult)
        step(last)
        for i in range(2):
            v = cs[:].rearrange("p (a i) n -> p a i n", i=2)[:, :, i, :]
            last = V.tensor_tensor(v, v, bc(con("cmp_ok", i * NCMP, (i + 1) * NCMP), 8), ALU.mult)
        step(last)
        V.tensor_tensor(cs[:], cs[:], cfac[:].unsqueeze(2).to_broadcast([P, 16, NCMP]), ALU.mult).then_inc(pr_dve, 1)
        for e in range(4):
            dve.wait_ge(pr_pe, PP[f"ct{e}"])
            V.tensor_copy(cst[0:NCMP, 2 * e:2 * e + 2, :, :],
                          ps[3 + e % 2][0:NCMP, :].rearrange("p (h i q) -> p h i q", h=2, i=2)).then_inc(pr_dve, 1)
        dve.wait_ge(pr_act, PA["rhi"])
        step(V.tensor_tensor(a_lo[:, 0:4, 0:S], r_t, a_hi[:, 0:4, 0:S].bitcast(F32), ALU.subtract))

    QD = counts(["rn", "nrm", "rot", "vt0", "vt2"])
    QA = counts(["sq", "sqrt", "vt1", "pool"])
    QP = counts(["ss", "rn", "rot", "vt0", "vt2", "vt1", "pool"])
    base_d, base_a, base_p = len(PD), len(PA), len(PP)

    def qd(l, n):
        return base_d + l * len(QD) + QD[n]

    def qa(l, n):
        return base_a + l * len(QA) + QA[n]

    def qp(l, n):
        return base_p + l * len(QP) + QP[n]

    def width(l, t):
        return T2 if l == 0 or t == 4 else S

    def pe_second(pe, l):
        pe.wait_ge(pr_act, qa(l, "sq"))
        for t in (4, 0, 1, 2, 3):
            w = width(l, t)
            last = nc.tensor.matmul(ps[5][0:10, 0:w], con("heads", 10 * t, 10 * (t + 1)), prep[:, t, 0:w],
                                    start=t == 4, stop=t == 3)
        last.then_inc(pr_pe, 1)
        pe.wait_ge(rows_loaded, 16)
        pe.wait_ge(pr_dve, qd(l, "rn"))
        for t in range(5):
            w = width(l, t)
            last = nc.tensor.matmul(ps[t][:, 0:w], rows10[0:10, t * P:(t + 1) * P], qn[0:10, 0:w], start=True,
                                    stop=True)
        last.then_inc(pr_pe, 1)
        pe.wait_ge(pr_dve, qd(l, "nrm"))
        for t in range(5):
            last = nc.tensor.matmul(ps[t][:, 0:S], con("rot2"), p2[:, 8 + t, 0:S], start=True, stop=True)
        last.then_inc(pr_pe, 1)
        for v, tile, b in ((0, 4, 5), (2, 13, 7), (1, 5, 5)):
            if v == 1:
                pe.wait_ge(pr_dve, qd(l, "vt0"))
            for k in range(4):
                last = nc.tensor.transpose(ps[b][:, k * P:(k + 1) * P], p2[:, tile, k * P:(k + 1) * P], con("ident"))
            last.then_inc(pr_pe, 1)
        nw = 2 if l == 0 else 1
        pe.wait_ge(pr_dve, qd(l, "rot"))
        for w in range(nw):
            pe.wait_ge(pool_ready, 1 + w if l == 0 else 3)
            for t in range(2):
                o = M_POOL + (2 * l + t) * P
                last = nc.tensor.matmul(ps[2 * w + t][:, 0:S], mats[:, o:o + P], yp[:, t, :] if w == 0 else yp2[:, t, :],
                                        start=True, stop=True)
        last.then_inc(pr_pe, 1)

    def act_second(act, l):
        for t in range(5):
            w = width(l, t)
            last = nc.scalar.activation(prep[:, t, 0:w], p2[:, 8 + t, 0:w], ACT.Square)
        last.then_inc(pr_act, 1)
        load_bias(act, l, (2, 3))
        act.wait_ge(pr_pe, qp(l, "ss"))
        nc.scalar.activation(qn[0:10], ps[5][0:10], ACT.Sqrt, scale=1.0 / HD, bias=eps[0:10, 0:1]).then_inc(pr_act, 1)
        act.wait_ge(pr_pe, qp(l, "vt1"))
        nc.scalar.activation(vt[:, 1], ps[5][:].rearrange("p (a b) -> p a b", a=4), ACT.Copy).then_inc(pr_act, 1)
        act.wait_ge(pr_pe, qp(l, "pool"))
        for w in range(2 if l == 0 else 1):
            for t in range(2):
                last = nc.scalar.activation(a_hi[:, 2 + t, w * S:(w + 1) * S], ps[2 * w + t][:, 0:S], ACT.Copy,
                                            scale=vcol("pool_scale", 2 * l + t))
        last.then_inc(pr_act, 1)

    def dve_second(dve, l, step):
        V = nc.vector
        dve.wait_ge(pr_act, qa(l, "sqrt"))
        V.reciprocal(qn[0:10], qn[0:10]).then_inc(pr_dve, 1)
        dve.wait_ge(nb_loaded, 256 * (l + 1))
        for q in range(4):
            v = nb[:, q].rearrange("p i (r c) -> p (i r) c", c=64)
            tq = nbt[:, 0:8, :]
            step(V.tensor_copy(tq, v[:, :, ::-1]))
            m = con("na_mask").rearrange("p (r c) -> p r c", c=64)
            for i in range(2):
                last = V.tensor_tensor(v[:, 4 * i:4 * i + 4, :], tq[:, 4 * i:4 * i + 4, :], m, ALU.add)
            step(last)
        dve.wait_ge(pr_pe, qp(l, "rn"))
        for t in range(5):
            w = width(l, t)
            g = vcol("k_g" if t == 4 else "q_g", l)
            last = V.scalar_tensor_tensor(p2[:, 8 + t, 0:w], p2[:, 8 + t, 0:w], g, ps[t][:, 0:w], ALU.mult, ALU.mult)
        last.then_inc(pr_dve, 1)
        dve.wait_ge(pr_dve, qd(l, "nrm"))
        dve.wait_ge(pr_pe, qp(l, "rot"))
        for t in range(5):
            V.tensor_tensor(prep[:, t, 0:S], p2[:, 8 + t, 0:S], con("cos2"), ALU.mult)
            last = V.tensor_tensor(prep[:, t, S:T2], ps[t][:, 0:S], con("sin2"), ALU.mult)
        step(last)
        last = V.tensor_tensor(p2[:, 8:13, 0:S], prep[:, :, 0:S], prep[:, :, S:T2], ALU.add)
        last.then_inc(pr_dve, 1)
        dve.wait_ge(pr_dve, qd(l, "rot"))
        V.tensor_copy(ksw[0:HD, 0, :], p2[HD:P, 12, :])
        V.tensor_copy(ksw[HD:P, 0, :], p2[0:HD, 12, :])
        for v, b in ((0, 5), (2, 7)):
            dve.wait_ge(pr_pe, qp(l, f"vt{v}"))
            V.tensor_copy(vt[:, v], ps[b][:].rearrange("p (a b) -> p a b", a=4)).then_inc(pr_dve, 1)
        dve.wait_ge(pr_act, qa(l, "pool"))
        for w in range(2 if l == 0 else 1):
            for t in range(2):
                c = slice(w * S, (w + 1) * S)
                last = V.scalar_tensor_tensor(a_lo[:, 2 + t, c], ps[2 * w + t][:, 0:S], vcol("pool_scale", 2 * l + t),
                                              a_hi[:, 2 + t, c].bitcast(F32), ALU.mult, ALU.subtract)
        step(last)

    def load_bias(eng, l, heads):
        for q in heads:
            for i in range(2):
                for r in range(2):
                    base = (4 * l + q) * 15 * 31 + (7 - (2 * i + r)) * 31 - 48
                    src = bass.AP(dram["rpb"].tensor, base, [[1, HD], [31, 4], [1, HD]])
                    dst = nb[r * HD:(r + 1) * HD, q, i, :].rearrange("p (r c) -> p r c", c=HD)
                    eng.dma_start(dst, src).then_inc(nb_loaded, 16)

    pool_count = [0]

    def pool_mix(pool, l):
        G = nc.gpsimd

        def pstep(ins):
            pool_count[0] += 1
            ins.then_inc(pool_step, 1)
            pool.wait_ge(pool_step, pool_count[0])

        for w in range(2 if l == 0 else 1):
            dst = yp if w == 0 else yp2
            if w == 0:
                for b in pu:
                    last = G.memset(b[:], 0.0)
                pstep(last)
            pstep(G.tensor_copy(pu[0][:, :, 16:16 + S], p2[:, 6:8, w * S:(w + 1) * S]))
            for n, (d0, d1) in enumerate(((1, 0), (1, 1), (2, 2), (4, 4))):
                lo, hi = 8, S + 24
                pstep(G.tensor_tensor(pu[n + 1][:, :, lo:hi], pu[n][:, :, lo - d0:hi - d0],
                                      pu[n][:, :, lo + d1:hi + d1], ALU.add))
            inv = con("pool_inv").rearrange("p (a b) -> p a b", a=2)
            for g in range(4):
                rows = slice((g % 2) * HD, (g % 2 + 1) * HD)
                last = G.tensor_tensor(dst[rows, g // 2, :], pu[g + 1][rows, g // 2, 16:16 + S], inv[rows, g // 2, :],
                                       ALU.mult)
            pstep(last)
            G.tensor_tensor(dst[:], dst[:], pu[0][:, :, 16:16 + S], ALU.subtract).then_inc(pool_ready, 1)
            pool.wait_ge(pool_ready, w + 1 if l == 0 else 3)

    def meet(eng, mine, others, k):
        eng.drain().then_inc(mine, 1)
        for o in others:
            eng.wait_ge(o, k)

    flow = []
    todo = list(products)

    def take(n):
        return [("product", todo.pop(0)) for _ in range(n)]

    def take_ffn():
        n = 1
        while n < len(todo) and todo[n].norm is None and todo[n].kind in ("gu", "down"):
            n += 1
        return take(n)

    flow += [("norm", "mix")] + take(2) + [("cmp", None), ("rwkv", None), ("meet", 1), ("first", None), ("meet", 2),
                                           ("attend", "first"), ("meet", 3)]
    flow += take(1) + [("norm", "ffn")] + take_ffn() + [("mods", 0), ("norm", "final1")]
    k_meet = 3
    for l in range(LAYERS):
        flow += [("norm", f"{l}.0")] + take_ffn() + [("norm", f"{l}.1")] + take(1)
        flow += [("meet", k_meet + 1), ("second", l), ("meet", k_meet + 2), ("attend", l), ("meet", k_meet + 3)]
        flow += take(1) + [("norm", f"{l}.2")] + take_ffn()
        if l + 1 < LAYERS:
            flow += [("mods", l + 1)]
        k_meet += 3
    flow += [("norm", "final2")]

    block = ctx.enter_context(nc.Block())

    @block.sync
    def _(sp):
        sp.dma_start(h[:], dram["x"]).then_inc(x_loaded, 16)
        for t, n in ((vecs, "vecs"), (consts, "consts")):
            sp.dma_start(t[:], dram[n]).then_inc(consts_loaded, 16)
        sp.dma_start(pos_i[:], dram["positions"].to_broadcast([P, S])).then_inc(pos_loaded, 16)
        for pr in products:
            def load(c, turn, slot, i, pr=pr):
                if pr.ada is not None:
                    wait(sp, lo_ready, c - RING + 1)
                    src = dram["w_ada"][bass.ds(pr.ada + i, 1)].rearrange("a p f -> p (a f)")
                    sp.dma_start(raw[slot][:], src).then_inc(landed[slot], 16)
                    c, slot = c + 1, (slot + 1) % RING
                wait(sp, lo_ready, c - RING + 1)
                sp.dma_start(raw[slot][:, 0:pr.size], source(pr, i)).then_inc(landed[slot], 16)
            if pr.name == "w_tail":
                sp.dma_start(mats[:], dram["mats"]).then_inc(mats_loaded, 16)
                feed_direct(sp, 0, 2)
            elif pr.name == "w_out":
                feed_direct(sp, 2, 4)
            if pr.name in ("w_out_0", "w_out_1"):
                l = int(pr.name[-1])
                for i in range(RING):
                    load(pr.base + i, 0, (pr.base + i) % RING, i)
                for phase in (pe_phase, act_phase, dve_phase):
                    sp.wait_ge(phase, 4 + 3 * l)
                load_bias(sp, l, (0, 1))
                load(pr.base + RING, 0, (pr.base + RING) % RING, RING)
            else:
                chunk_loop(sp, pr.base, pr.n, load, pr.stride)
            if pr.name == "w_out":
                sp.wait_ge(dve_phase, 2)
                sp.dma_start(rows10[0:10], dram["rows10"]).then_inc(rows_loaded, 16)
        sp.wait_ge(out_ready, 1)
        sp.dma_start(out, h[:, :, 0:S]).then_inc(out_stored, 16)
        sp.wait_ge(out_stored, 16)

    @block.gpsimd
    def _(pool):
        for l in range(LAYERS):
            pool.wait_ge(dve_phase, 4 + 3 * l)
            pool.wait_ge(pe_phase, 4 + 3 * l)
            pool.wait_ge(act_phase, 4 + 3 * l)
            pool_mix(pool, l)

    @block.tensor
    def _(pe):
        pe.wait_ge(consts_loaded, 32)
        pe.wait_ge(c_split_ready, 2)
        for kind, x in flow:
            if kind == "norm":
                pe_norm(pe, x)
            elif kind == "product":
                pe_product(pe, x)
            elif kind == "rwkv":
                pe.wait_ge(mats_loaded, 16)
                pe_rwkv(pe)
            elif kind == "meet":
                meet(pe, pe_phase, (act_phase, dve_phase), x)
            elif kind == "first":
                pe_first(pe)
            elif kind == "second":
                pe_second(pe, x)
            elif kind == "attend":
                pe_attend(pe, x)

    @block.scalar
    def _(act):
        act.wait_ge(consts_loaded, 32)
        nc.scalar.activation(silu_c[:], vcol("c", 0, 16).rearrange("p (k w) -> p k w", w=2),
                             ACT.Silu).then_inc(silu_c_ready, 1)
        act.wait_ge(silu_c_ready, 1)
        nc.scalar.activation(c_split[:, :, 0:2], silu_c[:], ACT.Copy).then_inc(c_split_ready, 1)
        act.wait_ge(x_loaded, 16)
        drained = 0
        for kind, x in flow:
            if kind == "norm":
                if drained and x not in own_squares:
                    act.wait_ge(chunk_drained, drained)
                if x == "0.0":
                    act.wait_ge(first_done, 1)
                act_norm(act, x)
                if x == "mix":
                    act_tables(act)
            elif kind == "product":
                act_product(act, x)
                drained = x.end
            elif kind == "rwkv":
                act_rwkv(act)
            elif kind == "meet":
                meet(act, act_phase, (pe_phase, dve_phase), x)
            elif kind == "first":
                act_first(act)
            elif kind == "second":
                act_second(act, x)
            elif kind == "attend":
                act_attend(act, x)

    @block.vector
    def _(dve):
        made = [0]

        def step(ins):
            made[0] += 1
            ins.then_inc(dve_step, 1)
            dve.wait_ge(dve_step, made[0])

        for i, v in enumerate((1e-6, 64e-5)):
            last = nc.vector.memset(eps[:, i:i + 1], v)
        step(last)
        dve.wait_ge(consts_loaded, 32)
        dve.wait_ge(c_split_ready, 1)
        nc.vector.tensor_tensor(c_split[:, :, 2:4], silu_c[:], c_split[:, :, 0:2].bitcast(F32),
                                ALU.subtract).then_inc(c_split_ready, 1)
        dve.wait_ge(x_loaded, 16)
        for kind, x in flow:
            if kind == "norm":
                if x == "0.0":
                    dve.wait_ge(first_done, 1)
                dve_norm(dve, x, step)
                if x == "mix":
                    dve_tables(dve, step)
            elif kind == "product":
                gate = None
                if x.name.startswith("w_dn1"):
                    l = int(x.name[-1])
                    gate = lambda j, w, l=l: half_gate[:, l, 0, bass.ds(j, 1), w:w + 1].rearrange("p a b -> p (a b)")
                elif x.name.startswith("w_dn2"):
                    l = int(x.name[-1])
                    gate = lambda j, w, l=l: half_gate[:, l, 1, bass.ds(j, 1), w:w + 1].rearrange("p a b -> p (a b)")
                elif x.name in ("w_out_0", "w_out_1"):
                    l = int(x.name[-1])
                    gate = lambda j, w, l=l: mod[:, l, bass.ds(5 * KT + j, 1), w:w + 1].rearrange("p a b -> p (a b)")
                dve_product(dve, x, gate)
            elif kind == "cmp":
                dve_cmp(dve, step)
            elif kind == "rwkv":
                dve_rwkv(dve, step)
            elif kind == "mods":
                dve_mods(dve, step, x)
            elif kind == "meet":
                meet(dve, dve_phase, (pe_phase, act_phase), x)
            elif kind == "first":
                dve_first(dve, step)
            elif kind == "second":
                dve_second(dve, x, step)
            elif kind == "attend":
                dve_attend(dve, x, step)


def kernel(**inputs):
    import numpy as _np
    import concourse.bacc as _bacc
    from concourse.bass_utils import run_bass_kernel_spmd as _run

    g = {k: _np.asarray(v) for k, v in inputs.items()}

    def cols(v):
        return v.reshape(-1, P).T

    def chunks(w, m):
        k, n = w.shape
        return w.reshape(k // P, P, n // m, m).transpose(2, 1, 0, 3).reshape(n // m, P, (k // P) * m)

    def ffn(gate, up):
        return _np.concatenate([chunks(gate, P), chunks(up, P)], axis=2)

    def down(w):
        return _np.concatenate([chunks(w[:FH * P], P), chunks(w[FH * P:], P)], axis=0)

    w_in = g["w_in"][0]
    tail = _np.zeros((D, P), w_in.dtype)
    tail[:, 0:32] = w_in[:, 1792:R_COLS]
    tail[:, 32:56] = w_in[:, R_COLS + 1280:]
    vec = _np.zeros((P, VN), _np.float32)

    def put(name, a, o=0, rows=P):
        vec[:rows, VAT[name][0] + o:VAT[name][0] + o + a.shape[1]] = a

    put("norm_mix", cols(g["norm_mix"]))
    put("norm_ffn", cols(g["norm_ffn"]))
    put("norm_final", cols(g["norm_final"]))
    put("final_g", cols(g["final_g_2"]))
    put("norm_g", cols(g["norm_g_2"]))
    put("mu", cols(g["mu_shift"][0, :1792]))
    put("mu", g["mu_shift"][0, 1792:].reshape(32, 1), 14, 32)
    for n in ("w0", "a0", "k_k", "k_a", "r_k", "lnx_w", "lnx_b", "pe_k", "pe_v", "bk1", "bv1"):
        put(n, cols(g[n]))
    put("b_ada", cols(g["b_ada_2"]))
    put("pool_scale", cols(g["pool_scale_2"]))
    for n, s in (("q_g", "q_norm_g_2"), ("k_g", "k_norm_g_2")):
        put(n, _np.concatenate([g[s].T, g[s].T], axis=0))
    put("c", _np.stack([cols(g["c_2"]), cols(g["c_ctx_2"])], axis=2).reshape(P, 16))
    mats = _np.zeros((P, MN), _np.float32)
    mats[:, M_G2:M_G2 + 512] = g["g2"][0, :128]
    mats[:32, M_G2T:M_G2T + 512] = g["g2"][0, 128:]
    mats[:64, M_LORA:M_LORA + 512] = g["w2"][0]
    mats[64:, M_LORA:M_LORA + 512] = g["a2"][0]
    k2 = g["wk2"][0].reshape(2, P, HD).transpose(1, 0, 2)
    mats[:, M_CK2:M_CK2 + 256] = _np.concatenate([k2, k2], axis=2).reshape(P, 256)
    mats[:, M_CV2:M_CV2 + 128] = g["wv2"][0].reshape(2, P, HD).transpose(1, 0, 2).reshape(P, 128)
    for l in range(LAYERS):
        for q in range(4):
            o = M_POOL + (2 * l + q // 2) * P + (q % 2) * HD
            mats[(q % 2) * HD:(q % 2) * HD + HD, o:o + HD] = g["pool_w_2"][l, q]
    up1 = [ffn(g["ffn1_up_2"][l][:, :FF], g["ffn1_up_2"][l][:, FF:]) for l in range(LAYERS)]
    up2 = [ffn(g["ffn2_up_2"][l][:, :FF], g["ffn2_up_2"][l][:, FF:]) for l in range(LAYERS)]
    rpb = g["na_rpb_2"]
    arrays = {
        "x": _np.concatenate([g["x"][0].T.reshape(KT, P, S), g["ctx_2"][0].T.reshape(KT, P, S)], axis=2)
                .transpose(1, 0, 2),
        "positions": g["positions"],
        "consts": const_array(),
        "rows10": head_rows(),
        "vecs": vec,
        "mats": mats,
        "rpb": rpb[..., ::-1].reshape(1, -1),
        "w_in": _np.concatenate([chunks(w_in[:, :1792], 2 * P), chunks(w_in[:, R_COLS:R_COLS + 1280], 2 * P)]),
        "w_tail": chunks(tail, P),
        "w_cmp": _np.concatenate([chunks(g[n][0][h * D:(h + 1) * D], 2 * P) for n in ("wk1", "wv1") for h in (0, 1)]),
        "w_out": chunks(g["w_out"][0], 2 * P),
        "w_gu": ffn(g["w_gate"][0], g["w_up"][0]),
        "w_dn": down(g["w_down"][0]),
        "w_ada": _np.concatenate([chunks(g["w_ada_2"][l], 2 * P) for l in range(LAYERS)]),
    }
    for l in range(LAYERS):
        arrays[f"w_gu1_{l}"] = up1[l]
        arrays[f"w_dn1_{l}"] = down(g["ffn1_down_2"][l])
        arrays[f"w_gu2_{l}"] = up2[l]
        arrays[f"w_dn2_{l}"] = down(g["ffn2_down_2"][l])
        arrays[f"w_in_{l}"] = chunks(g["w_in_2"][l], 2 * P)
        arrays[f"w_out_{l}"] = chunks(g["w_out_2"][l], 2 * P)
    arrays = {f"in_{k}": _np.ascontiguousarray(v) for k, v in arrays.items()}

    nc = _bacc.Bacc("TRN2", target_bir_lowering=False, num_devices=1)
    dram = {k[3:]: nc.dram_tensor(k, v.shape, mybir.dt.from_np(v.dtype), kind="ExternalInput").ap()
            for k, v in arrays.items()}
    out = nc.dram_tensor("out_h", (P, KT, S), F32, kind="ExternalOutput").ap()
    program(nc, dram, out)
    r = _run(nc, [arrays], core_ids=[0])
    got = r.results[0]["out_h"]
    return got.transpose(2, 1, 0).reshape(1, S, D)
```
